# Optimizing a Trainium2 kernel written in Bass

```python
import jax, jax.numpy as jnp
from jax import lax
import numpy as np

D_MODEL = 1024
BATCH = 1
SEQ = 512
DEPTH = 2

GRID_W = 64
HEAD_DIM = 64
QBLK = 128
EPS = 1e-6
NEG_INF = -1e30
ROPE_THETA = 10000.0

A_HEADS = 4
A_WIN_R = 8
A_WIN_C = 16
A_COL_BLK = 16
A_KEY_COLS = 32
B_HEADS = 4
B_KV_HEADS = 2
B_WINDOW = 128
T5_BUCKETS = 32
T5_MAX_DIST = 128
C_HEADS = 4
C_KV_HEADS = 2
D_HEADS = 4
D_Q_LORA = 256
D_KV_LORA = 128
D_NOPE = 64
D_ROPE = 32
D_V = 64

N_BRANCH = 4
BRANCH_W = 256
D_FF = ((8 * D_MODEL + 3 * 256 - 1) // (3 * 256)) * 256

A_W = A_HEADS * HEAD_DIM
B_QW = B_HEADS * HEAD_DIM
B_KVW = B_KV_HEADS * HEAD_DIM
C_QW = C_HEADS * HEAD_DIM
C_KVW = C_KV_HEADS * HEAD_DIM
IN_SPLITS = (A_W, A_W, A_W, B_QW, B_KVW, B_KVW, C_QW, C_KVW, C_KVW,
             D_Q_LORA, D_KV_LORA, D_ROPE, N_BRANCH * D_MODEL)
IN_WIDTH = sum(IN_SPLITS)

kernel_name = 'hybrid_gated_encoder_block'

def rms_norm(x, g):
    xf = x.astype(jnp.float32)
    y = xf * lax.rsqrt(jnp.mean(xf * xf, axis=-1, keepdims=True) + EPS)
    return (y * g.astype(jnp.float32)).astype(x.dtype)

def rope_rotate(x, pos):
    d = x.shape[-1]
    half = d // 2
    inv_freq = 1.0 / (ROPE_THETA ** (jnp.arange(half, dtype=jnp.float32) * (2.0 / d)))
    ang = pos[:, None] * inv_freq[None, :]
    cos = jnp.cos(ang)[:, None, :]
    sin = jnp.sin(ang)[:, None, :]
    xf = x.astype(jnp.float32)
    x1, x2 = xf[..., :half], xf[..., half:]
    return jnp.concatenate([x1 * cos - x2 * sin, x2 * cos + x1 * sin], axis=-1).astype(x.dtype)

def axial_rope(x, row_pos, col_pos):
    h = x.shape[-1] // 2
    return jnp.concatenate([rope_rotate(x[..., :h], row_pos), rope_rotate(x[..., h:], col_pos)], axis=-1)

def t5_buckets(rel):
    nb = T5_BUCKETS // 2
    max_exact = nb // 2
    ret = (rel > 0).astype(np.int32) * nb
    n = np.abs(rel)
    large = max_exact + (np.log(np.maximum(n, 1) / max_exact) / np.log(T5_MAX_DIST / max_exact)
                         * (nb - max_exact)).astype(np.int32)
    large = np.minimum(large, nb - 1)
    return ret + np.where(n < max_exact, n, large)

def neighborhood_attention(q, k, v, rpb):
    b, s, h, d = q.shape
    rows = s // GRID_W
    kr = min(A_WIN_R, rows)
    ncb = GRID_W // A_COL_BLK
    nk = kr * A_KEY_COLS
    r = np.arange(rows)
    rs = np.clip(r - A_WIN_R // 2, 0, rows - kr)
    key_rows = rs[:, None] + np.arange(kr)[None, :]
    col0 = np.clip(np.arange(ncb) * A_COL_BLK - A_WIN_C // 2, 0, GRID_W - A_KEY_COLS)
    key_cols = col0[:, None] + np.arange(A_KEY_COLS)[None, :]
    idx = key_rows[:, None, :, None] * GRID_W + key_cols[None, :, None, :]
    flat = jnp.asarray(idx.reshape(-1))
    kg = jnp.take(k, flat, axis=1).reshape(b, rows, ncb, nk, h, d)
    vg = jnp.take(v, flat, axis=1).reshape(b, rows, ncb, nk, h, d)
    qb = q.reshape(b, rows, ncb, A_COL_BLK, h, d)
    q_cols = np.arange(ncb)[:, None] * A_COL_BLK + np.arange(A_COL_BLK)[None, :]
    cs = np.clip(q_cols - A_WIN_C // 2, 0, GRID_W - A_WIN_C)
    kc = key_cols[:, None, :]
    col_ok = (kc >= cs[:, :, None]) & (kc < cs[:, :, None] + A_WIN_C)
    mask = np.broadcast_to(col_ok[:, :, None, :], (ncb, A_COL_BLK, kr, A_KEY_COLS)).reshape(ncb, A_COL_BLK, nk)
    dr = key_rows - r[:, None] + (A_WIN_R - 1)
    dc = np.clip(kc - q_cols[:, :, None], -(A_WIN_C - 1), A_WIN_C - 1) + (A_WIN_C - 1)
    bias = rpb[:, dr[:, None, None, :, None], dc[None, :, :, None, :]]
    bias = bias.reshape(h, rows, ncb, A_COL_BLK, nk).transpose(1, 2, 0, 3, 4)
    sc = jnp.einsum('brjqhd,brjkhd->brjhqk', qb, kg, preferred_element_type=jnp.float32) * (d ** -0.5)
    sc = jnp.where(mask[None, None, :, None], sc + bias.astype(jnp.float32), NEG_INF)
    p = jax.nn.softmax(sc, axis=-1).astype(v.dtype)
    o = jnp.einsum('brjhqk,brjkhd->brjqhd', p, vg)
    return o.reshape(b, s, h * d)

def window_sink_attention(q, k, v, sink, t5_table):
    b, s, hkv, g, d = q.shape
    nb = s // QBLK
    kl = QBLK + 2 * B_WINDOW
    kp = jnp.pad(k, ((0, 0), (B_WINDOW, B_WINDOW), (0, 0), (0, 0)))
    vp = jnp.pad(v, ((0, 0), (B_WINDOW, B_WINDOW), (0, 0), (0, 0)))
    idx = np.arange(nb)[:, None] * QBLK + np.arange(kl)[None, :]
    flat = jnp.asarray(idx.reshape(-1))
    kb = jnp.take(kp, flat, axis=1).reshape(b, nb, kl, hkv, d)
    vb = jnp.take(vp, flat, axis=1).reshape(b, nb, kl, hkv, d)
    kpos = idx - B_WINDOW
    qpos = np.arange(nb)[:, None] * QBLK + np.arange(QBLK)[None, :]
    rel = kpos[:, None, :] - qpos[:, :, None]
    valid = (np.abs(rel) <= B_WINDOW) & (kpos[:, None, :] >= 0) & (kpos[:, None, :] < s)
    bucket = t5_buckets(rel[0])
    bias = t5_table[bucket].transpose(2, 0, 1).reshape(hkv, g, QBLK, kl).astype(jnp.float32)
    qb = q.reshape(b, nb, QBLK, hkv, g, d)
    sc = jnp.einsum('bnqhgd,bnkhd->bnhgqk', qb, kb, preferred_element_type=jnp.float32) * (d ** -0.5)
    sc = jnp.where(valid[None, :, None, None], sc + bias[None, None], NEG_INF)
    sk = sink.astype(jnp.float32).reshape(hkv, g)[None, None, :, :, None, None]
    m = jnp.maximum(jnp.max(sc, axis=-1, keepdims=True), sk)
    e = jnp.exp(sc - m)
    p = e / (jnp.sum(e, axis=-1, keepdims=True) + jnp.exp(sk - m))
    o = jnp.einsum('bnhgqk,bnkhd->bnqhgd', p.astype(v.dtype), vb)
    return o.reshape(b, s, hkv * g * d)

def dense_block_attention(q, k, v, scale):
    b, s, hkv, g, dq = q.shape
    dv = v.shape[-1]
    nb = s // QBLK
    qb = q.reshape(b, nb, QBLK, hkv, g, dq).transpose(1, 0, 2, 3, 4, 5)

    def one_block(qblk):
        sc = jnp.einsum('bqhgd,bkhd->bhgqk', qblk, k, preferred_element_type=jnp.float32) * scale
        p = jax.nn.softmax(sc, axis=-1).astype(v.dtype)
        return jnp.einsum('bhgqk,bkhd->bqhgd', p, v)

    o = lax.map(one_block, qb)
    return o.transpose(1, 0, 2, 3, 4, 5).reshape(b, s, hkv * g * dv)

def hybrid_mixer(xn, w_in, a_rpb, b_sink, t5_table, c_qn, c_kn, d_qn, d_kvn, d_wq, d_wkv, w_branch, w_out):
    b, s, _ = xn.shape
    proj = xn @ w_in
    offsets = np.cumsum(IN_SPLITS)[:-1].tolist()
    (aq, ak, av, bq, bk, bv, cq, ck, cv, dcq, dckv, dkr, gate_logits) = jnp.split(proj, offsets, axis=-1)
    t = jnp.arange(s)
    pos = t.astype(jnp.float32)
    row_pos = (t // GRID_W).astype(jnp.float32)
    col_pos = (t % GRID_W).astype(jnp.float32)

    o_a = neighborhood_attention(aq.reshape(b, s, A_HEADS, HEAD_DIM), ak.reshape(b, s, A_HEADS, HEAD_DIM),
                                 av.reshape(b, s, A_HEADS, HEAD_DIM), a_rpb)
    o_b = window_sink_attention(bq.reshape(b, s, B_KV_HEADS, B_HEADS // B_KV_HEADS, HEAD_DIM),
                                bk.reshape(b, s, B_KV_HEADS, HEAD_DIM), bv.reshape(b, s, B_KV_HEADS, HEAD_DIM),
                                b_sink, t5_table)
    qc = axial_rope(rms_norm(cq.reshape(b, s, C_HEADS, HEAD_DIM), c_qn), row_pos, col_pos)
    kc = axial_rope(rms_norm(ck.reshape(b, s, C_KV_HEADS, HEAD_DIM), c_kn), row_pos, col_pos)
    o_c = dense_block_attention(qc.reshape(b, s, C_KV_HEADS, C_HEADS // C_KV_HEADS, HEAD_DIM), kc,
                                cv.reshape(b, s, C_KV_HEADS, HEAD_DIM), HEAD_DIM ** -0.5)
    qd = (rms_norm(dcq, d_qn) @ d_wq).reshape(b, s, D_HEADS, D_NOPE + D_ROPE)
    qd = jnp.concatenate([qd[..., :D_NOPE], rope_rotate(qd[..., D_NOPE:], pos)], axis=-1)
    kvd = (rms_norm(dckv, d_kvn) @ d_wkv).reshape(b, s, D_HEADS, D_NOPE + D_V)
    k_rope = rope_rotate(dkr.reshape(b, s, 1, D_ROPE), pos)
    kd = jnp.concatenate([kvd[..., :D_NOPE], jnp.broadcast_to(k_rope, (b, s, D_HEADS, D_ROPE))], axis=-1)
    o_d = dense_block_attention(qd[:, :, :, None, :], kd, kvd[..., D_NOPE:], (D_NOPE + D_ROPE) ** -0.5)

    branches = jnp.stack([o_a, o_b, o_c, o_d], axis=2)
    y = jnp.einsum('bsnc,ncd->bsnd', branches, w_branch)
    gates = jax.nn.sigmoid(gate_logits.astype(jnp.float32)).astype(xn.dtype).reshape(b, s, N_BRANCH, D_MODEL)
    merged = jnp.sum(gates * y, axis=2)
    return merged @ w_out

def setup_inputs(seed: int = 0) -> dict:
    key = jax.random.key(seed)
    ks = jax.random.split(key, 20)
    f32 = jnp.float32

    def nrm(k, shape, scale):
        return jax.random.normal(k, shape, f32) * scale

    def gain(k, shape):
        return 1.0 + 0.05 * jax.random.normal(k, shape, f32)

    return {
        'x': nrm(ks[0], (BATCH, SEQ, D_MODEL), 1.0),
        'w_in': nrm(ks[1], (DEPTH, D_MODEL, IN_WIDTH), D_MODEL ** -0.5),
        'a_rpb': nrm(ks[2], (DEPTH, A_HEADS, 2 * A_WIN_R - 1, 2 * A_WIN_C - 1), 0.5),
        'b_sink': nrm(ks[3], (DEPTH, B_HEADS), 1.0),
        't5_bias': nrm(ks[4], (T5_BUCKETS, B_HEADS), 0.5),
        'c_q_norm': gain(ks[5], (DEPTH, HEAD_DIM)),
        'c_k_norm': gain(ks[6], (DEPTH, HEAD_DIM)),
        'd_q_norm': gain(ks[7], (DEPTH, D_Q_LORA)),
        'd_kv_norm': gain(ks[8], (DEPTH, D_KV_LORA)),
        'd_w_q_up': nrm(ks[9], (DEPTH, D_Q_LORA, D_HEADS * (D_NOPE + D_ROPE)), D_Q_LORA ** -0.5),
        'd_w_kv_up': nrm(ks[10], (DEPTH, D_KV_LORA, D_HEADS * (D_NOPE + D_V)), D_KV_LORA ** -0.5),
        'w_branch': nrm(ks[11], (DEPTH, N_BRANCH, BRANCH_W, D_MODEL), BRANCH_W ** -0.5),
        'w_out': nrm(ks[12], (DEPTH, D_MODEL, D_MODEL), D_MODEL ** -0.5),
        'ln_pre_mix': gain(ks[13], (DEPTH, D_MODEL)),
        'ln_post_mix': gain(ks[14], (DEPTH, D_MODEL)),
        'ln_pre_ffn': gain(ks[15], (DEPTH, D_MODEL)),
        'ln_post_ffn': gain(ks[16], (DEPTH, D_MODEL)),
        'ffn_w_gu': nrm(ks[17], (DEPTH, D_MODEL, 2 * D_FF), D_MODEL ** -0.5),
        'ffn_w_down': nrm(ks[18], (DEPTH, D_FF, D_MODEL), D_FF ** -0.5),
    }

def reference(x, w_in, a_rpb, b_sink, t5_bias, c_q_norm, c_k_norm, d_q_norm, d_kv_norm, d_w_q_up, d_w_kv_up,
              w_branch, w_out, ln_pre_mix, ln_post_mix, ln_pre_ffn, ln_post_ffn, ffn_w_gu, ffn_w_down):
    for l in range(DEPTH):
        h = rms_norm(x, ln_pre_mix[l])
        m = hybrid_mixer(h, w_in[l], a_rpb[l], b_sink[l], t5_bias, c_q_norm[l], c_k_norm[l], d_q_norm[l],
                         d_kv_norm[l], d_w_q_up[l], d_w_kv_up[l], w_branch[l], w_out[l])
        x = x + rms_norm(m, ln_post_mix[l])
        h = rms_norm(x, ln_pre_ffn[l])
        gu = h @ ffn_w_gu[l]
        f = (jax.nn.silu(gu[..., :D_FF]) * gu[..., D_FF:]) @ ffn_w_down[l]
        x = x + rms_norm(f, ln_post_ffn[l])
    return x


_drawn_inputs = setup_inputs


def setup_inputs(seed=0):
    import zlib

    import numpy as np

    out = dict(_drawn_inputs(seed))
    spreads = {}
    factors = {'b_sink': 8.0, 'c_q_norm': 3.47, 'c_k_norm': 3.959, 'd_q_norm': 2.903}
    for name, (base, spread) in spreads.items():
        noise = np.random.default_rng([zlib.crc32(name.encode()), seed]).standard_normal(out[name].shape)
        drawn = base * np.exp(spread * noise) if base else spread * noise
        out[name] = __import__('jax').numpy.asarray(drawn.astype(out[name].dtype))
    for name, factor in factors.items():
        out[name] = (out[name] * factor).astype(out[name].dtype)
    return out
```

```python
from contextlib import ExitStack

import numpy as np

import concourse.bass as bass
from concourse import mybir

ALU = mybir.AluOpType
ACT = mybir.ActivationFunctionType
AX = mybir.AxisListType
F32 = mybir.dt.float32
F32R = mybir.dt.float32r
I32 = mybir.dt.int32

P = 128
DM = 1024
KD = DM // P
S = 512
NT = S // P
L = 2
HD = 64
GRID_W, ROWS = 64, 8
DFF = 2816
KF = DFF // P
EPS = 1e-6
NEG = -1e30
QL, KVL, ROPE, DQK = 256, 128, 32, 96
ROPE_THETA = 10000.0

BR = "DABC"
W_IN_AT = dict(Aq=0, Ak=256, Av=512, Bq=768, Bkv=1024, Cq=1280, Ckv=1536, Dcq=1792, Dckv=2048, gates=2208)

PIECES = []
for _b in BR:
    PIECES += dict(D=[("Dcq", 2048), ("Dckv", 1280), ("gateD0", 2048), ("Dup", 1280)], A=[("Aq", 2048), ("Ak", 2048), ("Av", 2048)],
                   B=[("Bq", 2048), ("Bkv", 2048)], C=[("Cq", 2048), ("Ckv", 2048)])[_b]
    PIECES += [(f"gate{_b}{j}", 2048) for j in range(_b == "D", 4)] + [(f"branch{_b}", 2048)]
N_FIRST = len(PIECES)
N_OUT, N_GU, N_DOWN = 4, KF, 2 * KD
OUT0 = N_FIRST
GU0 = OUT0 + N_OUT
DOWN0 = GU0 + N_GU
PIECES += [(f"out{j}", 2048) for j in range(N_OUT)] + [(f"gu{j}", 2048) for j in range(N_GU)]
PIECES += [(f"down{d}{h}", 1408) for d in range(KD) for h in range(2)]
NP_ = len(PIECES)
PIECE = {name: n for n, (name, _) in enumerate(PIECES)}
KH = KF // 2

GATE0 = {b: 16 * i for i, b in enumerate(BR)}
Y0 = {b: 16 * i + 8 for i, b in enumerate(BR)}
WOUT0 = 64
GUM0 = WOUT0 + KD
DOWNM0 = GUM0 + 2 * KF
N_MAIN = DOWNM0 + KD

WORK = []
for _b in BR:
    WORK += dict(D=["Dcq0", "Dcq1", "Dckv0", "Dckv1"] + [f"Dq{t}" for t in range(NT)] + [f"Dkv{t}" for t in range(NT)],
                 A=["Aq0", "Aq1", "Ak0", "Ak1", "Av0", "Av1"], B=["Bq0", "Bq1", "Bk", "Bv"],
                 C=["Cq0", "Cq1", "Ck", "Cv"])[_b]
    WORK += [("score", _b, h, t) for h in range(4) for t in range(NT)]
WORK_AT = {n: i for i, n in enumerate(WORK)}
N_WORK = len(WORK)

TURN = [("stat", "pre_mix"), ("spread", "pre_mix")]
for _b in BR:
    TURN += dict(D=[("latent", c) for c in range(3)] + [(x, h) for h in range(4) for x in ("Dq", "Dk")],
                 B=["Bv"], C=[("C", c) for c in range(3)]).get(_b, [])
    TURN += [("prob", _b, h, k) for h in range(4) for k in range(NT)]
for _n in ("post_mix", "pre_ffn", "post_ffn"):
    TURN += [("stat", _n), ("spread", _n)]
TURN_AT = {n: i for i, n in enumerate(TURN)}
N_TURN = len(TURN)
NORMS = ["pre_mix", "post_mix", "pre_ffn", "post_ffn"]

SPLIT = [("h", "pre_mix", d) for d in range(KD)]
for _b in BR:
    SPLIT += dict(D=[("latent", c) for c in range(3)] + [("V", "D", t) for t in range(NT)]
                  + [(x, h) for h in range(4) for x in ("Dq", "Dk")],
                  A=["Aq0", "Aq1", "Ak0", "Ak1"] + [("V", "A", t) for t in range(NT)],
                  B=["Bq0", "Bq1", "Bk"] + [("V", "B", t) for t in range(NT)],
                  C=[("V", "C", t) for t in range(NT)] + [("C", c) for c in range(3)])[_b]
    for _h in range(4):
        SPLIT += [("prob", _b, _h, k) for k in range(NT)]
        SPLIT += [("o", _b, _h // 2)] if _h % 2 else []
SPLIT += [("merged", d) for d in range(KD)] + [("h", "pre_ffn", d) for d in range(KD)]
ACT0 = len(SPLIT)
SPLIT += [("act", j) for j in range(KF)]
SPLIT_AT = {n: i for i, n in enumerate(SPLIT)}
N_SPLIT = len(SPLIT)

COPY = ["Dcq0", "Dcq1", "Dckv0", "Dckv1"] + [f"Dq{t}" for t in range(NT)] + [f"Dk{t}" for t in range(NT)] + ["Bv", "Cq0", "Cq1", "Ck"]
COPY_AT = {n: i for i, n in enumerate(COPY)}
N_COPY = len(COPY)

STEPS = 3 * KD
GATE_BEFORE = dict(D=[48, 48, 72], A=[0], B=[0], C=[72])


def gate_points(b):
    at = GATE_BEFORE[b][-1]
    s, t = dict(A=(9, 4), B=(9, 4), C=(6, 2), D=(6, 2))[b]
    points = list(GATE_BEFORE[b])
    for _ in range(4):
        for n in (s, s, s, s, t, t, t):
            at += n
            points.append(at)
    assert at == 8 * STEPS
    return points


GATE_POINTS = {b: gate_points(b) for b in BR}


def gate_point(b, h, n):
    return len(GATE_BEFORE[b]) + 7 * h + n


def gate_tiles(b, point):
    before = GATE_POINTS[b][point - 1] if point else 0
    return range(before // STEPS, GATE_POINTS[b][point] // STEPS)


def banded(b):
    return b in "AB"


def window(b, t):
    return range(max(0, t - 1), min(NT, t + 2)) if banded(b) else range(NT)


PARAMS = {}
_at = 0
for _n, _w in (("pre_mix", 8), ("post_mix", 8), ("pre_ffn", 8), ("post_ffn", 8), ("latent", 3), ("sink", 4), ("cq", 64), ("ck", 64)):
    PARAMS[_n] = (_at, _at + _w)
    _at += _w
N_PARAM = _at
CONST = {}
_at = 0
for _n, _w in (("ident", P), ("ones", P), ("cosC", NT * 32), ("sinC", NT * 32), ("cosD", NT * 16), ("sinD", NT * 16),
               ("maskA", 3 * 48), ("params", L * N_PARAM)):
    CONST[_n] = (_at, _at + _w)
    _at += _w
N_CONST = _at
BIAS_X = 512
RPB_ROW = 64
RPB_HEAD = 15 * RPB_ROW
N_RPB = 4 * RPB_HEAD + RPB_ROW

N_CHAIN = 256


def at(l, per_layer, n):
    return l * per_layer + n


def view(ap, dims):
    return bass.AP(tensor=ap.tensor, offset=ap.offset, ap=[list(ap.ap[0])] + [list(d) for d in dims])


def program(nc, stream, x_in, const_in, rpb_in, t5_in, hot_in, out):
    stream = stream.rearrange("l n p c -> (l n) p c")
    rpb_line = nc.dram_tensor("rpb_line", (16, N_RPB), F32).ap()
    t5_line = nc.dram_tensor("t5_line", (P, 4 * BIAS_X), F32).ap()

    base = (nc.sbuf_base + 31) // 32 * 32

    def sb(name, shape, dt, offset):
        size = 4 * int(np.prod(shape[1:]))
        assert base + offset + size <= nc.sbuf_usable_end, (name, base + offset + size)
        return nc.alloc_sbuf_tensor_at(name, shape, dt, offset=base + offset)

    K = 1024
    x = sb("x", [P, KD, S], F32, 0)
    h_hi = sb("h_hi", [P, KD, S], F32R, 16 * K)
    h_lo = sb("h_lo", [P, KD, S], F32R, 32 * K)
    raw = sb("raw", [P, 2, 2048], F32, 48 * K)
    w_hi = sb("w_hi", [P, 2, 2048], F32R, 64 * K)
    w_lo = sb("w_lo", [P, 2, 2048], F32R, 80 * K)
    Z = 96 * K
    gates = sb("gates", [P, KD, S], F32, Z)
    merged = sb("merged", [P, KD, S], F32, Z + 16 * K)
    o_hi = sb("o_hi", [P, 2, S], F32R, Z + 32 * K)
    o_lo = sb("o_lo", [P, 2, S], F32R, Z + 36 * K)
    prob = sb("prob", [P, NT, S], F32, Z + 40 * K)
    pt_hi = sb("pt_hi", [P, 2, S], F32R, Z + 48 * K)
    pt_lo = sb("pt_lo", [P, 2, S], F32R, Z + 52 * K)
    yt = sb("yt", [P, 2, S], F32, Z + 52 * K)
    QT, KT = Z + 56 * K, Z + 72 * K
    qa_hi, qa_lo = (sb(f"qa_{n}", [P, 2, S], F32R, QT + o * K) for n, o in (("hi", 0), ("lo", 4)))
    ka_hi, ka_lo = (sb(f"ka_{n}", [P, 2, S], F32R, KT + o * K) for n, o in (("hi", 0), ("lo", 4)))
    qd_hi, qd_lo = (sb(f"qd_{n}", [P, 4, S], F32R, QT + o * K) for n, o in (("hi", 0), ("lo", 8)))
    kd_hi, kd_lo = (sb(f"kd_{n}", [P, 4, S], F32R, KT + o * K) for n, o in (("hi", 0), ("lo", 8)))
    bias_a = sb("bias_a", [P, 2, 896], F32, QT + 8 * K)
    rpb = sb("rpb", [P, 4, 512], F32, KT + 8 * K)
    d_tm = sb("d_tm", [P, NT, 416], F32, QT)
    d_sq = sb("d_sq", [P, NT, 384], F32, QT + 6656)
    lat_hi = sb("lat_hi", [P, 3, S], F32R, KT)
    lat_lo = sb("lat_lo", [P, 3, S], F32R, KT + 6 * K)
    dq_tm = sb("dq_tm", [P, NT, 384], F32, Z + 40 * K)
    dk_tm = sb("dk_tm", [P, NT, 384], F32, Z + 46 * K)
    b_fm = sb("b_fm", [P, S], F32, Z + 40 * K)
    rope_d = sb("rope_d", [P, 4, 256], F32, Z + 52 * K)
    c_tm = sb("c_tm", [P, NT, 384], F32, Z + 40 * K)
    c_sq = sb("c_sq", [P, NT * 384], F32, Z + 46 * K)
    act_hi = sb("act_hi", [P, KF, S], F32R, Z)
    act_lo = sb("act_lo", [P, KF, S], F32R, Z + 44 * K)
    hot = sb("hot", [33, BIAS_X], F32, QT)
    t5 = sb("t5", [33, 4, P], F32, QT + 2 * K)
    t5_rows = sb("t5_rows", [P, 4, BIAS_X], F32, QT + 4 * K)
    V = Z + 88 * K
    v_hi = sb("v_hi", [P, NT, 2, 192], F32R, V)
    v_lo = sb("v_lo", [P, NT, 2, 192], F32R, V + 6 * K)
    ffn_t = sb("ffn_t", [P, 2, S], F32, V)
    ffn_g = sb("ffn_g", [P, 2, S], F32, V + 4 * K)
    ffn_f = sb("ffn_f", [P, 2, S], F32, V + 8 * K)
    bias_b = sb("bias_b", [P, 4, 384], F32, V + 12 * K)
    const = sb("const", [P, N_CONST], F32, V + 18 * K)
    at_params = V + 18 * K + (4 * N_CONST + 31) // 32 * 32
    params = sb("params", [P, N_PARAM], F32, at_params)
    tiny = sb("tiny", [P, 72], F32, at_params + (4 * N_PARAM + 31) // 32 * 32)

    def scratch(name, offset):
        return dict(sq=sb(f"sq_{name}", [P, 2, S], F32, offset), sum=sb(f"sum_{name}", [P, S], F32, offset + 4 * K),
                    tmp=sb(f"tmp_{name}", [P, 3, S], F32, offset + 6 * K), diag=sb(f"diag_{name}", [P, S], F32, offset + 12 * K))

    norm_z, norm_h = scratch("z", Z + 16 * K), scratch("h", 32 * K)
    scratch_of = dict(pre_mix=norm_z, post_mix=norm_z, pre_ffn=norm_z, post_ffn=norm_h)
    kept_h = sb("kept_h", [P, KD, S], F32, 16 * K)
    kept_of = dict(post_mix=gates, post_ffn=kept_h)

    def c(name):
        return const[:, CONST[name][0]:CONST[name][1]]

    def param(name, j=0, n=1):
        a = PARAMS[name][0] + j
        return params[:, a:a + n]

    ident, ones = c("ident"), c("ones")
    negmax, sums, recip, esink, maxima = (tiny[:, 4 * i:4 * i + 4] for i in range(5))
    r_in, r_out, r_tmp = tiny[:, 0:24], tiny[:, 24:48], tiny[:, 48:72]

    def in_sequence(ap):
        return ap.rearrange("p (r b c) -> p b r c", r=ROWS, b=NT)

    def in_blocks(ap):
        return ap.rearrange("p (b r c) -> p b r c", r=ROWS, b=NT)


    with ExitStack() as ctx:
        def psum(name):
            return ctx.enter_context(nc.psum_tensor(name, [P, 512], F32))

        def sem(name):
            return ctx.enter_context(nc.semaphore(name))

        main = [psum(f"main{i}") for i in range(2)]
        work = [psum(f"work{i}") for i in range(3)]
        turn = [psum(f"turn{i}") for i in range(2)]
        pv = psum("pv")

        loaded = sem("loaded")
        piece_in = [sem(f"piece_in{i}") for i in range(2)]
        piece_hi = sem("piece_hi")
        piece_split = sem("piece_split")
        main_done = sem("main_done")
        down_half = sem("down_half")
        work_done = sem("work_done")
        turn_done = sem("turn_done")
        pv_done = sem("pv_done")
        hi_done = sem("hi_done")
        lo_done = sem("lo_done")
        copied = sem("copied")
        max_done = sem("max_done")
        exp_done = sem("exp_done")
        prob_done = sem("prob_done")
        bias_done = sem("bias_done")
        tanh_done = sem("tanh_done")
        y_used = sem("y_used")
        merged_done = sem("merged_done")
        squared = sem("squared")
        kept_done = sem("kept_done")
        recip_done = sem("recip_done")
        summed = sem("summed")
        diag_done = sem("diag_done")
        scaled = sem("scaled")
        x_done = sem("x_done")
        ffn_tanh = sem("ffn_tanh")
        ffn_gate = sem("ffn_gate")
        ffn_full = sem("ffn_full")
        latents = sem("latents")
        c_ready = sem("c_ready")
        v_clear = sem("v_clear")
        chain = sem("chain")
        t5_sem = sem("t5_sem")
        t5_mm = sem("t5_mm")
        t5_copied = sem("t5_copied")
        t5_ready = sem("t5_ready")
        rpb_sem = sem("rpb_sem")
        rpb_in_place = sem("rpb_in_place")
        waited = sem("waited")
        stored = sem("stored")

        def value_place(part, b, t):
            place = part[:, t, :, :].rearrange("p a (c d) -> p a c d", d=HD)[:, :, 0:3:2, :]
            return place if b in "AD" else place[:, 0]

        block = ctx.enter_context(nc.Block())

        @block.sync
        def _(sp):
            sp.dma_start(const[:, :], const_in).then_inc(loaded, 16)
            sp.dma_start(x[:, :, :], x_in).then_inc(loaded, 16)
            sp.dma_start(hot[:, :], hot_in).then_inc(loaded, 16)
            sp.dma_start(t5[:, :, :], t5_in).then_inc(loaded, 16)

            def load(l, n, slot, size):
                sp.wait_ge(piece_split, l * NP_ + n + 1)
                src = stream[bass.ds(l * NP_ + n, 1), :, 0:size].rearrange("a p c -> (a p) c")
                sp.dma_start(raw[:, slot, 0:size], src).then_inc(piece_in[slot], 16)

            with sp.Fori(0, L) as l:
                for n in range(4):
                    load(l, n, n % 2, PIECES[n][1])
                with sp.Fori(2, DOWN0 // 2) as i:
                    for s in range(2):
                        load(l, 2 * i + s, s, 2048)
                with sp.Fori(DOWN0 // 2, NP_ // 2) as i:
                    for s in range(2):
                        load(l, 2 * i + s, s, KH * P)
            sp.wait_ge(x_done, 1 + L * 2 * KD)
            sp.dma_start(out, x[:, :, :]).then_inc(stored, 16)
            sp.wait_ge(stored, 16)

        @block.gpsimd
        def _(pool):
            pool.sem_inc(piece_split, 2)

            def split(l, n, slot, size, freed):
                pool.wait_ge(piece_in[slot], l * (8 * NP_) + (n // 2 if isinstance(n, int) else n[1]) * 16 + 16)
                pool.wait_ge(*freed)
                pool.sem_inc(waited, 1)
                pool.tensor_scalar(w_hi[:, slot, 0:size], raw[:, slot, 0:size], 1.0, 0.0, ALU.mult, ALU.add).then_inc(piece_hi, 1)
                m = n if isinstance(n, int) else n[0]
                pool.wait_ge(piece_hi, l * NP_ + m + 1)
                pool.tensor_tensor(w_lo[:, slot, 0:size], raw[:, slot, 0:size], w_hi[:, slot, 0:size].bitcast(F32),
                                   ALU.subtract).then_inc(piece_split, 1)

            ends = dict(Dcq=(work_done, "Dcq1"), Dckv=(work_done, "Dckv1"), Dup=(work_done, "Dkv3"),
                        Aq=(work_done, "Aq1"), Ak=(work_done, "Ak1"), Av=(work_done, "Av1"), Bq=(work_done, "Bq1"),
                        Bkv=(work_done, "Bv"), Cq=(work_done, "Cq1"), Ckv=(work_done, "Cv"))

            def free_after(l, n):
                name = PIECES[n][0]
                if name in ends:
                    return work_done, at(l, N_WORK, WORK_AT[ends[name][1]] + 1)
                if name.startswith("gate"):
                    return main_done, at(l, N_MAIN, GATE0[name[4]] + 2 * int(name[5]) + 2 + 1)
                return main_done, at(l, N_MAIN, Y0[name[6]] + KD + 1)

            with pool.Fori(0, L) as l:
                for n in range(OUT0 + 2):
                    split(l, n, n % 2, PIECES[n][1], free_after(l, n - 2) if n >= 2 else (main_done, at(l, N_MAIN, 1)))
                with pool.Fori(OUT0 // 2 + 1, DOWN0 // 2) as i:
                    for s in range(2):
                        split(l, (2 * i + s, i), s, 2048, (main_done, at(l, N_MAIN, (2 * i + s - OUT0) * 2 + WOUT0 - 2 + 1)))
                for n in (DOWN0, DOWN0 + 1):
                    split(l, n, n % 2, KH * P, (main_done, at(l, N_MAIN, (n - OUT0) * 2 + WOUT0 - 2 + 1)))
                with pool.Fori(DOWN0 // 2 + 1, NP_ // 2) as i:
                    split(l, (2 * i, i), 0, KH * P, (down_half, l * KD + i - DOWN0 // 2))
                    split(l, (2 * i + 1, i), 1, KH * P, (main_done, at(l, N_MAIN, DOWNM0 + i - DOWN0 // 2 + 1)))

        @block.tensor
        def _(pe):
            pe.sem_inc(main_done, 1)
            pe.wait_ge(loaded, 64)
            for h in range(4):
                bank = work[h] if h < 3 else pv
                pe.matmul(bank[:, :], t5[:, h, :], hot[:, :], start=True, stop=True).then_inc(t5_mm, 1)
            pe.wait_ge(t5_copied, 4)

            def three(dst, a_hi, a_lo, b_hi, b_lo, first, last, **kw):
                pe.matmul(dst, a_hi, b_hi, start=first, stop=False, **kw)
                pe.matmul(dst, a_hi, b_lo, start=False, stop=False, **kw)
                return pe.matmul(dst, a_lo, b_hi, start=False, stop=last, **kw)

            def wait_piece(l, n):
                pe.wait_ge(piece_split, at(l, NP_, n + 3))

            def wait_split(l, name):
                pe.wait_ge(lo_done, at(l, N_SPLIT, SPLIT_AT[name] + 1))

            def wait_main(l, m):
                p = m - 2
                if p < 0:
                    return
                b, j = p // 16, p % 16
                if j < KD:
                    pe.wait_ge(tanh_done, at(l, 4 * KD, KD * b + j + 1))
                else:
                    pe.wait_ge(y_used, at(l, 4 * KD, KD * b + j - KD + 1))

            def wait_work(l, w):
                p = w - 3
                if p < 0:
                    return
                n = WORK[p]
                if n[0] == "score":
                    q = 16 * BR.index(n[1]) + 4 * n[2] + n[3]
                    pe.wait_ge(max_done if banded(n[1]) else exp_done, at(l, 64, q + 1))
                elif n in ("Dcq0", "Dcq1", "Dckv0", "Dckv1", "Bv", "Cq0", "Cq1", "Ck") or n[:2] == "Dq":
                    pe.wait_ge(copied, at(l, N_COPY, COPY_AT[n] + 1))
                elif n[:3] == "Dkv":
                    wait_split(l, ("V", "D", int(n[3])))
                elif n[:2] == "Av":
                    wait_split(l, ("V", "A", 2 * int(n[2]) + 1))
                elif n == "Cv":
                    wait_split(l, ("V", "C", NT - 1))
                else:
                    wait_split(l, n)

            def wait_turn(l, t):
                p = t - 2
                if p < 0:
                    return
                n = TURN[p]
                if n[0] == "stat":
                    pe.wait_ge(diag_done, at(l, 4, NORMS.index(n[1]) + 1))
                elif n[0] == "spread":
                    pe.wait_ge(scaled, at(l, 4 * KD, KD * (NORMS.index(n[1]) + 1)))
                elif n == "Bv":
                    wait_split(l, ("V", "B", NT - 1))
                else:
                    wait_split(l, n)

            def norm(l, name):
                sc, i = scratch_of[name], NORMS.index(name)
                t = TURN_AT[("stat", name)]
                wait_turn(l, t)
                pe.wait_ge(summed, at(l, 4 * KD, KD * (i + 1)))
                for tt in range(NT):
                    last = pe.matmul(turn[t % 2][:, tt:tt + 1], sc["sum"][:, P * tt:P * tt + P], ones[:, 0:1], start=True, stop=True)
                last.then_inc(turn_done, 1)
                wait_turn(l, t + 1)
                pe.wait_ge(diag_done, at(l, 4, i + 1))
                pe.matmul(turn[(t + 1) % 2][:, :], ones, sc["diag"][:, :], start=True, stop=True).then_inc(turn_done, 1)

            def gate_steps(l, b, point):
                before = GATE_POINTS[b][point - 1] if point else 0
                for s in range(before, GATE_POINTS[b][point]):
                    j, k, which = s // STEPS, s % STEPS // 3, s % 3
                    m = GATE0[b] + j
                    if s % STEPS == 0:
                        wait_main(l, m)
                        if j % 2 == 0:
                            wait_piece(l, PIECE[f"gate{b}{j // 2}"])
                    slot = PIECE[f"gate{b}{j // 2}"] % 2
                    col = 256 * k + P * (j % 2)
                    w = (w_lo if which == 2 else w_hi)[:, slot, col:col + P]
                    mm = pe.matmul(main[m % 2][:, :], w, (h_lo if which == 1 else h_hi)[:, k, :],
                                   start=(s % STEPS == 0), stop=(s % STEPS == STEPS - 1))
                    if s % STEPS == STEPS - 1:
                        mm.then_inc(main_done, 1)

            def by_feature(l, name, n, col, width, first=False):
                w = WORK_AT[name]
                wait_work(l, w)
                for k in range(KD):
                    if first:
                        wait_split(l, ("h", "pre_mix", k))
                    a = width * k + col
                    mm = three(work[w % 3][:, :], w_hi[:, n % 2, a:a + P], w_lo[:, n % 2, a:a + P],
                               h_hi[:, k, :], h_lo[:, k, :], k == 0, k == KD - 1)
                mm.then_inc(work_done, 1)

            def by_token(l, name, n, tiles, col, cols, width, first=False):
                w = WORK_AT[name]
                wait_work(l, w)
                for i, t in enumerate(tiles):
                    dst = work[w % 3][:, i * cols:(i + 1) * cols]
                    for k in range(KD):
                        if first and i == 0:
                            wait_split(l, ("h", "pre_mix", k))
                        a = width * k + col
                        mm = three(dst, h_hi[:, k, P * t:P * t + P], h_lo[:, k, P * t:P * t + P],
                                   w_hi[:, n % 2, a:a + cols], w_lo[:, n % 2, a:a + cols], k == 0, k == KD - 1)
                mm.then_inc(work_done, 1)

            def turn_tiles(l, name, sources, rows=P):
                t = TURN_AT[name]
                wait_turn(l, t)
                for i, src in enumerate(sources):
                    mm = pe.transpose(turn[t % 2][0:rows, P * i:P * i + P], src, ident)
                mm.then_inc(turn_done, 1)

            def queries(b, h):
                if b == "D":
                    return qd_hi[0:DQK, h, :], qd_lo[0:DQK, h, :]
                a = HD * (h % 2)
                return qa_hi[a:a + HD, h // 2, :], qa_lo[a:a + HD, h // 2, :]

            def keys(b, h):
                if b == "D":
                    return kd_hi[0:DQK, h, :], kd_lo[0:DQK, h, :]
                a, j = HD * (h % 2), h // 2 if b == "A" else 0
                return ka_hi[a:a + HD, j, :], ka_lo[a:a + HD, j, :]

            def head(l, b, h):
                (q_h, q_l), (k_h, k_l) = queries(b, h), keys(b, h)
                for t in range(NT):
                    w = WORK_AT[("score", b, h, t)]
                    ks = window(b, t)
                    a, n = P * ks[0], P * len(ks)
                    wait_work(l, w)
                    three(work[w % 3][:, 0:n], q_h[:, P * t:P * t + P], q_l[:, P * t:P * t + P],
                          k_h[:, a:a + n], k_l[:, a:a + n], True, True).then_inc(work_done, 1)
                    gate_steps(l, b, gate_point(b, h, t))

                def turn_prob(k):
                    t = TURN_AT[("prob", b, h, k)]
                    wait_turn(l, t)
                    qs = [q for q in range(NT) if k in window(b, q)]
                    pe.wait_ge(prob_done, at(l, 64, 16 * BR.index(b) + 4 * h + qs[-1] + 1))
                    for q in qs:
                        a = P * (k - window(b, q)[0])
                        mm = pe.transpose(turn[t % 2][:, P * q:P * q + P], prob[:, q, a:a + P], ident)
                    mm.then_inc(turn_done, 1)

                def values(k):
                    qs = [q for q in range(NT) if k in window(b, q)]
                    a, z = P * qs[0], P * (qs[-1] + 1)
                    wait_split(l, ("prob", b, h, k))
                    v = slice(HD * (h % 2), HD * (h % 2) + P)
                    j = 0 if b in "BC" else h // 2
                    mm = three(pv[:, a:z], v_hi[:, k, j, v], v_lo[:, k, j, v], pt_hi[:, k % 2, a:z],
                               pt_lo[:, k % 2, a:z], h % 2 == 0 and k == 0, h % 2 == 1 and k == NT - 1, skip_group_check=True)
                    if h % 2 == 1 and k == NT - 1:
                        mm.then_inc(pv_done, 1)

                turn_prob(0)
                gate_steps(l, b, gate_point(b, h, 4))
                turn_prob(1)
                gate_steps(l, b, gate_point(b, h, 5))
                if h == 2:
                    wait_split(l, ("o", b, 0))
                values(0)
                turn_prob(2)
                gate_steps(l, b, gate_point(b, h, 6))
                values(1)
                turn_prob(3)
                values(2)
                values(3)

            def branch_out(l, b):
                n = PIECE[f"branch{b}"]
                wait_piece(l, n)
                for d in range(KD):
                    m = Y0[b] + d
                    wait_main(l, m)
                    for k in range(2):
                        if d == 0:
                            wait_split(l, ("o", b, k))
                        a = DM * k + P * d
                        mm = three(main[m % 2][:, :], w_hi[:, n % 2, a:a + P], w_lo[:, n % 2, a:a + P],
                                   o_hi[:, k, :], o_lo[:, k, :], k == 0, k == 1)
                    mm.then_inc(main_done, 1)

            with pe.Fori(0, L) as l:
                norm(l, "pre_mix")

                wait_piece(l, PIECE["Dcq"])
                by_token(l, "Dcq0", PIECE["Dcq"], (0, 1), 0, 256, 256, first=True)
                by_token(l, "Dcq1", PIECE["Dcq"], (2, 3), 0, 256, 256)
                wait_piece(l, PIECE["Dckv"])
                by_token(l, "Dckv0", PIECE["Dckv"], (0, 1), 0, 160, 160)
                by_token(l, "Dckv1", PIECE["Dckv"], (2, 3), 0, 160, 160)
                gate_steps(l, "D", 0)
                for j in range(3):
                    pe.wait_ge(latents, at(l, 4, 1 if j < 2 else 2))
                    turn_tiles(l, ("latent", j), [d_tm[:, t, P * j:P * j + P] for t in range(NT)])
                gate_steps(l, "D", 1)
                n = PIECE["Dup"]
                wait_piece(l, n)
                for t in range(NT):
                    w = WORK_AT[f"Dq{t}"]
                    wait_work(l, w)
                    for j in range(2):
                        if t == 0:
                            wait_split(l, ("latent", j))
                        mm = three(work[w % 3][:, 0:384], lat_hi[:, j, P * t:P * t + P], lat_lo[:, j, P * t:P * t + P],
                                   w_hi[:, n % 2, 384 * j:384 * j + 384], w_lo[:, n % 2, 384 * j:384 * j + 384], j == 0, j == 1)
                    mm.then_inc(work_done, 1)
                wait_split(l, ("latent", 2))
                for t in range(NT):
                    w = WORK_AT[f"Dkv{t}"]
                    wait_work(l, w)
                    three(work[w % 3][:, :], lat_hi[:, 2, P * t:P * t + P], lat_lo[:, 2, P * t:P * t + P],
                          w_hi[:, n % 2, 768:1280], w_lo[:, n % 2, 768:1280], True, True).then_inc(work_done, 1)
                gate_steps(l, "D", 2)
                pe.wait_ge(copied, at(l, N_COPY, COPY_AT["Dk3"] + 1))
                for h in range(4):
                    for name, tm, count in (("Dq", dq_tm, 4), ("Dk", dk_tm, 3)):
                        pe.wait_ge(latents, at(l, 4, count))
                        turn_tiles(l, (name, h), [tm[:, t, DQK * h:DQK * h + DQK] for t in range(NT)], DQK)
                for h in range(4):
                    wait_split(l, ("Dk", h))
                    head(l, "D", h)
                branch_out(l, "D")

                for name in ("Aq", "Ak"):
                    wait_piece(l, PIECE[name])
                    for j in range(2):
                        by_feature(l, f"{name}{j}", PIECE[name], P * j, 256)
                wait_piece(l, PIECE["Av"])
                for j in range(2):
                    by_token(l, f"Av{j}", PIECE["Av"], (2 * j, 2 * j + 1), 0, 256, 256)
                for h in range(4):
                    if h == 0:
                        wait_split(l, ("V", "A", NT - 1))
                    head(l, "A", h)
                branch_out(l, "A")

                wait_piece(l, PIECE["Bq"])
                for j in range(2):
                    by_feature(l, f"Bq{j}", PIECE["Bq"], P * j, 256)
                wait_piece(l, PIECE["Bkv"])
                by_feature(l, "Bk", PIECE["Bkv"], 0, 256)
                by_feature(l, "Bv", PIECE["Bkv"], P, 256)
                pe.wait_ge(copied, at(l, N_COPY, COPY_AT["Bv"] + 1))
                turn_tiles(l, "Bv", [b_fm[:, P * t:P * t + P] for t in range(NT)])
                for h in range(4):
                    if h == 0:
                        wait_split(l, ("V", "B", NT - 1))
                    head(l, "B", h)
                branch_out(l, "B")

                wait_piece(l, PIECE["Cq"])
                by_token(l, "Cq0", PIECE["Cq"], (0, 1), 0, 256, 256)
                by_token(l, "Cq1", PIECE["Cq"], (2, 3), 0, 256, 256)
                wait_piece(l, PIECE["Ckv"])
                by_token(l, "Ck", PIECE["Ckv"], range(NT), 0, P, 256)
                by_token(l, "Cv", PIECE["Ckv"], range(NT), P, P, 256)
                gate_steps(l, "C", 0)
                for j in range(3):
                    pe.wait_ge(c_ready, at(l, 1, 1))
                    turn_tiles(l, ("C", j), [c_tm[:, t, P * j:P * j + P] for t in range(NT)])
                for h in range(4):
                    if h == 0:
                        wait_split(l, ("C", 2))
                    head(l, "C", h)
                branch_out(l, "C")

                with pe.Fori(0, 2) as i:
                    for s in range(2):
                        pe.wait_ge(piece_split, l * NP_ + 2 * i + (OUT0 + s + 3))
                        for j in range(2):
                            m = 2 * s + j
                            if m < 2:
                                pe.wait_ge(y_used, at(l, 4 * KD, 3 * KD + 6 + m + 1))
                            pe.wait_ge(kept_done, l * 2 * KD + 4 * i + m + 1)
                            for k in range(KD):
                                if m == 0:
                                    wait_split(l, ("merged", k))
                                a = 256 * k + P * j
                                mm = three(main[m % 2][:, :], w_hi[:, s, a:a + P], w_lo[:, s, a:a + P],
                                           h_hi[:, k, :], h_lo[:, k, :], k == 0, k == KD - 1)
                            mm.then_inc(main_done, 1)

                norm(l, "post_mix")
                norm(l, "pre_ffn")

                with pe.Fori(0, KF // 2) as i:
                    for s in range(2):
                        pe.wait_ge(piece_split, l * NP_ + 2 * i + (GU0 + s + 3))
                        for j in range(2):
                            pe.wait_ge(ffn_full if j else ffn_gate, l * KF + 2 * i + s + 1)
                            for k in range(KD):
                                if s == 0 and j == 0:
                                    wait_split(l, ("h", "pre_ffn", k))
                                a = 256 * k + P * j
                                mm = three(main[j][:, :], w_hi[:, s, a:a + P], w_lo[:, s, a:a + P],
                                           h_hi[:, k, :], h_lo[:, k, :], k == 0, k == KD - 1)
                            mm.then_inc(main_done, 1)

                with pe.Fori(0, KD // 2) as i:
                    for d in range(2):
                        pe.wait_ge(ffn_full if d else ffn_gate, at(l, KF, KF + 1))
                        pe.wait_ge(kept_done, l * 2 * KD + 2 * i + KD + d + 1)
                        for s in range(2):
                            pe.wait_ge(piece_split, l * NP_ + 4 * i + (DOWN0 + 2 * d + s + 3))
                            for k in range(KH):
                                if d == 0:
                                    wait_split(l, ("act", KH * s + k))
                                kk = KH * s + k
                                mm = three(main[d][:, :], w_hi[:, s, P * k:P * k + P], w_lo[:, s, P * k:P * k + P],
                                           act_hi[:, kk, :], act_lo[:, kk, :], kk == 0, kk == KF - 1)
                            mm.then_inc(main_done if s else down_half, 1)
                norm(l, "post_ffn")

        @block.scalar
        def _(act):
            splits = iter(SPLIT)

            def hi(l, name, dst, src, scale=1.0):
                assert next(splits) == name
                act.activation(dst, src, ACT.Copy, scale=scale).then_inc(hi_done, 1)

            def wait_turn_done(l, name):
                act.wait_ge(turn_done, at(l, N_TURN, TURN_AT[name] + 1))

            def wait_work_done(l, name):
                act.wait_ge(work_done, at(l, N_WORK, WORK_AT[name] + 1))

            copies = iter(COPY)

            def copy(l, name, dst, src):
                assert next(copies) == name
                act.activation(dst, src, ACT.Copy).then_inc(copied, 1)

            def squares_of_x(l, name):
                i, sc = NORMS.index(name), scratch_of[name]
                for d in range(KD):
                    act.wait_ge(x_done, at(l, 2 * KD, 1) if name == "pre_mix" else at(l, 2 * KD, 1 + d + 1))
                    if d >= 2:
                        act.wait_ge(summed, at(l, 4 * KD, KD * i + d - 1))
                    act.activation(sc["sq"][:, d % 2, :], x[:, d, :], ACT.Square).then_inc(squared, 1)

            def keep(l, name):
                i, sc, kept = NORMS.index(name), scratch_of[name], kept_of[name]
                m0 = WOUT0 if name == "post_mix" else DOWNM0
                for d in range(KD):
                    act.wait_ge(main_done, at(l, N_MAIN, m0 + d + 2))
                    if d >= 2:
                        act.wait_ge(summed, at(l, 4 * KD, KD * i + d - 1))
                    act.activation(sc["sq"][:, d % 2, :], main[d % 2][:, :], ACT.Square).then_inc(squared, 1)
                    act.activation(kept[:, d, :], main[d % 2][:, :], ACT.Copy).then_inc(kept_done, 1)

            def h_parts(l, name):
                i, sc = NORMS.index(name), scratch_of[name]
                for d in range(KD):
                    act.wait_ge(scaled, at(l, 4 * KD, KD * i + d + 1))
                    hi(l, ("h", name, d), h_hi[:, d, :], sc["tmp"][:, d % 3, :])

            def gate_tanh(l, b, point):
                for j in gate_tiles(b, point):
                    m = GATE0[b] + j
                    act.wait_ge(main_done, at(l, N_MAIN, m + 2))
                    act.activation(gates[:, j, :], main[m % 2][:, :], ACT.Tanh, scale=0.5).then_inc(tanh_done, 1)

            def value_parts(l, b, t, src):
                hi(l, ("V", b, t), value_place(v_hi, b, t), src)

            def head(l, b, h):
                q0 = 16 * BR.index(b) + 4 * h
                for t in range(NT):
                    w = WORK_AT[("score", b, h, t)]
                    n = P * len(window(b, t))
                    src = prob[:, t, 0:n] if banded(b) else work[w % 3][:, 0:n]
                    act.wait_ge(max_done, at(l, 64, q0 + t + 1))
                    e = act.activation(prob[:, t, 0:n], src, ACT.Exp, bias=negmax[:, t:t + 1], accum_out=sums[:, t:t + 1])
                    if b == "B":
                        e = act.activation(esink[:, t:t + 1], param("sink", h), ACT.Exp, bias=negmax[:, t:t + 1])
                    e.then_inc(exp_done, 1)
                    gate_tanh(l, b, gate_point(b, h, t))
                for k in range(NT):
                    qs = [q for q in range(NT) if k in window(b, q)]
                    a, z = P * qs[0], P * (qs[-1] + 1)
                    wait_turn_done(l, ("prob", b, h, k))
                    hi(l, ("prob", b, h, k), pt_hi[:, k % 2, a:z], turn[TURN_AT[("prob", b, h, k)] % 2][:, a:z])
                    if k < 3:
                        gate_tanh(l, b, gate_point(b, h, 4 + k))
                if h % 2:
                    act.wait_ge(pv_done, at(l, 8, 2 * BR.index(b) + h // 2 + 1))
                    dst, src = o_hi[:, h // 2, :], pv[:, :]
                    if b == "B":
                        dst, src = in_blocks(dst), in_sequence(src)
                    hi(l, ("o", b, h // 2), dst, src)

            act.sem_inc(kept_done, 2)
            act.wait_ge(t5_copied, 4)
            act.dma_start(t5_line, t5_rows[:, :, :].rearrange("p h x -> p (h x)")).then_inc(t5_sem, 16)
            act.wait_ge(t5_sem, 16)
            act.dma_start(bias_b[:, :, :], bass.AP(tensor=t5_line.tensor, offset=P - 1,
                                                   ap=[[4 * BIAS_X - 1, P], [BIAS_X, 4], [1, 384]])).then_inc(t5_ready, 16)
            act.wait_ge(loaded, 64)
            with act.Fori(0, L) as l:
                line = rpb_in[bass.ds(l, 1), :]
                act.dma_start(rpb_line, bass.AP(tensor=line.tensor, offset=line.offset, ap=[[0, 16], [1, N_RPB]])).then_inc(rpb_sem, 16)
                squares_of_x(l, "pre_mix")
                h_parts(l, "pre_mix")

                for i in range(2):
                    wait_work_done(l, f"Dcq{i}")
                    copy(l, f"Dcq{i}", d_tm[:, 2 * i:2 * i + 2, 0:256], work[WORK_AT[f"Dcq{i}"] % 3][:, :].rearrange("p (t c) -> p t c", t=2))
                for i in range(2):
                    wait_work_done(l, f"Dckv{i}")
                    copy(l, f"Dckv{i}", d_tm[:, 2 * i:2 * i + 2, 256:416],
                         work[WORK_AT[f"Dckv{i}"] % 3][:, 0:320].rearrange("p (t c) -> p t c", t=2))
                gate_tanh(l, "D", 0)
                for j in range(3):
                    wait_turn_done(l, ("latent", j))
                    hi(l, ("latent", j), lat_hi[:, j, :], turn[TURN_AT[("latent", j)] % 2][:, :], param("latent", j))
                gate_tanh(l, "D", 1)
                for t in range(NT):
                    wait_work_done(l, f"Dq{t}")
                    copy(l, f"Dq{t}", dq_tm[:, t, :], work[WORK_AT[f"Dq{t}"] % 3][:, 0:384])
                act.wait_ge(v_clear, at(l, 2, 2))
                for t in range(NT):
                    wait_work_done(l, f"Dkv{t}")
                    kv = work[WORK_AT[f"Dkv{t}"] % 3][:, :].rearrange("p (h c) -> p h c", h=4)
                    copy(l, f"Dk{t}", dk_tm[:, t, :].rearrange("p (h c) -> p h c", h=4)[:, :, 0:HD], kv[:, :, 0:HD])
                    value_parts(l, "D", t, view(kv[:, :, HD:P], [[2 * P, 2], [P, 2], [1, HD]]))
                gate_tanh(l, "D", 2)
                for h in range(4):
                    wait_turn_done(l, ("Dq", h))
                    hi(l, ("Dq", h), qd_hi[0:DQK, h, :], turn[TURN_AT[("Dq", h)] % 2][0:DQK, :], DQK ** -0.5)
                    wait_turn_done(l, ("Dk", h))
                    hi(l, ("Dk", h), kd_hi[0:DQK, h, :], turn[TURN_AT[("Dk", h)] % 2][0:DQK, :])
                for h in range(4):
                    head(l, "D", h)

                for name, dst, scale in (("Aq", qa_hi, HD ** -0.5), ("Ak", ka_hi, 1.0)):
                    for j in range(2):
                        wait_work_done(l, f"{name}{j}")
                        hi(l, f"{name}{j}", dst[:, j, :], work[WORK_AT[f"{name}{j}"] % 3][:, :], scale)
                        if name == "Aq" and j == 0:
                            act.wait_ge(rpb_sem, 16 * l + 16)
                            for r in range(ROWS):
                                act.dma_start(rpb[16 * r:16 * r + 16, :, :],
                                              bass.AP(tensor=rpb_line.tensor, offset=(7 - r) * RPB_ROW + 15,
                                                      ap=[[N_RPB - 1, 16], [RPB_HEAD, 4], [1, 512]])).then_inc(rpb_in_place, 16)
                for j in range(2):
                    wait_work_done(l, f"Av{j}")
                    for i in range(2):
                        src = work[WORK_AT[f"Av{j}"] % 3][:, 256 * i:256 * i + 256].rearrange("p (a c d) -> p a c d", a=2, c=2)
                        value_parts(l, "A", 2 * j + i, src)
                for h in range(4):
                    head(l, "A", h)

                for j in range(2):
                    wait_work_done(l, f"Bq{j}")
                    hi(l, f"Bq{j}", in_sequence(qa_hi[:, j, :]), in_blocks(work[WORK_AT[f"Bq{j}"] % 3][:, :]), HD ** -0.5)
                wait_work_done(l, "Bk")
                hi(l, "Bk", in_sequence(ka_hi[:, 0, :]), in_blocks(work[WORK_AT["Bk"] % 3][:, :]))
                wait_work_done(l, "Bv")
                copy(l, "Bv", in_sequence(b_fm[:, :]), in_blocks(work[WORK_AT["Bv"] % 3][:, :]))
                wait_turn_done(l, "Bv")
                for t in range(NT):
                    src = turn[TURN_AT["Bv"] % 2][:, P * t:P * t + P]
                    value_parts(l, "B", t, src.rearrange("p (c d) -> p c d", d=HD))
                for h in range(4):
                    head(l, "B", h)

                for i in range(2):
                    wait_work_done(l, f"Cq{i}")
                    copy(l, f"Cq{i}", c_tm[:, 2 * i:2 * i + 2, 0:256], work[WORK_AT[f"Cq{i}"] % 3][:, :].rearrange("p (t c) -> p t c", t=2))
                wait_work_done(l, "Ck")
                copy(l, "Ck", c_tm[:, :, 256:384], work[WORK_AT["Ck"] % 3][:, :].rearrange("p (t c) -> p t c", t=NT))
                wait_work_done(l, "Cv")
                for t in range(NT):
                    src = work[WORK_AT["Cv"] % 3][:, P * t:P * t + P]
                    value_parts(l, "C", t, src.rearrange("p (c d) -> p c d", d=HD))
                gate_tanh(l, "C", 0)
                for j in range(3):
                    wait_turn_done(l, ("C", j))
                    src = turn[TURN_AT[("C", j)] % 2][:, :]
                    if j < 2:
                        hi(l, ("C", j), qa_hi[:, j, :], src, HD ** -0.5)
                    else:
                        hi(l, ("C", j), ka_hi[:, 0, :], src)
                for h in range(4):
                    head(l, "C", h)
                for d in range(KD):
                    act.wait_ge(merged_done, at(l, 3 * KD, 2 * KD + d + 1))
                    hi(l, ("merged", d), h_hi[:, d, :], merged[:, d, :], 0.5)

                keep(l, "post_mix")
                squares_of_x(l, "pre_ffn")
                h_parts(l, "pre_ffn")
                with act.Fori(0, KF // 2) as i:
                    for s in range(2):
                        act.wait_ge(main_done, l * N_MAIN + 4 * i + (GUM0 + 2 * s + 2))
                        act.activation(ffn_t[:, s, :], main[0][:, :], ACT.Tanh, scale=0.5).then_inc(ffn_tanh, 1)
                        act.wait_ge(ffn_full, l * KF + 2 * i + s + 2)
                        act.sem_inc(waited, 1)
                        act.activation(act_hi[:, bass.ds(2 * i + s, 1), :].rearrange("p a s -> p (a s)"), ffn_f[:, s, :],
                                       ACT.Copy).then_inc(hi_done, 1)
                keep(l, "post_ffn")

        @block.vector
        def _(dve):
            dve.sem_inc(x_done, 1)
            dve.sem_inc(ffn_gate, 1)
            dve.sem_inc(ffn_full, 1)
            for h in range(4):
                dve.wait_ge(t5_mm, h + 1)
                dve.tensor_copy(t5_rows[:, h, :], (work[h] if h < 3 else pv)[:, :]).then_inc(t5_copied, 1)
            dve.wait_ge(loaded, 64)
            dve.wait_ge(t5_ready, 16)
            steps = [0]

            def step(l, ins):
                ins.then_inc(chain, 1)
                steps[0] += 1
                dve.wait_ge(chain, at(l, N_CHAIN, steps[0]))

            splits = iter(SPLIT)

            def lo(l, name, dst, src, part, scale=None, after=None):
                assert next(splits) == name
                dve.wait_ge(hi_done, at(l, N_SPLIT, SPLIT_AT[after or name] + 1))
                if scale is None:
                    dve.tensor_tensor(dst, src, part.bitcast(F32), ALU.subtract).then_inc(lo_done, 1)
                else:
                    dve.scalar_tensor_tensor(out=dst, in0=src, scalar=scale, in1=part.bitcast(F32),
                                             op0=ALU.mult, op1=ALU.subtract).then_inc(lo_done, 1)

            def scaled_lo(l, name, dst, src, part, scale):
                assert next(splits) == name
                dve.wait_ge(hi_done, at(l, N_SPLIT, SPLIT_AT[name] + 1))
                for b in range(NT):
                    e = dve.scalar_tensor_tensor(out=dst[:, b], in0=src[:, b], scalar=scale, in1=part[:, b].bitcast(F32),
                                                 op0=ALU.mult, op1=ALU.subtract)
                e.then_inc(lo_done, 1)

            def root(l, n):
                v, y, t = r_in[:, 0:n], r_out[:, 0:n], r_tmp[:, 0:n]
                step(l, dve.tensor_scalar(y.bitcast(I32), v.bitcast(I32), -0.5, float(0x5F3759DF), ALU.mult, ALU.add))
                for _ in range(3):
                    step(l, dve.tensor_tensor(t, y, y, ALU.mult))
                    step(l, dve.tensor_tensor(t, t, v, ALU.mult))
                    step(l, dve.tensor_scalar(t, t, -0.5, 1.5, ALU.mult, ALU.add))
                    step(l, dve.tensor_tensor(y, y, t, ALU.mult))

            def sum_squares(l, name):
                i, sc = NORMS.index(name), scratch_of[name]
                for d in range(KD):
                    dve.wait_ge(squared, at(l, 4 * KD, KD * i + d + 1))
                    if d == 0:
                        dve.tensor_copy(sc["sum"][:, :], sc["sq"][:, 0, :]).then_inc(summed, 1)
                    else:
                        dve.wait_ge(summed, at(l, 4 * KD, KD * i + d))
                        dve.tensor_tensor(sc["sum"][:, :], sc["sum"][:, :], sc["sq"][:, d % 2, :], ALU.add).then_inc(summed, 1)

            def factors(l, name):
                sc, t = scratch_of[name], TURN_AT[("stat", name)]
                dve.wait_ge(turn_done, at(l, N_TURN, t + 1))
                step(l, dve.tensor_scalar(r_in[:, 0:NT], turn[t % 2][:, 0:NT], 1.0 / DM, EPS, ALU.mult, ALU.add))
                root(l, NT)
                diag = sc["diag"][:, :].rearrange("p (t c) -> p t c", t=NT)
                dve.tensor_tensor(diag, view(ident, [[0, NT], [1, P]]), view(r_out, [[1, NT], [0, P]]), ALU.mult).then_inc(diag_done, 1)
                dve.wait_ge(turn_done, at(l, N_TURN, t + 2))

            def scale_tile(l, name, d, src):
                sc, t = scratch_of[name], TURN_AT[("spread", name)]
                dve.scalar_tensor_tensor(out=sc["tmp"][:, d % 3, :], in0=src, scalar=param(name, d), in1=turn[t % 2][:, :],
                                         op0=ALU.mult, op1=ALU.mult).then_inc(scaled, 1)

            def pre_norm(l, name):
                sum_squares(l, name)
                factors(l, name)
                for d in range(KD + 1):
                    if d < KD:
                        if d >= 3:
                            dve.wait_ge(lo_done, at(l, N_SPLIT, SPLIT_AT[("h", name, d - 3)] + 1))
                        scale_tile(l, name, d, x[:, d, :])
                    if d:
                        lo(l, ("h", name, d - 1), h_lo[:, d - 1, :], scratch_of[name]["tmp"][:, (d - 1) % 3, :], h_hi[:, d - 1, :])

            def post_norm(l, name):
                sum_squares(l, name)
                i = NORMS.index(name)
                dve.wait_ge(kept_done, at(l, 2 * KD, KD * (name == "post_ffn") + KD + 2))
                factors(l, name)
                for d in range(KD + 1):
                    if d < KD:
                        if d >= 3:
                            dve.wait_ge(x_done, at(l, 2 * KD, KD * (name == "post_ffn") + d - 1))
                        scale_tile(l, name, d, kept_of[name][:, d, :])
                    if d:
                        dve.wait_ge(scaled, at(l, 4 * KD, KD * i + d))
                        dve.tensor_tensor(x[:, d - 1, :], x[:, d - 1, :], scratch_of[name]["tmp"][:, (d - 1) % 3, :],
                                          ALU.add).then_inc(x_done, 1)

            def wait_work_done(l, name):
                dve.wait_ge(work_done, at(l, N_WORK, WORK_AT[name] + 1))

            def value_parts(l, b, t, src):
                last = dict(A=t | 1, D=t).get(b, NT - 1)
                lo(l, ("V", b, t), value_place(v_lo, b, t), src, value_place(v_hi, b, t), after=("V", b, last))

            def window_bias(l, h):
                a, blocks = 0, ((1, 2), (0, 3), (0, 2))
                for v, (b0, nb) in enumerate(blocks):
                    src = view(rpb[:, h, 16 * b0:], [[16, nb], [RPB_ROW, ROWS], [1, 16]])
                    mask = view(c("maskA")[:, 48 * v + 16 * b0:], [[16, nb], [0, ROWS], [1, 16]])
                    dst = bias_a[:, h % 2, a:a + nb * P].rearrange("p (b r c) -> p b r c", r=ROWS, c=16)
                    step(l, dve.tensor_tensor(dst, src, mask, ALU.add))
                    a += nb * P

            def head(l, b, h):
                q0, w0 = 16 * BR.index(b) + 4 * h, WORK_AT[("score", b, h, 0)]

                def maximum(t):
                    n = P * len(window(b, t))
                    scores = work[(w0 + t) % 3][:, 0:n]
                    dve.wait_ge(work_done, at(l, N_WORK, w0 + t + 1))
                    if not banded(b):
                        dve.tensor_reduce(negmax[:, t:t + 1], scores, AX.X, ALU.max, negate=True).then_inc(max_done, 1)
                        return
                    if b == "A":
                        bias = bias_a[:, h % 2, (0, 256, 256, 640)[t]:(0, 256, 256, 640)[t] + n]
                        least = -3.0e38
                    else:
                        bias = bias_b[:, h, (P if t == 0 else 0):(P if t == 0 else 0) + n]
                        least = param("sink", h)
                    dve.sem_inc(waited, 1)
                    dve.tensor_tensor_reduce(prob[:, t, 0:n], scores, bias, 1.0, least, ALU.add, ALU.max,
                                             maxima[:, t:t + 1]).then_inc(bias_done, 1)
                    dve.wait_ge(bias_done, at(l, 32, q0 - 16 + t + 1))
                    dve.tensor_scalar(negmax[:, t:t + 1], maxima[:, t:t + 1], -1.0, None, ALU.mult).then_inc(max_done, 1)

                def normalise(t):
                    n = P * len(window(b, t))
                    dve.wait_ge(exp_done, at(l, 64, q0 + t + 1))
                    if b == "B":
                        step(l, dve.tensor_tensor(sums[:, t:t + 1], sums[:, t:t + 1], esink[:, t:t + 1], ALU.add))
                    dve.reciprocal(recip[:, t:t + 1], sums[:, t:t + 1]).then_inc(recip_done, 1)
                    dve.wait_ge(recip_done, at(l, 64, q0 + t + 1))
                    dve.tensor_scalar(prob[:, t, 0:n], prob[:, t, 0:n], recip[:, t:t + 1], None, ALU.mult).then_inc(prob_done, 1)

                for t in range(NT + 1):
                    if t < NT:
                        maximum(t)
                    if t:
                        normalise(t - 1)
                for k in range(NT):
                    qs = [q for q in range(NT) if k in window(b, q)]
                    a, z = P * qs[0], P * (qs[-1] + 1)
                    lo(l, ("prob", b, h, k), pt_lo[:, k % 2, a:z], turn[TURN_AT[("prob", b, h, k)] % 2][:, a:z], pt_hi[:, k % 2, a:z])
                if h % 2:
                    j = h // 2
                    dst, src, part = o_lo[:, j, :], pv[:, :], o_hi[:, j, :]
                    if b == "B":
                        dst, src, part = in_blocks(dst), in_sequence(src), in_blocks(part)
                    lo(l, ("o", b, j), dst, src, part)

            def gate_outputs(l, b):
                for d in range(KD + (b == BR[-1])):
                    if d < KD:
                        m = Y0[b] + d
                        dve.wait_ge(main_done, at(l, N_MAIN, m + 2))
                        dst = merged[:, d, :] if b == BR[0] else yt[:, d % 2, :]
                        if b != BR[0] and d >= 2:
                            dve.wait_ge(merged_done, at(l, 3 * KD, KD * (BR.index(b) - 1) + d - 1))
                        dve.scalar_tensor_tensor(out=dst, in0=gates[:, d, :], scalar=1.0, in1=main[m % 2][:, :],
                                                 op0=ALU.add, op1=ALU.mult).then_inc(y_used, 1)
                        if b != BR[0]:
                            dve.wait_ge(y_used, at(l, 4 * KD, KD * BR.index(b) + d + 1))
                            dve.tensor_tensor(merged[:, d, :], merged[:, d, :], yt[:, d % 2, :], ALU.add).then_inc(merged_done, 1)
                    if b == BR[-1] and d:
                        lo(l, ("merged", d - 1), h_lo[:, d - 1, :], merged[:, d - 1, :], h_hi[:, d - 1, :], 0.5)

            with dve.Fori(0, L) as l:
                a = CONST["params"][0]
                step(l, dve.tensor_copy(params[:, :], const[:, bass.ds(a + l * N_PARAM, N_PARAM)]))
                for part in (v_hi, v_lo):
                    dve.memset(part[:, :, :, HD:2 * HD].rearrange("p a b c -> p (a b) c").bitcast(F32), 0.0).then_inc(v_clear, 1)
                pre_norm(l, "pre_mix")

                dve.wait_ge(copied, at(l, N_COPY, COPY_AT["Dckv1"] + 1))
                step(l, dve.tensor_tensor(d_sq[:, :, :], d_tm[:, :, 0:384], d_tm[:, :, 0:384], ALU.mult))
                step(l, dve.tensor_reduce(r_in[:, 0:NT], d_sq[:, :, 0:QL], AX.X, ALU.add))
                step(l, dve.tensor_reduce(r_in[:, NT:2 * NT], d_sq[:, :, QL:384], AX.X, ALU.add))
                step(l, dve.tensor_scalar(r_in[:, 0:NT], r_in[:, 0:NT], 1.0 / QL, EPS, ALU.mult, ALU.add))
                step(l, dve.tensor_scalar(r_in[:, NT:2 * NT], r_in[:, NT:2 * NT], 1.0 / KVL, EPS, ALU.mult, ALU.add))
                root(l, 2 * NT)
                for i, (lo_c, hi_c) in enumerate(((0, QL), (QL, QL + KVL))):
                    dve.tensor_tensor(d_tm[:, :, lo_c:hi_c], d_tm[:, :, lo_c:hi_c],
                                      view(r_out[:, NT * i:], [[1, NT], [0, hi_c - lo_c]]), ALU.mult).then_inc(latents, 1)
                cos, sin = (c(n).rearrange("p (t c) -> p t c", t=NT) for n in ("cosD", "sinD"))
                k1, k2 = d_tm[:, :, 384:400], d_tm[:, :, 400:416]
                kr = [rope_d[:, i, 0:64].rearrange("p (t c) -> p t c", t=NT) for i in range(4)]
                for i, (a1, a2) in enumerate(((k1, cos), (k2, sin), (k2, cos), (k1, sin))):
                    e = dve.tensor_tensor(kr[i], a1, a2, ALU.mult)
                step(l, e)
                k_out = dk_tm[:, :, :].rearrange("p t (h c) -> p t h c", h=4)
                wide = [view(rope_d[:, i, 0:64], [[16, NT], [0, 4], [1, 16]]) for i in range(4)]
                dve.tensor_tensor(k_out[:, :, :, 64:80], wide[0], wide[1], ALU.subtract)
                dve.tensor_tensor(k_out[:, :, :, 80:96], wide[2], wide[3], ALU.add).then_inc(latents, 1)
                for j in range(3):
                    lo(l, ("latent", j), lat_lo[:, j, :], turn[TURN_AT[("latent", j)] % 2][:, :], lat_hi[:, j, :], param("latent", j))
                dve.wait_ge(copied, at(l, N_COPY, COPY_AT["Dq3"] + 1))
                q = dq_tm[:, :, :].rearrange("p t (h c) -> p t h c", h=4)
                q1, q2 = q[:, :, :, 64:80], q[:, :, :, 80:96]
                wcos, wsin = (view(c(n), [[16, NT], [0, 4], [1, 16]]) for n in ("cosD", "sinD"))
                qr = [rope_d[:, i, :].rearrange("p (t h c) -> p t h c", t=NT, h=4) for i in range(4)]
                for i, (a1, a2) in enumerate(((q1, wcos), (q2, wsin), (q2, wcos), (q1, wsin))):
                    e = dve.tensor_tensor(qr[i], a1, a2, ALU.mult)
                step(l, e)
                dve.tensor_tensor(q1, qr[0], qr[1], ALU.subtract)
                dve.tensor_tensor(q2, qr[2], qr[3], ALU.add).then_inc(latents, 1)
                for t in range(NT):
                    kv = work[WORK_AT[f"Dkv{t}"] % 3][:, :].rearrange("p (h c) -> p h c", h=4)
                    value_parts(l, "D", t, view(kv[:, :, HD:P], [[2 * P, 2], [P, 2], [1, HD]]))
                for h in range(4):
                    lo(l, ("Dq", h), qd_lo[0:DQK, h, :], turn[TURN_AT[("Dq", h)] % 2][0:DQK, :], qd_hi[0:DQK, h, :], DQK ** -0.5)
                    lo(l, ("Dk", h), kd_lo[0:DQK, h, :], turn[TURN_AT[("Dk", h)] % 2][0:DQK, :], kd_hi[0:DQK, h, :])
                for h in range(4):
                    head(l, "D", h)
                gate_outputs(l, "D")

                for name, dst, part, scale in (("Aq", qa_lo, qa_hi, HD ** -0.5), ("Ak", ka_lo, ka_hi, None)):
                    for j in range(2):
                        lo(l, f"{name}{j}", dst[:, j, :], work[WORK_AT[f"{name}{j}"] % 3][:, :], part[:, j, :], scale)
                for j in range(2):
                    for i in range(2):
                        src = work[WORK_AT[f"Av{j}"] % 3][:, 256 * i:256 * i + 256].rearrange("p (a c d) -> p a c d", a=2, c=2)
                        value_parts(l, "A", 2 * j + i, src)
                dve.wait_ge(rpb_in_place, 128 * l + 128)
                for h in range(4):
                    window_bias(l, h)
                    head(l, "A", h)
                gate_outputs(l, "A")

                for j in range(2):
                    scaled_lo(l, f"Bq{j}", in_sequence(qa_lo[:, j, :]), in_blocks(work[WORK_AT[f"Bq{j}"] % 3][:, :]),
                              in_sequence(qa_hi[:, j, :]), HD ** -0.5)
                lo(l, "Bk", in_sequence(ka_lo[:, 0, :]), in_blocks(work[WORK_AT["Bk"] % 3][:, :]), in_sequence(ka_hi[:, 0, :]))
                for t in range(NT):
                    value_parts(l, "B", t, turn[TURN_AT["Bv"] % 2][:, P * t:P * t + P].rearrange("p (c d) -> p c d", d=HD))
                for h in range(4):
                    head(l, "B", h)
                gate_outputs(l, "B")

                dve.wait_ge(copied, at(l, N_COPY, COPY_AT["Ck"] + 1))
                flat = c_tm[:, :, :].rearrange("p t c -> p (t c)")
                by_head = flat.rearrange("p (g d) -> p g d", d=HD)
                n_c = NT * 6
                step(l, dve.tensor_tensor(c_sq[:, :], flat, flat, ALU.mult))
                step(l, dve.tensor_reduce(r_in[:, 0:n_c], c_sq[:, :].rearrange("p (g d) -> p g d", d=HD), AX.X, ALU.add))
                step(l, dve.tensor_scalar(r_in[:, 0:n_c], r_in[:, 0:n_c], 1.0 / HD, EPS, ALU.mult, ALU.add))
                root(l, n_c)
                step(l, dve.tensor_tensor(by_head, by_head, view(r_out, [[1, n_c], [0, HD]]), ALU.mult))
                heads = c_tm[:, :, :].rearrange("p t (g d) -> p t g d", d=HD)
                dve.tensor_tensor(heads[:, :, 0:4, :], heads[:, :, 0:4, :], view(param("cq", 0, HD), [[0, NT], [0, 4], [1, HD]]), ALU.mult)
                step(l, dve.tensor_tensor(heads[:, :, 4:6, :], heads[:, :, 4:6, :],
                                          view(param("ck", 0, HD), [[0, NT], [0, 2], [1, HD]]), ALU.mult))
                for t in range(NT):
                    half = c_tm[:, t, :].rearrange("p (g f c) -> p g f c", f=2, c=32)
                    x1, x2 = half[:, :, :, 0:16], half[:, :, :, 16:32]
                    cos, sin = (view(c(n)[:, 32 * t:], [[0, 6], [16, 2], [1, 16]]) for n in ("cosC", "sinC"))
                    tmp = [c_sq[:, a:a + 192].rearrange("p (g f c) -> p g f c", g=6, f=2) for a in range(768 * (t % 2), 768 * (t % 2) + 768, 192)]
                    for i, (a1, a2) in enumerate(((x1, cos), (x2, sin), (x2, cos), (x1, sin))):
                        e = dve.tensor_tensor(tmp[i], a1, a2, ALU.mult)
                    step(l, e)
                    dve.tensor_tensor(x1, tmp[0], tmp[1], ALU.subtract)
                    e = dve.tensor_tensor(x2, tmp[2], tmp[3], ALU.add)
                    if t == NT - 1:
                        e.then_inc(c_ready, 1)
                for t in range(NT):
                    value_parts(l, "C", t, work[WORK_AT["Cv"] % 3][:, P * t:P * t + P].rearrange("p (c d) -> p c d", d=HD))
                for j in range(3):
                    src = turn[TURN_AT[("C", j)] % 2][:, :]
                    if j < 2:
                        lo(l, ("C", j), qa_lo[:, j, :], src, qa_hi[:, j, :], HD ** -0.5)
                    else:
                        lo(l, ("C", j), ka_lo[:, 0, :], src, ka_hi[:, 0, :])
                for h in range(4):
                    head(l, "C", h)
                gate_outputs(l, "C")

                post_norm(l, "post_mix")
                pre_norm(l, "pre_ffn")
                with dve.Fori(0, KF // 2) as i:
                    for s in range(2):
                        dve.wait_ge(ffn_tanh, l * KF + 2 * i + s + 1)
                        dve.scalar_tensor_tensor(out=ffn_g[:, s, :], in0=ffn_t[:, s, :], scalar=1.0, in1=main[0][:, :],
                                                 op0=ALU.add, op1=ALU.mult).then_inc(ffn_gate, 1)
                        dve.wait_ge(ffn_gate, l * KF + 2 * i + s + 2)
                        dve.wait_ge(main_done, l * N_MAIN + 4 * i + (GUM0 + 2 * s + 3))
                        dve.scalar_tensor_tensor(out=ffn_f[:, s, :], in0=ffn_g[:, s, :], scalar=0.5, in1=main[1][:, :],
                                                 op0=ALU.mult, op1=ALU.mult).then_inc(ffn_full, 1)
                        dve.wait_ge(hi_done, l * N_SPLIT + 2 * i + (ACT0 + s + 1))
                        j = bass.ds(2 * i + s, 1)
                        dve.tensor_tensor(act_lo[:, j, :].rearrange("p a s -> p (a s)"), ffn_f[:, s, :],
                                          act_hi[:, j, :].rearrange("p a s -> p (a s)").bitcast(F32), ALU.subtract).then_inc(lo_done, 1)
                post_norm(l, "post_ffn")
                dve.sem_inc(chain, N_CHAIN - steps[0])


def weight_stream(w_in, w_q, w_kv, w_branch, w_out, w_gu, w_down):
    def piece(w):
        k, n = w.shape
        return w.reshape(k // P, P, n).transpose(1, 0, 2).reshape(P, -1)

    def order(heads):
        return heads.reshape(4, HD, -1)[[0, 2, 1, 3]].reshape(4 * HD, -1)

    stream = np.zeros((L, NP_, P, 2048), np.float32)
    for l in range(L):
        for n, (name, size) in enumerate(PIECES):
            if name == "Dup":
                p = np.concatenate([piece(w_q[l]), w_kv[l]], axis=1)
            elif name.startswith("gate"):
                a = W_IN_AT["gates"] + "ABCD".index(name[4]) * DM + 256 * int(name[5])
                p = piece(w_in[l][:, a:a + 256])
            elif name.startswith("branch"):
                w = w_branch[l]["ABCD".index(name[6])]
                p = piece(order(w) if name[6] in "BC" else w)
            elif name.startswith("out"):
                p = piece(w_out[l][:, 256 * int(name[3:]):256 * int(name[3:]) + 256])
            elif name.startswith("gu"):
                j = P * int(name[2:])
                p = piece(np.concatenate([w_gu[l][:, j:j + P], w_gu[l][:, DFF + j:DFF + j + P]], axis=1))
            elif name.startswith("down"):
                d, h = int(name[4]), int(name[5])
                p = piece(w_down[l][KH * P * h:KH * P * (h + 1), P * d:P * d + P])
            else:
                w = w_in[l][:, W_IN_AT[name]:W_IN_AT[name] + size // KD]
                p = piece(order(w.T).T if name in ("Bq", "Cq") else w)
            assert p.shape == (P, size), (name, p.shape)
            stream[l, n, :, :size] = p
    return stream


def in_blocks_order(a):
    s = a.shape[:-1]
    return a.reshape(*s, ROWS, NT, 16).swapaxes(-3, -2).reshape(*s, S)


def t5_one_hot():
    hot = np.zeros((33, BIAS_X), np.float32)
    rel = np.arange(BIAS_X) - 255
    n = np.abs(rel)
    large = 8 + (np.log(np.maximum(n, 1) / 8) / np.log(128 / 8) * 8).astype(np.int32)
    bucket = (rel > 0).astype(np.int32) * 16 + np.where(n < 8, n, np.minimum(large, 15))
    hot[bucket, np.arange(BIAS_X)] = 1.0
    hot[32, n > 128] = NEG
    return hot


def constants(params):
    out = np.zeros((P, N_CONST), np.float32)

    def put(name, a):
        out[:, CONST[name][0]:CONST[name][1]] = a.reshape(P, -1)

    put("ident", np.eye(P, dtype=np.float32))
    put("ones", np.ones((P, P), np.float32))

    def angles(pos, d):
        inv = 1.0 / (np.float32(ROPE_THETA) ** (np.arange(d // 2, dtype=np.float32) * np.float32(2.0 / d)))
        return pos.astype(np.float32)[:, None] * inv.astype(np.float32)[None, :]

    tok = in_blocks_order(np.arange(S))
    tiled = lambda a: a.reshape(NT, P, -1).transpose(1, 0, 2)
    axial = np.concatenate([angles(tok // GRID_W, 32), angles(tok % GRID_W, 32)], axis=1)
    for n, ang in (("C", axial), ("D", angles(tok, ROPE))):
        put("cos" + n, tiled(np.cos(ang)))
        put("sin" + n, tiled(np.sin(ang)))
    mask = np.zeros((P, 3, 48), np.float32)
    for v, block in enumerate((0, 1, 3)):
        for p in range(P):
            qc = 16 * block + p % 16
            start = min(max(qc - 8, 0), GRID_W - 16)
            kc = 16 * block - 16 + np.arange(48)
            mask[p, v, (kc < start) | (kc >= start + 16)] = NEG
    put("maskA", mask)
    put("params", params)
    return out


def kernel(x, w_in, a_rpb, b_sink, t5_bias, c_q_norm, c_k_norm, d_q_norm, d_kv_norm, d_w_q_up, d_w_kv_up,
           w_branch, w_out, ln_pre_mix, ln_post_mix, ln_pre_ffn, ln_post_ffn, ffn_w_gu, ffn_w_down):
    import concourse.bacc as bacc
    from concourse.bass_utils import run_bass_kernel_spmd

    given = [np.asarray(a) for a in (x, w_in, a_rpb, b_sink, t5_bias, c_q_norm, c_k_norm, d_q_norm, d_kv_norm, d_w_q_up,
                                     d_w_kv_up, w_branch, w_out, ln_pre_mix, ln_post_mix, ln_pre_ffn, ln_post_ffn,
                                     ffn_w_gu, ffn_w_down)]
    (x, w_in, a_rpb, b_sink, t5_bias, c_q_norm, c_k_norm, d_q_norm, d_kv_norm, d_w_q_up, d_w_kv_up,
     w_branch, w_out, ln_pre_mix, ln_post_mix, ln_pre_ffn, ln_post_ffn, ffn_w_gu, ffn_w_down) = given

    swap = [0, 2, 1, 3]
    params = np.zeros((P, L, N_PARAM), np.float32)

    def put(name, l, a):
        params[:, l, PARAMS[name][0]:PARAMS[name][1]] = a

    for l in range(L):
        for name, g in (("pre_mix", ln_pre_mix), ("post_mix", ln_post_mix), ("pre_ffn", ln_pre_ffn), ("post_ffn", ln_post_ffn)):
            put(name, l, g[l].reshape(-1, P).T)
        put("latent", l, np.concatenate([d_q_norm[l].reshape(-1, P), d_kv_norm[l].reshape(-1, P)]).T)
        put("sink", l, b_sink[l][swap][None, :])
        put("cq", l, c_q_norm[l][None, :])
        put("ck", l, c_k_norm[l][None, :])

    rpb = np.zeros((L, N_RPB), np.float32)
    rpb[:, :4 * RPB_HEAD].reshape(L, 4, 15, RPB_ROW)[:, :, :, 16:47] = a_rpb
    t5 = np.ones((33, 4, P), np.float32)
    t5[:32] = t5_bias[:, swap, None]

    arrays = dict(
        stream=weight_stream(w_in, d_w_q_up, d_w_kv_up, w_branch, w_out, ffn_w_gu, ffn_w_down),
        x_in=np.ascontiguousarray(in_blocks_order(x[0].T).reshape(KD, P, S).transpose(1, 0, 2)),
        const_in=constants(params), rpb_in=rpb, t5_in=t5, hot_in=t5_one_hot())
    nc = bacc.Bacc("TRN2", target_bir_lowering=False, num_devices=1)
    args = [nc.dram_tensor(n, a.shape, F32, kind="ExternalInput").ap() for n, a in arrays.items()]
    args.append(nc.dram_tensor("out", (P, KD, S), F32, kind="ExternalOutput").ap())
    program(nc, *args)
    r = run_bass_kernel_spmd(nc, [arrays], core_ids=[0])
    y = np.asarray(r.results[0]["out"])
    y = y.transpose(1, 0, 2).reshape(DM, NT, ROWS, 16).swapaxes(1, 2).reshape(DM, S)
    return np.ascontiguousarray(y.T)[None]
```

```python
from contextlib import ExitStack

import numpy as np

import concourse.bass as bass
from concourse import mybir

ALU = mybir.AluOpType
ACT = mybir.ActivationFunctionType
AX = mybir.AxisListType
F32 = mybir.dt.float32
F32R = mybir.dt.float32r
I32 = mybir.dt.int32

P = 128
DM = 1024
KD = DM // P
S = 512
NT = S // P
L = 2
HD = 64
GRID_W, ROWS = 64, 8
DFF = 2816
KF = DFF // P
EPS = 1e-6
NEG = -1e30
QL, KVL, ROPE, DQK = 256, 128, 32, 96
ROPE_THETA = 10000.0

BR = "DABC"
W_IN_AT = dict(Aq=0, Ak=256, Av=512, Bq=768, Bkv=1024, Cq=1280, Ckv=1536, Dlat=1792, gates=2208)
N_LAT = W_IN_AT["gates"] - W_IN_AT["Dlat"]

PIECES = []
for _b in BR:
    PIECES += dict(D=[("Dlat0", 4 * N_LAT), ("Dlat1", 4 * N_LAT), ("gateD0", 2048), ("Dup", 1280)], A=[("Aq", 2048), ("Ak", 2048), ("Av", 2048)],
                   B=[("Bq", 2048), ("Bkv", 2048)], C=[("Cq", 2048), ("Ckv", 2048)])[_b]
    PIECES += [(f"gate{_b}{j}", 2048) for j in range(_b == "D", 4)] + [(f"branch{_b}", 2048)]
N_FIRST = len(PIECES)
N_OUT, N_GU, N_DOWN = 4, KF, 2 * KD
OUT0 = N_FIRST
GU0 = OUT0 + N_OUT
DOWN0 = GU0 + N_GU
PIECES += [(f"out{j}", 2048) for j in range(N_OUT)] + [(f"gu{j}", 2048) for j in range(N_GU)]
PIECES += [(f"down{d}{h}", 1408) for d in range(KD) for h in range(2)]
NP_ = len(PIECES)
PIECE = {name: n for n, (name, _) in enumerate(PIECES)}
KH = KF // 2

GATE0 = {b: 16 * i for i, b in enumerate(BR)}
Y0 = {b: 16 * i + 8 for i, b in enumerate(BR)}
WOUT0 = 64
GUM0 = WOUT0 + KD
DOWNM0 = GUM0 + 2 * KF
N_MAIN = DOWNM0 + KD

WORK = []
for _b in BR:
    WORK += dict(D=["Dlat0", "Dlat1", "Dlat2"] + [f"Dq{t}" for t in range(NT)] + [f"Dkv{t}" for t in range(NT)],
                 A=["Aq0", "Aq1", "Ak0", "Ak1", "Av0", "Av1"], B=["Bq0", "Bq1", "Bk", "Bv"],
                 C=["Cq0", "Cq1", "Ck", "Cv"])[_b]
    WORK += [("score", _b, h, t) for h in range(4) for t in range(NT)]
WORK_AT = {n: i for i, n in enumerate(WORK)}
N_WORK = len(WORK)

TURN = [("stat", "pre_mix"), ("spread", "pre_mix")]
for _b in BR:
    TURN += dict(D=[("latent", c) for c in range(3)] + [(x, h) for h in range(4) for x in ("Dq", "Dk")],
                 B=["Bv0", "Bv1"], C=[("C", c) for c in range(3)]).get(_b, [])
    TURN += [("prob", _b, h, k) for h in range(4) for k in range(NT)]
for _n in ("post_mix", "pre_ffn", "post_ffn"):
    TURN += [("stat", _n), ("spread", _n)]
TURN_AT = {n: i for i, n in enumerate(TURN)}
N_TURN = len(TURN)
X_BY_DVE = 3
N_X = X_BY_DVE + KD
NORMS = ["pre_mix", "post_mix", "pre_ffn", "post_ffn"]

SPLIT = [("h", "pre_mix", d) for d in range(KD)]
for _b in BR:
    SPLIT += dict(D=[("latent", c) for c in range(3)] + [("V", "D", t) for t in range(NT)]
                  + [(x, h) for h in range(4) for x in ("Dq", "Dk")],
                  A=["Aq0", "Aq1", "Ak0", "Ak1"] + [("V", "A", t) for t in range(NT)],
                  B=["Bq0", "Bq1", "Bk"] + [("V", "B", t) for t in range(NT)],
                  C=[("V", "C", t) for t in range(NT)] + [("C", c) for c in range(3)])[_b]
    for _h in range(4):
        SPLIT += [("prob", _b, _h, k) for k in range(NT)]
        SPLIT += [("o", _b, _h // 2)] if _h % 2 else []
SPLIT += [("merged", d) for d in range(KD)] + [("h", "pre_ffn", d) for d in range(KD)]
ACT0 = len(SPLIT)
SPLIT += [("act", j) for j in range(KF)]
SPLIT_AT = {n: i for i, n in enumerate(SPLIT)}
N_SPLIT = len(SPLIT)

COPY = [f"Dlat{t}" for t in range(NT)] + [f"Dq{t}" for t in range(NT)] + [f"Dk{t}" for t in range(NT)] + ["Cq0", "Cq1", "Ck"]
COPY_AT = {n: i for i, n in enumerate(COPY)}
N_COPY = len(COPY)

FEATURE = ["Aq0", "Aq1", "Ak0", "Ak1", "Bq0", "Bq1", "Bk", "Bv"]

STEPS = 3 * KD
GATE_BEFORE = dict(D=[24, 48, 48, 72, 73, 75, 76, 78, 79, 81, 82, 84], A=[0], B=[0], C=[72])


def gate_points(b):
    points = list(GATE_BEFORE[b])
    for _ in range(4):
        for n in dict(A=(9, 9, 9, 9, 3, 3, 3, 3), B=(9, 9, 9, 9, 3, 3, 3, 3), D=(3, 3, 3, 6, 3, 3, 2, 4), C=(3, 3, 3, 8, 3, 3, 3, 4))[b]:
            points.append(points[-1] + n)
    assert points[-1] == 8 * STEPS
    return points


GATE_POINTS = {b: gate_points(b) for b in BR}


def gate_point(b, h, n):
    return len(GATE_BEFORE[b]) + 8 * h + n


def gate_tiles(b, point):
    before = GATE_POINTS[b][point - 1] if point else 0
    return range(before // STEPS, GATE_POINTS[b][point] // STEPS)


def banded(b):
    return b in "AB"


def window(b, t):
    return range(max(0, t - 1), min(NT, t + 2)) if banded(b) else range(NT)


PARAMS = {}
_at = 0
for _n, _w in (("pre_mix", 8), ("post_mix", 8), ("pre_ffn", 8), ("post_ffn", 8), ("latent", 3), ("sink", 4), ("cq", 64), ("ck", 64)):
    PARAMS[_n] = (_at, _at + _w)
    _at += _w
N_PARAM = _at
CONST = {}
_at = 0
for _n, _w in (("ident", P), ("mean", 1), ("cosC", NT * 32), ("sinC", NT * 32), ("cosD", NT * 16), ("sinD", NT * 16),
               ("maskA", 3 * 48)):
    CONST[_n] = (_at, _at + _w)
    _at += _w
N_CONST = _at
BIAS_X = 512
RPB_ROW = 64
RPB_HEAD = 15 * RPB_ROW
N_RPB = 4 * RPB_HEAD + RPB_ROW

N_CHAIN = 256


def at(l, per_layer, n):
    return l * per_layer + n


def view(ap, dims):
    return bass.AP(tensor=ap.tensor, offset=ap.offset, ap=[list(ap.ap[0])] + [list(d) for d in dims])


def program(nc, stream, x_in, const_in, params_in, rpb_in, t5_in, hot_in, out):
    stream = stream.rearrange("l n p c -> (l n) p c")
    rpb_line = nc.dram_tensor("rpb_line", (16, N_RPB), F32).ap()
    t5_first = nc.dram_tensor("t5_first", (4, BIAS_X), F32).ap()
    t5_line = nc.dram_tensor("t5_line", (P, 4 * BIAS_X), F32).ap()

    base = (nc.sbuf_base + 31) // 32 * 32

    def sb(name, shape, dt, offset):
        size = 4 * int(np.prod(shape[1:]))
        assert base + offset + size <= nc.sbuf_usable_end, (name, base + offset + size)
        return nc.alloc_sbuf_tensor_at(name, shape, dt, offset=base + offset)

    K = 1024
    x = sb("x", [P, KD, S], F32, 0)
    h_hi = sb("h_hi", [P, KD, S], F32R, 16 * K)
    h_lo = sb("h_lo", [P, KD, S], F32R, 32 * K)
    raw = sb("raw", [P, 2, 2048], F32, 48 * K)
    w_hi = sb("w_hi", [P, 2, 2048], F32R, 64 * K)
    w_lo = sb("w_lo", [P, 2, 2048], F32R, 80 * K)
    Z = 96 * K
    gates = sb("gates", [P, KD, S], F32, Z)
    merged = sb("merged", [P, KD, S], F32, Z + 16 * K)
    o_hi = sb("o_hi", [P, 2, S], F32R, Z + 32 * K)
    o_lo = sb("o_lo", [P, 2, S], F32R, Z + 36 * K)
    prob = sb("prob", [P, NT, S], F32, Z + 40 * K)
    pt_hi = sb("pt_hi", [P, 2, S], F32R, Z + 48 * K)
    pt_lo = sb("pt_lo", [P, 2, S], F32R, Z + 52 * K)
    yt = sb("yt", [P, 2, S], F32, Z + 52 * K)
    QT, KT = Z + 56 * K, Z + 72 * K
    qa_hi, qa_lo = (sb(f"qa_{n}", [P, 2, S], F32R, QT + o * K) for n, o in (("hi", 0), ("lo", 4)))
    ka_hi, ka_lo = (sb(f"ka_{n}", [P, 2, S], F32R, KT + o * K) for n, o in (("hi", 0), ("lo", 4)))
    qd_hi, qd_lo = (sb(f"qd_{n}", [P, 4, S], F32R, QT + o * K) for n, o in (("hi", 0), ("lo", 8)))
    kd_hi, kd_lo = (sb(f"kd_{n}", [P, 4, S], F32R, KT + o * K) for n, o in (("hi", 0), ("lo", 8)))
    bias_a = sb("bias_a", [P, 2, 896], F32, QT + 8 * K)
    rpb = sb("rpb", [P, 4, 512], F32, KT + 8 * K)
    d_tm = sb("d_tm", [P, NT, 416], F32, QT)
    d_sq = sb("d_sq", [P, NT, 384], F32, QT + 6656)
    lat_hi = sb("lat_hi", [P, 3, S], F32R, KT)
    lat_lo = sb("lat_lo", [P, 3, S], F32R, KT + 6 * K)
    dq_tm = sb("dq_tm", [P, NT, 384], F32, Z + 40 * K)
    dk_tm = sb("dk_tm", [P, NT, 384], F32, Z + 46 * K)
    feature = sb("feature", [P, NT, S], F32, Z + 40 * K)
    rope_d = sb("rope_d", [P, 4, 256], F32, Z + 52 * K)
    c_tm = sb("c_tm", [P, NT, 384], F32, Z + 40 * K)
    c_sq = sb("c_sq", [P, NT * 384], F32, Z + 46 * K)
    act_hi = sb("act_hi", [P, KF, S], F32R, Z)
    act_lo = sb("act_lo", [P, KF, S], F32R, Z + 44 * K)
    hot = sb("hot", [33, BIAS_X], F32, QT)
    t5 = sb("t5", [33, 4], F32, QT + 2 * K)
    t5_row = sb("t5_row", [4, BIAS_X], F32, QT + 4 * K)
    V = Z + 88 * K
    v_hi = sb("v_hi", [P, NT, 2, 192], F32R, V)
    v_lo = sb("v_lo", [P, NT, 2, 192], F32R, V + 6 * K)
    ffn_t = sb("ffn_t", [P, 2, S], F32, V)
    ffn_g = sb("ffn_g", [P, 2, S], F32, V + 4 * K)
    r_ffn = sb("r_ffn", [P, S], F32, V + 8 * K)
    bias_b = sb("bias_b", [P, 4, 384], F32, V + 12 * K)
    const = sb("const", [P, N_CONST], F32, V + 18 * K)
    at_params = V + 18 * K + (4 * N_CONST + 31) // 32 * 32
    params = sb("params", [P, N_PARAM], F32, at_params)
    tiny = sb("tiny", [P, 76], F32, at_params + (4 * N_PARAM + 31) // 32 * 32)
    r_all = sb("r_all", [P, S], F32, at_params + (4 * N_PARAM + 31) // 32 * 32 + 320)

    def scratch(name, offset):
        return dict(sq=sb(f"sq_{name}", [P, 2, S], F32, offset), sum=sb(f"sum_{name}", [P, S], F32, offset + 4 * K))

    norm_z, norm_h = scratch("z", Z + 16 * K), scratch("h", 32 * K)
    norm_f = dict(sq=sb("sq_f", [P, KD, S], F32, Z + 40 * K), sum=sb("sum_f", [P, S], F32, Z + 56 * K))
    scratch_of = dict(pre_mix=norm_z, post_mix=norm_z, pre_ffn=norm_f, post_ffn=norm_h)
    kept_h = sb("kept_h", [P, KD, S], F32, 16 * K)
    kept_of = dict(post_mix=gates, post_ffn=kept_h)

    def c(name):
        return const[:, CONST[name][0]:CONST[name][1]]

    def param(name, j=0, n=1):
        a = PARAMS[name][0] + j
        return params[:, a:a + n]

    ident, mean = c("ident"), c("mean")
    negmax, sums, recip, esink, maxima = (tiny[:, 4 * i:4 * i + 4] for i in range(5))
    r_in, r_out, r_tmp = tiny[:, 0:24], tiny[:, 24:48], tiny[:, 48:72]
    r_token = tiny[:, 72:76]

    def in_sequence(ap):
        return ap.rearrange("p (r b c) -> p b r c", r=ROWS, b=NT)

    def in_blocks(ap):
        return ap.rearrange("p (b r c) -> p b r c", r=ROWS, b=NT)


    with ExitStack() as ctx:
        def psum(name):
            return ctx.enter_context(nc.psum_tensor(name, [P, 512], F32))

        def sem(name):
            return ctx.enter_context(nc.semaphore(name))

        main = [psum(f"main{i}") for i in range(2)]
        work = [psum(f"work{i}") for i in range(3)]
        turn = [psum(f"turn{i}") for i in range(2)]
        pv = psum("pv")
        ffn_bank = [main, work[:2]]

        t5_loaded = sem("t5_loaded")
        loaded = sem("loaded")
        x_loaded = [sem(f"x_loaded{i}") for i in range(KD // 2)]
        piece_in = [sem(f"piece_in{i}") for i in range(2)]
        piece_hi = sem("piece_hi")
        piece_split = sem("piece_split")
        main_done = sem("main_done")
        down_half = sem("down_half")
        work_done = sem("work_done")
        turn_done = sem("turn_done")
        pv_done = sem("pv_done")
        hi_done = sem("hi_done")
        lo_done = sem("lo_done")
        copied = sem("copied")
        max_done = sem("max_done")
        exp_done = sem("exp_done")
        prob_done = sem("prob_done")
        bias_done = sem("bias_done")
        tanh_done = sem("tanh_done")
        y_used = sem("y_used")
        merged_done = sem("merged_done")
        squared = sem("squared")
        kept_done = sem("kept_done")
        recip_done = sem("recip_done")
        params_in_place = sem("params_in_place")
        lat_half = sem("lat_half")
        sq_added = sem("sq_added")
        token_ready = sem("token_ready")
        mix_factor = sem("mix_factor")
        feature_done = sem("feature_done")
        gate_scaled = sem("gate_scaled")
        summed = sem("summed")
        factor_done = sem("factor_done")
        scaled = sem("scaled")
        x_dve = sem("x_dve")
        x_pool = sem("x_pool")
        ffn_tanh = sem("ffn_tanh")
        ffn_scaled = sem("ffn_scaled")
        ffn_gate = sem("ffn_gate")
        ffn_up = sem("ffn_up")
        ffn_full = sem("ffn_full")
        latents = sem("latents")
        c_ready = sem("c_ready")
        v_clear = sem("v_clear")
        chain = sem("chain")
        t5_sem = sem("t5_sem")
        t5_mm = sem("t5_mm")
        t5_copied = sem("t5_copied")
        t5_ready = sem("t5_ready")
        rpb_sem = sem("rpb_sem")
        rpb_in_place = sem("rpb_in_place")
        waited = sem("waited")
        stored = sem("stored")

        def value_place(part, b, t):
            place = part[:, t, :, :].rearrange("p a (c d) -> p a c d", d=HD)[:, :, 0:3:2, :]
            return place if b in "AD" else place[:, 0]

        block = ctx.enter_context(nc.Block())

        @block.sync
        def _(sp):
            sp.dma_start(hot[:, :], hot_in).then_inc(t5_loaded, 16)
            sp.dma_start(t5[:, :], t5_in).then_inc(t5_loaded, 16)

            def load(l, n, slot, size):
                sp.wait_ge(piece_split, l * NP_ + n + 1)
                src = stream[bass.ds(l * NP_ + n, 1), :, 0:size].rearrange("a p c -> (a p) c")
                sp.dma_start(raw[:, slot, 0:size], src).then_inc(piece_in[slot], 16)

            sp.dma_start(const[:, :], const_in).then_inc(loaded, 16)
            with sp.Fori(0, L) as l:
                for n in range(4):
                    load(l, n, n % 2, PIECES[n][1])
                with sp.Fori(2, DOWN0 // 2) as i:
                    for s in range(2):
                        load(l, 2 * i + s, s, 2048)
                with sp.Fori(DOWN0 // 2, NP_ // 2) as i:
                    for s in range(2):
                        load(l, 2 * i + s, s, KH * P)
            for d in range(0, KD, 2):
                sp.wait_ge(x_dve, L * N_X + d + 2)
                sp.dma_start(out[:, d:d + 2, :], x[:, d:d + 2, :]).then_inc(stored, 16)
            sp.wait_ge(stored, 16 * KD // 2)

        @block.gpsimd
        def _(pool):
            pool.sem_inc(piece_split, 2)

            def split(l, n, slot, size, freed):
                pool.wait_ge(piece_in[slot], l * (8 * NP_) + (n // 2 if isinstance(n, int) else n[1]) * 16 + 16)
                pool.wait_ge(*freed)
                pool.sem_inc(waited, 1)
                pool.tensor_scalar(w_hi[:, slot, 0:size], raw[:, slot, 0:size], 1.0, 0.0, ALU.mult, ALU.add).then_inc(piece_hi, 1)
                m = n if isinstance(n, int) else n[0]
                pool.wait_ge(piece_hi, l * NP_ + m + 1)
                pool.tensor_tensor(w_lo[:, slot, 0:size], raw[:, slot, 0:size], w_hi[:, slot, 0:size].bitcast(F32),
                                   ALU.subtract).then_inc(piece_split, 1)

            ends = dict(Dup=(work_done, "Dkv3"),
                        Aq=(work_done, "Aq1"), Ak=(work_done, "Ak1"), Av=(work_done, "Av1"), Bq=(work_done, "Bq1"),
                        Bkv=(work_done, "Bv"), Cq=(work_done, "Cq1"), Ckv=(work_done, "Cv"))

            def free_after(l, n):
                name = PIECES[n][0]
                if name == "Dlat0":
                    return lat_half, at(l, 1, 1)
                if name == "Dlat1":
                    return pv_done, at(l, 9, 1)
                if name in ends:
                    return work_done, at(l, N_WORK, WORK_AT[ends[name][1]] + 1)
                if name.startswith("out"):
                    return main_done, at(l, N_MAIN, WOUT0 + 2 * int(name[3:]) + 2 + 1)
                if name.startswith("gate"):
                    return main_done, at(l, N_MAIN, GATE0[name[4]] + 2 * int(name[5]) + 2 + 1)
                return main_done, at(l, N_MAIN, Y0[name[6]] + KD + 1)

            with pool.Fori(0, L) as l:
                split(l, 0, 0, PIECES[0][1], (main_done, at(l, N_MAIN, 1)))
                sq, total = norm_z["sq"], norm_z["sum"][:, :]
                for d in range(1, KD):
                    if d > 1:
                        pool.wait_ge(sq_added, at(l, KD - 1, d - 1))
                    pool.wait_ge(squared, at(l, 4 * KD, d + 1))
                    pool.tensor_tensor(total, sq[:, 0, :] if d == 1 else total, sq[:, d % 2, :], ALU.add).then_inc(sq_added, 1)
                for n in range(1, GU0 + 2):
                    split(l, n, n % 2, PIECES[n][1], free_after(l, n - 2) if n >= 2 else (main_done, at(l, N_MAIN, 1)))
                for d in range(X_BY_DVE, KD):
                    pool.wait_ge(scaled, at(l, 2 * KD, d + 1))
                    pool.tensor_tensor(x[:, d, :], x[:, d, :], gates[:, d, :], ALU.add).then_inc(x_pool, 1)
                with pool.Fori(GU0 // 2 + 1, DOWN0 // 2) as i:
                    for s in range(2):
                        split(l, (2 * i + s, i), s, 2048, (main_done, at(l, N_MAIN, (2 * i + s - OUT0) * 2 + WOUT0 - 2 + 1)))
                for n in (DOWN0, DOWN0 + 1):
                    split(l, n, n % 2, KH * P, (main_done, at(l, N_MAIN, (n - OUT0) * 2 + WOUT0 - 2 + 1)))
                with pool.Fori(DOWN0 // 2 + 1, NP_ // 2) as i:
                    split(l, (2 * i, i), 0, KH * P, (down_half, l * KD + i - DOWN0 // 2))
                    split(l, (2 * i + 1, i), 1, KH * P, (main_done, at(l, N_MAIN, DOWNM0 + i - DOWN0 // 2 + 1)))

        @block.tensor
        def _(pe):
            pe.sem_inc(main_done, 1)
            pe.wait_ge(t5_loaded, 32)
            pe.matmul(work[0][0:4, :], t5[:, :], hot[:, :], start=True, stop=True).then_inc(t5_mm, 1)
            pe.wait_ge(t5_copied, 1)
            pe.wait_ge(loaded, 16)

            def three(dst, a_hi, a_lo, b_hi, b_lo, first, last, **kw):
                pe.matmul(dst, a_hi, b_hi, start=first, stop=False, **kw)
                pe.matmul(dst, a_hi, b_lo, start=False, stop=False, **kw)
                return pe.matmul(dst, a_lo, b_hi, start=False, stop=last, **kw)

            def wait_piece(l, n):
                pe.wait_ge(piece_split, at(l, NP_, n + 3))

            def wait_split(l, name):
                pe.wait_ge(lo_done, at(l, N_SPLIT, SPLIT_AT[name] + 1))

            def wait_main(l, m):
                p = m - 2
                if p < 0:
                    return
                b, j = p // 16, p % 16
                if j < KD:
                    pe.wait_ge(gate_scaled, at(l, 4 * KD, KD * b + j + 1))
                else:
                    pe.wait_ge(y_used, at(l, 4 * KD, KD * b + j - KD + 1))

            def wait_work(l, w):
                p = w - 3
                if p < 0:
                    return
                n = WORK[p]
                if n[0] == "score":
                    q = 16 * BR.index(n[1]) + 4 * n[2] + n[3]
                    pe.wait_ge(max_done if banded(n[1]) else exp_done, at(l, 64, q + 1))
                elif n in FEATURE:
                    pe.wait_ge(feature_done, at(l, len(FEATURE), FEATURE.index(n) + 1))
                elif n in COPY:
                    pe.wait_ge(copied, at(l, N_COPY, COPY_AT[n] + 1))
                elif n[:3] == "Dkv":
                    wait_split(l, ("V", "D", int(n[3])))
                elif n[:2] == "Av":
                    wait_split(l, ("V", "A", 2 * int(n[2]) + 1))
                elif n == "Cv":
                    wait_split(l, ("V", "C", NT - 1))
                else:
                    wait_split(l, n)

            def wait_turn(l, t):
                p = t - 2
                if p < 0:
                    return
                n = TURN[p]
                if n[0] == "stat":
                    pe.wait_ge(factor_done, at(l, 4, NORMS.index(n[1]) + 1))
                elif n[1] == "pre_ffn":
                    pe.wait_ge(ffn_up, at(l, KF, KF + 2))
                elif n == ("spread", "pre_mix"):
                    pe.wait_ge(mix_factor, at(l, 1, 1))
                elif n[0] == "spread":
                    pe.wait_ge(scaled, at(l, 2 * KD, KD))
                elif n in ("Bv0", "Bv1"):
                    wait_split(l, ("V", "B", 2 * int(n[2]) + 1))
                else:
                    wait_split(l, n)

            def mean_square(l, name):
                sc, t = scratch_of[name], TURN_AT[("stat", name)]
                wait_turn(l, t)

                def tile(sq, first, last):
                    for tt in range(NT):
                        mm = pe.matmul(turn[t % 2][:, tt:tt + 1], sq[:, P * tt:P * tt + P], mean,
                                       start=first and tt == 0, stop=last, skip_group_check=True)
                    return mm

                if name == "pre_mix":
                    pe.wait_ge(sq_added, at(l, KD - 1, KD - 1))
                    tile(sc["sum"][:, :], True, True).then_inc(turn_done, 1)
                elif name == "pre_ffn":
                    pe.wait_ge(summed, at(l, 3 * KD - 2, 2 * KD - 1))
                    tile(sc["sum"][:, :], True, True).then_inc(turn_done, 1)
                else:
                    pe.wait_ge(summed, at(l, 3 * KD - 2, KD - 1 if name == "post_mix" else 3 * KD - 2))
                    tile(sc["sum"][:, :], True, False)
                    pe.wait_ge(squared, at(l, 4 * KD, KD * (NORMS.index(name) + 1)))
                    tile(sc["sq"][:, 1, :], False, True).then_inc(turn_done, 1)

            def spread(l, name):
                t = TURN_AT[("spread", name)]
                wait_turn(l, t)
                pe.wait_ge(factor_done, at(l, 4, NORMS.index(name) + 1))
                for tt in range(NT):
                    mm = pe.matmul(turn[t % 2][:, P * tt:P * tt + P], view(r_out[:, tt:], [[0, P]]), ident, start=True, stop=True)
                mm.then_inc(turn_done, 1)

            def gate_steps(l, b, point):
                before = GATE_POINTS[b][point - 1] if point else 0
                for s in range(before, GATE_POINTS[b][point]):
                    j, k, which = s // STEPS, s % STEPS // 3, s % 3
                    m = GATE0[b] + j
                    if s % STEPS == 0:
                        wait_main(l, m)
                        if j % 2 == 0:
                            wait_piece(l, PIECE[f"gate{b}{j // 2}"])
                    slot = PIECE[f"gate{b}{j // 2}"] % 2
                    col = 256 * k + P * (j % 2)
                    w = (w_lo if which == 2 else w_hi)[:, slot, col:col + P]
                    mm = pe.matmul(main[m % 2][:, :], w, (h_lo if which == 1 else h_hi)[:, k, :],
                                   start=(s % STEPS == 0), stop=(s % STEPS == STEPS - 1))
                    if s % STEPS == STEPS - 1:
                        mm.then_inc(main_done, 1)

            def by_feature(l, name, n, col, width):
                w = WORK_AT[name]
                wait_work(l, w)
                for k in range(KD):
                    a = width * k + col
                    mm = three(work[w % 3][:, :], w_hi[:, n % 2, a:a + P], w_lo[:, n % 2, a:a + P],
                               h_hi[:, k, :], h_lo[:, k, :], k == 0, k == KD - 1)
                mm.then_inc(work_done, 1)

            def by_token(l, name, n, tiles, col, cols, width):
                w = WORK_AT[name]
                wait_work(l, w)
                for i, t in enumerate(tiles):
                    dst = work[w % 3][:, i * cols:(i + 1) * cols]
                    for k in range(KD):
                        a = width * k + col
                        mm = three(dst, h_hi[:, k, P * t:P * t + P], h_lo[:, k, P * t:P * t + P],
                                   w_hi[:, n % 2, a:a + cols], w_lo[:, n % 2, a:a + cols], k == 0, k == KD - 1)
                mm.then_inc(work_done, 1)

            def turn_tiles(l, name, sources, rows=P):
                t = TURN_AT[name]
                wait_turn(l, t)
                for i, src in enumerate(sources):
                    mm = pe.transpose(turn[t % 2][0:rows, P * i:P * i + P], src, ident)
                mm.then_inc(turn_done, 1)

            def queries(b, h):
                if b == "D":
                    return qd_hi[0:DQK, h, :], qd_lo[0:DQK, h, :]
                a = HD * (h % 2)
                return qa_hi[a:a + HD, h // 2, :], qa_lo[a:a + HD, h // 2, :]

            def keys(b, h):
                if b == "D":
                    return kd_hi[0:DQK, h, :], kd_lo[0:DQK, h, :]
                a, j = HD * (h % 2), h // 2 if b == "A" else 0
                return ka_hi[a:a + HD, j, :], ka_lo[a:a + HD, j, :]

            def head(l, b, h):
                (q_h, q_l), (k_h, k_l) = queries(b, h), keys(b, h)
                for t in range(NT):
                    w = WORK_AT[("score", b, h, t)]
                    ks = window(b, t)
                    a, n = P * ks[0], P * len(ks)
                    wait_work(l, w)
                    three(work[w % 3][:, 0:n], q_h[:, P * t:P * t + P], q_l[:, P * t:P * t + P],
                          k_h[:, a:a + n], k_l[:, a:a + n], True, True).then_inc(work_done, 1)
                    gate_steps(l, b, gate_point(b, h, t))

                def turn_prob(k):
                    t = TURN_AT[("prob", b, h, k)]
                    wait_turn(l, t)
                    qs = [q for q in range(NT) if k in window(b, q)]
                    pe.wait_ge(prob_done, at(l, 64, 16 * BR.index(b) + 4 * h + qs[-1] + 1))
                    for q in qs:
                        a = P * (k - window(b, q)[0])
                        mm = pe.transpose(turn[t % 2][:, P * q:P * q + P], prob[:, q, a:a + P], ident)
                    mm.then_inc(turn_done, 1)

                def values(k):
                    qs = [q for q in range(NT) if k in window(b, q)]
                    a, z = P * qs[0], P * (qs[-1] + 1)
                    wait_split(l, ("prob", b, h, k))
                    v = slice(HD * (h % 2), HD * (h % 2) + P)
                    j = 0 if b in "BC" else h // 2
                    mm = three(pv[:, a:z], v_hi[:, k, j, v], v_lo[:, k, j, v], pt_hi[:, k % 2, a:z],
                               pt_lo[:, k % 2, a:z], h % 2 == 0 and k == 0, h % 2 == 1 and k == NT - 1, skip_group_check=True)
                    if h % 2 == 1 and k == NT - 1:
                        mm.then_inc(pv_done, 1)

                turn_prob(0)
                gate_steps(l, b, gate_point(b, h, 4))
                turn_prob(1)
                gate_steps(l, b, gate_point(b, h, 5))
                if h == 2:
                    wait_split(l, ("o", b, 0))
                values(0)
                turn_prob(2)
                gate_steps(l, b, gate_point(b, h, 6))
                values(1)
                turn_prob(3)
                gate_steps(l, b, gate_point(b, h, 7))
                values(2)
                values(3)

            def branch_out(l, b):
                n = PIECE[f"branch{b}"]
                wait_piece(l, n)
                for d in range(KD):
                    m = Y0[b] + d
                    wait_main(l, m)
                    for k in range(2):
                        if d == 0:
                            wait_split(l, ("o", b, k))
                        a = DM * k + P * d
                        mm = three(main[m % 2][:, :], w_hi[:, n % 2, a:a + P], w_lo[:, n % 2, a:a + P],
                                   o_hi[:, k, :], o_lo[:, k, :], k == 0, k == 1)
                    mm.then_inc(main_done, 1)

            with pe.Fori(0, L) as l:
                for t in range(3):
                    wait_work(l, WORK_AT[f"Dlat{t}"])
                for k in range(KD):
                    if k % 4 == 0:
                        wait_piece(l, PIECE[f"Dlat{k // 4}"])
                    wait_split(l, ("h", "pre_mix", k))
                    a, slot = N_LAT * (k % 4), k // 4
                    for t in range(NT):
                        mm = three((work[t] if t < 3 else pv)[:, 0:N_LAT],
                                   h_hi[:, k, P * t:P * t + P], h_lo[:, k, P * t:P * t + P],
                                   w_hi[:, slot, a:a + N_LAT], w_lo[:, slot, a:a + N_LAT], k == 0, k == KD - 1)
                        if k == KD - 1:
                            mm.then_inc(work_done if t < 3 else pv_done, 1)
                    if k == 3:
                        mm.then_inc(lat_half, 1)
                mean_square(l, "pre_mix")
                gate_steps(l, "D", 0)
                spread(l, "pre_mix")
                gate_steps(l, "D", 1)
                for j in range(3):
                    pe.wait_ge(latents, at(l, 4, 1 if j < 2 else 2))
                    turn_tiles(l, ("latent", j), [d_tm[:, t, P * j:P * j + P] for t in range(NT)])
                gate_steps(l, "D", 2)
                n = PIECE["Dup"]
                wait_piece(l, n)
                for t in range(NT):
                    w = WORK_AT[f"Dq{t}"]
                    wait_work(l, w)
                    for j in range(2):
                        if t == 0:
                            wait_split(l, ("latent", j))
                        mm = three(work[w % 3][:, 0:384], lat_hi[:, j, P * t:P * t + P], lat_lo[:, j, P * t:P * t + P],
                                   w_hi[:, n % 2, 384 * j:384 * j + 384], w_lo[:, n % 2, 384 * j:384 * j + 384], j == 0, j == 1)
                    mm.then_inc(work_done, 1)
                wait_split(l, ("latent", 2))
                for t in range(NT):
                    w = WORK_AT[f"Dkv{t}"]
                    wait_work(l, w)
                    three(work[w % 3][:, :], lat_hi[:, 2, P * t:P * t + P], lat_lo[:, 2, P * t:P * t + P],
                          w_hi[:, n % 2, 768:1280], w_lo[:, n % 2, 768:1280], True, True).then_inc(work_done, 1)
                gate_steps(l, "D", 3)
                pe.wait_ge(copied, at(l, N_COPY, COPY_AT["Dk3"] + 1))
                for h in range(4):
                    for i, (name, tm, count) in enumerate((("Dq", dq_tm, 4), ("Dk", dk_tm, 3))):
                        pe.wait_ge(latents, at(l, 4, count))
                        turn_tiles(l, (name, h), [tm[:, t, DQK * h:DQK * h + DQK] for t in range(NT)], DQK)
                        gate_steps(l, "D", 4 + 2 * h + i)
                for h in range(4):
                    wait_split(l, ("Dk", h))
                    head(l, "D", h)
                branch_out(l, "D")

                for name in ("Aq", "Ak"):
                    wait_piece(l, PIECE[name])
                    for j in range(2):
                        by_feature(l, f"{name}{j}", PIECE[name], P * j, 256)
                wait_piece(l, PIECE["Av"])
                for j in range(2):
                    by_token(l, f"Av{j}", PIECE["Av"], (2 * j, 2 * j + 1), 0, 256, 256)
                for h in range(4):
                    if h == 0:
                        wait_split(l, ("V", "A", NT - 1))
                    head(l, "A", h)
                branch_out(l, "A")

                wait_piece(l, PIECE["Bq"])
                for j in range(2):
                    by_feature(l, f"Bq{j}", PIECE["Bq"], P * j, 256)
                wait_piece(l, PIECE["Bkv"])
                by_feature(l, "Bk", PIECE["Bkv"], 0, 256)
                by_feature(l, "Bv", PIECE["Bkv"], P, 256)
                pe.wait_ge(feature_done, at(l, len(FEATURE), FEATURE.index("Bv") + 1))
                for j in range(2):
                    turn_tiles(l, f"Bv{j}", [feature[:, 3, P * t:P * t + P] for t in (2 * j, 2 * j + 1)])
                for h in range(4):
                    if h == 0:
                        wait_split(l, ("V", "B", NT - 1))
                    head(l, "B", h)
                branch_out(l, "B")

                wait_piece(l, PIECE["Cq"])
                by_token(l, "Cq0", PIECE["Cq"], (0, 1), 0, 256, 256)
                by_token(l, "Cq1", PIECE["Cq"], (2, 3), 0, 256, 256)
                wait_piece(l, PIECE["Ckv"])
                by_token(l, "Ck", PIECE["Ckv"], range(NT), 0, P, 256)
                by_token(l, "Cv", PIECE["Ckv"], range(NT), P, P, 256)
                gate_steps(l, "C", 0)
                for j in range(3):
                    pe.wait_ge(c_ready, at(l, 1, 1))
                    turn_tiles(l, ("C", j), [c_tm[:, t, P * j:P * j + P] for t in range(NT)])
                for h in range(4):
                    if h == 0:
                        wait_split(l, ("C", 2))
                    head(l, "C", h)
                branch_out(l, "C")

                with pe.Fori(0, 2) as i:
                    for s in range(2):
                        pe.wait_ge(piece_split, l * NP_ + 2 * i + (OUT0 + s + 3))
                        for j in range(2):
                            m = 2 * s + j
                            if m < 2:
                                pe.wait_ge(y_used, at(l, 4 * KD, 3 * KD + 6 + m + 1))
                            pe.wait_ge(kept_done, l * 2 * KD + 4 * i + m + 1)
                            for k in range(KD):
                                if m == 0:
                                    wait_split(l, ("merged", k))
                                a = 256 * k + P * j
                                mm = three(main[m % 2][:, :], w_hi[:, s, a:a + P], w_lo[:, s, a:a + P],
                                           h_hi[:, k, :], h_lo[:, k, :], k == 0, k == KD - 1)
                            mm.then_inc(main_done, 1)

                mean_square(l, "post_mix")
                spread(l, "post_mix")

                def gate_up(i, s, js, first=False):
                    for j in js:
                        pe.wait_ge(ffn_up if j else ffn_scaled, l * KF + 2 * i + s + 1)
                    for k in range(KD):
                        if first:
                            wait_split(l, ("h", "pre_ffn", k))
                        for j in js:
                            a = 256 * k + P * j
                            mm = three(ffn_bank[s][j][:, :], w_hi[:, s, a:a + P], w_lo[:, s, a:a + P],
                                       h_hi[:, k, :], h_lo[:, k, :], k == 0, k == KD - 1)
                            if k == KD - 1:
                                mm.then_inc(main_done, 1)

                wait_piece(l, GU0)
                gate_up(0, 0, (0, 1), True)
                wait_piece(l, GU0 + 1)
                gate_up(0, 1, (0,))
                mean_square(l, "pre_ffn")
                gate_up(0, 1, (1,))
                spread(l, "pre_ffn")
                with pe.Fori(1, KF // 2) as i:
                    for s in range(2):
                        pe.wait_ge(piece_split, l * NP_ + 2 * i + (GU0 + s + 3))
                        gate_up(i, s, (0,))
                        gate_up(i, s, (1,))

                with pe.Fori(0, KD // 2) as i:
                    for d in range(2):
                        pe.wait_ge(ffn_up if d else ffn_scaled, at(l, KF, KF + 2))
                        pe.wait_ge(kept_done, l * 2 * KD + 2 * i + KD + d + 1)
                        for s in range(2):
                            pe.wait_ge(piece_split, l * NP_ + 4 * i + (DOWN0 + 2 * d + s + 3))
                            for k in range(KH):
                                if d == 0:
                                    wait_split(l, ("act", KH * s + k))
                                kk = KH * s + k
                                mm = three(main[d][:, :], w_hi[:, s, P * k:P * k + P], w_lo[:, s, P * k:P * k + P],
                                           act_hi[:, kk, :], act_lo[:, kk, :], kk == 0, kk == KF - 1)
                            mm.then_inc(main_done if s else down_half, 1)
                mean_square(l, "post_ffn")
                spread(l, "post_ffn")

        @block.scalar
        def _(act):
            splits = iter(SPLIT)

            def hi(l, name, dst, src, scale=1.0):
                assert next(splits) == name
                act.activation(dst, src, ACT.Copy, scale=scale).then_inc(hi_done, 1)

            def wait_turn_done(l, name):
                act.wait_ge(turn_done, at(l, N_TURN, TURN_AT[name] + 1))

            def wait_work_done(l, name):
                act.wait_ge(work_done, at(l, N_WORK, WORK_AT[name] + 1))

            copies = iter(COPY)

            def copy(l, name, dst, src):
                assert next(copies) == name
                act.activation(dst, src, ACT.Copy).then_inc(copied, 1)

            def keep(l, name):
                i, sc, kept = NORMS.index(name), scratch_of[name], kept_of[name]
                m0 = WOUT0 if name == "post_mix" else DOWNM0
                for d in range(KD):
                    act.wait_ge(main_done, at(l, N_MAIN, m0 + d + 2))
                    if d >= 2:
                        act.wait_ge(summed, at(l, 3 * KD - 2, (0 if name == "post_mix" else 2 * KD - 1) + d - 1))
                    act.activation(sc["sq"][:, d % 2, :], main[d % 2][:, :], ACT.Square).then_inc(squared, 1)
                    act.activation(kept[:, d, :], main[d % 2][:, :], ACT.Copy, scale=param(name, d)).then_inc(kept_done, 1)

            def mixer_input(l):
                for d in range(KD):
                    act.wait_ge(x_dve, at(l, N_X, d + 1))
                    hi(l, ("h", "pre_mix", d), h_hi[:, d, :], x[:, d, :], param("pre_mix", d))
                    if d >= 2:
                        act.wait_ge(sq_added, at(l, KD - 1, max(1, d - 2)))
                    act.activation(norm_z["sq"][:, d % 2, :], x[:, d, :], ACT.Square).then_inc(squared, 1)

            def ffn_input(l):
                for d in range(KD):
                    if d < X_BY_DVE:
                        act.wait_ge(x_dve, at(l, N_X, KD + d + 1))
                    else:
                        act.wait_ge(x_pool, at(l, KD - X_BY_DVE, d - X_BY_DVE + 1))
                    hi(l, ("h", "pre_ffn", d), h_hi[:, d, :], x[:, d, :], param("pre_ffn", d))
                    act.activation(norm_f["sq"][:, d, :], x[:, d, :], ACT.Square).then_inc(squared, 1)

            def gate_tanh(l, b, point):
                for j in gate_tiles(b, point):
                    act.wait_ge(gate_scaled, at(l, 4 * KD, KD * BR.index(b) + j + 1))
                    act.activation(gates[:, j, :], gates[:, j, :], ACT.Tanh, scale=0.5).then_inc(tanh_done, 1)

            def value_parts(l, b, t, src, scale=1.0):
                hi(l, ("V", b, t), value_place(v_hi, b, t), src, scale)

            def head(l, b, h):
                q0 = 16 * BR.index(b) + 4 * h
                for t in range(NT):
                    w = WORK_AT[("score", b, h, t)]
                    n = P * len(window(b, t))
                    src = prob[:, t, 0:n] if banded(b) else work[w % 3][:, 0:n]
                    act.wait_ge(max_done, at(l, 64, q0 + t + 1))
                    e = act.activation(prob[:, t, 0:n], src, ACT.Exp, bias=negmax[:, t:t + 1], accum_out=sums[:, t:t + 1])
                    if b == "B":
                        e = act.activation(esink[:, t:t + 1], param("sink", h), ACT.Exp, bias=negmax[:, t:t + 1])
                    e.then_inc(exp_done, 1)
                    gate_tanh(l, b, gate_point(b, h, t))
                for k in range(NT):
                    qs = [q for q in range(NT) if k in window(b, q)]
                    a, z = P * qs[0], P * (qs[-1] + 1)
                    wait_turn_done(l, ("prob", b, h, k))
                    hi(l, ("prob", b, h, k), pt_hi[:, k % 2, a:z], turn[TURN_AT[("prob", b, h, k)] % 2][:, a:z])
                    gate_tanh(l, b, gate_point(b, h, 4 + k))
                if h % 2:
                    act.wait_ge(pv_done, at(l, 9, 1 + 2 * BR.index(b) + h // 2 + 1))
                    dst, src = o_hi[:, h // 2, :], pv[:, :]
                    if b == "B":
                        dst, src = in_blocks(dst), in_sequence(src)
                    hi(l, ("o", b, h // 2), dst, src)

            act.sem_inc(kept_done, 2)
            for d in range(0, KD, 2):
                act.dma_start(x[:, d:d + 2, :], x_in[:, d:d + 2, :]).then_inc(x_loaded[d // 2], 16)
            act.wait_ge(t5_copied, 1)
            act.dma_start(t5_first, t5_row[:, :]).then_inc(t5_sem, 16)
            act.wait_ge(loaded, 16)
            with act.Fori(0, L) as l:
                act.wait_ge(kept_done, at(l, 2 * KD, 2))
                act.dma_start(params[:, :], params_in[bass.ds(l, 1), :, :].rearrange("a p c -> (a p) c")).then_inc(params_in_place, 16)
                line = rpb_in[bass.ds(l, 1), :]
                act.dma_start(rpb_line, bass.AP(tensor=line.tensor, offset=line.offset, ap=[[0, 16], [1, N_RPB]])).then_inc(rpb_sem, 16)
                act.wait_ge(params_in_place, 16 * l + 16)
                mixer_input(l)
                act.wait_ge(t5_sem, 16 * l + 16)
                act.dma_start(t5_line, bass.AP(tensor=t5_first.tensor, offset=0, ap=[[0, P], [1, 4 * BIAS_X]])).then_inc(t5_sem, 16)

                act.wait_ge(token_ready, at(l, 1, 1))
                for t in range(NT):
                    if t < 3:
                        wait_work_done(l, f"Dlat{t}")
                    else:
                        act.wait_ge(pv_done, at(l, 9, 1))
                    bank, r = (work[t] if t < 3 else pv), r_token[:, t:t + 1]
                    act.activation(d_sq[:, t, 0:QL], bank[:, 0:QL], ACT.Square, scale=r, accum_out=r_in[:, t:t + 1])
                    act.activation(d_sq[:, t, QL:384], bank[:, QL:384], ACT.Square, scale=r, accum_out=r_in[:, NT + t:NT + t + 1])
                    assert next(copies) == f"Dlat{t}"
                    act.activation(d_tm[:, t, :], bank[:, 0:N_LAT], ACT.Copy, scale=r).then_inc(copied, 1)
                act.wait_ge(t5_sem, 16 * l + 32)
                act.dma_start(bias_b[:, :, :], bass.AP(tensor=t5_line.tensor, offset=P - 1,
                                                       ap=[[4 * BIAS_X - 1, P], [BIAS_X, 4], [1, 384]])).then_inc(t5_ready, 16)
                gate_tanh(l, "D", 0)
                for j in range(3):
                    wait_turn_done(l, ("latent", j))
                    hi(l, ("latent", j), lat_hi[:, j, :], turn[TURN_AT[("latent", j)] % 2][:, :], param("latent", j))
                gate_tanh(l, "D", 1)
                gate_tanh(l, "D", 2)
                for t in range(NT):
                    wait_work_done(l, f"Dq{t}")
                    copy(l, f"Dq{t}", dq_tm[:, t, :], work[WORK_AT[f"Dq{t}"] % 3][:, 0:384])
                act.wait_ge(v_clear, at(l, 2, 2))
                for t in range(NT):
                    wait_work_done(l, f"Dkv{t}")
                    kv = work[WORK_AT[f"Dkv{t}"] % 3][:, :].rearrange("p (h c) -> p h c", h=4)
                    copy(l, f"Dk{t}", dk_tm[:, t, :].rearrange("p (h c) -> p h c", h=4)[:, :, 0:HD], kv[:, :, 0:HD])
                    value_parts(l, "D", t, view(kv[:, :, HD:P], [[2 * P, 2], [P, 2], [1, HD]]))
                gate_tanh(l, "D", 3)
                for h in range(4):
                    wait_turn_done(l, ("Dq", h))
                    hi(l, ("Dq", h), qd_hi[0:DQK, h, :], turn[TURN_AT[("Dq", h)] % 2][0:DQK, :], DQK ** -0.5)
                    wait_turn_done(l, ("Dk", h))
                    hi(l, ("Dk", h), kd_hi[0:DQK, h, :], turn[TURN_AT[("Dk", h)] % 2][0:DQK, :])
                for h in range(4):
                    head(l, "D", h)

                for name, dst, scale in (("Aq", qa_hi, HD ** -0.5), ("Ak", ka_hi, 1.0)):
                    for j in range(2):
                        n = FEATURE.index(f"{name}{j}")
                        act.wait_ge(feature_done, at(l, len(FEATURE), n + 1))
                        hi(l, f"{name}{j}", dst[:, j, :], feature[:, n, :], scale)
                        if n == 0:
                            act.wait_ge(rpb_sem, 16 * l + 16)
                            for r in range(ROWS):
                                act.dma_start(rpb[16 * r:16 * r + 16, :, :],
                                              bass.AP(tensor=rpb_line.tensor, offset=(7 - r) * RPB_ROW + 15,
                                                      ap=[[N_RPB - 1, 16], [RPB_HEAD, 4], [1, 512]])).then_inc(rpb_in_place, 16)
                for j in range(2):
                    wait_work_done(l, f"Av{j}")
                    for i in range(2):
                        src = work[WORK_AT[f"Av{j}"] % 3][:, 256 * i:256 * i + 256].rearrange("p (a c d) -> p a c d", a=2, c=2)
                        value_parts(l, "A", 2 * j + i, src, r_token[:, 2 * j + i:2 * j + i + 1])
                for h in range(4):
                    head(l, "A", h)

                for j, (name, dst, scale) in enumerate((("Bq0", qa_hi[:, 0, :], HD ** -0.5), ("Bq1", qa_hi[:, 1, :], HD ** -0.5),
                                                        ("Bk", ka_hi[:, 0, :], 1.0))):
                    act.wait_ge(feature_done, at(l, len(FEATURE), FEATURE.index(name) + 1))
                    hi(l, name, dst, feature[:, j, :], scale)
                for t in range(NT):
                    wait_turn_done(l, f"Bv{t // 2}")
                    src = turn[TURN_AT[f"Bv{t // 2}"] % 2][:, P * (t % 2):P * (t % 2) + P]
                    value_parts(l, "B", t, src.rearrange("p (c d) -> p c d", d=HD))
                for h in range(4):
                    head(l, "B", h)

                def copy_tiles(name, tiles, cols, at_col):
                    wait_work_done(l, name)
                    assert next(copies) == name
                    for i, t in enumerate(tiles):
                        e = act.activation(c_tm[:, t, at_col:at_col + cols], work[WORK_AT[name] % 3][:, cols * i:cols * i + cols],
                                           ACT.Copy, scale=r_token[:, t:t + 1])
                    e.then_inc(copied, 1)

                copy_tiles("Cq0", (0, 1), 256, 0)
                copy_tiles("Cq1", (2, 3), 256, 0)
                copy_tiles("Ck", range(NT), P, 256)
                wait_work_done(l, "Cv")
                for t in range(NT):
                    src = work[WORK_AT["Cv"] % 3][:, P * t:P * t + P]
                    value_parts(l, "C", t, src.rearrange("p (c d) -> p c d", d=HD), r_token[:, t:t + 1])
                gate_tanh(l, "C", 0)
                for j in range(3):
                    wait_turn_done(l, ("C", j))
                    src = turn[TURN_AT[("C", j)] % 2][:, :]
                    if j < 2:
                        hi(l, ("C", j), qa_hi[:, j, :], src, HD ** -0.5)
                    else:
                        hi(l, ("C", j), ka_hi[:, 0, :], src)
                for h in range(4):
                    head(l, "C", h)
                for d in range(KD):
                    act.wait_ge(merged_done, at(l, 3 * KD, 2 * KD + d + 1))
                    hi(l, ("merged", d), h_hi[:, d, :], merged[:, d, :], 0.5)

                keep(l, "post_mix")
                ffn_input(l)
                with act.Fori(0, KF // 2) as i:
                    for s in range(2):
                        act.wait_ge(ffn_scaled, l * KF + 2 * i + s + 3)
                        act.activation(ffn_t[:, s, :], ffn_g[:, s, :], ACT.Tanh, scale=0.5).then_inc(ffn_tanh, 1)
                        act.wait_ge(ffn_full, l * KF + 2 * i + s + 1)
                        act.sem_inc(waited, 1)
                        act.activation(act_hi[:, bass.ds(2 * i + s, 1), :].rearrange("p a s -> p (a s)"), ffn_g[:, s, :],
                                       ACT.Copy).then_inc(hi_done, 1)
                keep(l, "post_ffn")

        @block.vector
        def _(dve):
            dve.sem_inc(ffn_scaled, 2)
            dve.sem_inc(ffn_up, 2)
            for d in range(KD):
                dve.wait_ge(x_loaded[d // 2], 16)
                dve.sem_inc(x_dve, 1)
            dve.wait_ge(t5_mm, 1)
            dve.tensor_copy(t5_row[:, :], work[0][0:4, :]).then_inc(t5_copied, 1)
            dve.wait_ge(loaded, 16)
            steps = [0]

            def step(l, ins):
                ins.then_inc(chain, 1)
                steps[0] += 1
                dve.wait_ge(chain, at(l, N_CHAIN, steps[0]))

            splits = iter(SPLIT)

            def lo(l, name, dst, src, part, scale=None, after=None):
                assert next(splits) == name
                dve.wait_ge(hi_done, at(l, N_SPLIT, SPLIT_AT[after or name] + 1))
                if scale is None:
                    dve.tensor_tensor(dst, src, part.bitcast(F32), ALU.subtract).then_inc(lo_done, 1)
                else:
                    dve.scalar_tensor_tensor(out=dst, in0=src, scalar=scale, in1=part.bitcast(F32),
                                             op0=ALU.mult, op1=ALU.subtract).then_inc(lo_done, 1)

            def feature_tile(l, name, in_order=False):
                n = FEATURE.index(name)
                dve.wait_ge(work_done, at(l, N_WORK, WORK_AT[name] + 1))
                dst, src, factors = feature[:, n % 4, :], work[WORK_AT[name] % 3][:, :], r_all[:, :]
                if in_order:
                    dst, src, factors = in_sequence(dst), in_blocks(src), in_blocks(factors)
                dve.tensor_tensor(dst, src, factors, ALU.mult).then_inc(feature_done, 1)

            def gate_scale(l, b, point):
                for j in gate_tiles(b, point):
                    if j == 0 and b != BR[0]:
                        dve.wait_ge(y_used, at(l, 4 * KD, KD * BR.index(b)))
                    m = GATE0[b] + j
                    dve.wait_ge(main_done, at(l, N_MAIN, m + 2))
                    dve.tensor_tensor(gates[:, j, :], main[m % 2][:, :], r_all[:, :], ALU.mult).then_inc(gate_scaled, 1)

            def root(l, n, last=None):
                v, y, t = r_in[:, 0:n], r_out[:, 0:n], r_tmp[:, 0:n]
                step(l, dve.tensor_scalar(y.bitcast(I32), v.bitcast(I32), -0.5, float(0x5F3759DF), ALU.mult, ALU.add))
                for i in range(3):
                    step(l, dve.tensor_tensor(t, y, y, ALU.mult))
                    step(l, dve.scalar_tensor_tensor(out=t, in0=t, scalar=-0.5, in1=v, op0=ALU.mult, op1=ALU.mult))
                    e = dve.scalar_tensor_tensor(out=y, in0=t, scalar=1.5, in1=y, op0=ALU.add, op1=ALU.mult)
                    if i == 2 and last is not None:
                        e.then_inc(last, 1)
                    else:
                        step(l, e)

            def sum_squares(l, name, tiles):
                base = dict(post_mix=0, pre_ffn=KD - 1, post_ffn=2 * KD - 1)[name]
                i, sc = NORMS.index(name), scratch_of[name]
                ring = sc["sq"].shape[1]
                for d in range(tiles):
                    dve.wait_ge(squared, at(l, 4 * KD, KD * i + d + 1))
                    if d == 0:
                        dve.tensor_copy(sc["sum"][:, :], sc["sq"][:, 0, :]).then_inc(summed, 1)
                    else:
                        dve.wait_ge(summed, at(l, 3 * KD - 2, base + d))
                        dve.tensor_tensor(sc["sum"][:, :], sc["sum"][:, :], sc["sq"][:, d % ring, :], ALU.add).then_inc(summed, 1)

            def token_factor(l, name, keep=None):
                t = TURN_AT[("stat", name)]
                dve.wait_ge(turn_done, at(l, N_TURN, t + 1))
                step(l, dve.tensor_scalar(r_in[:, 0:NT], turn[t % 2][:, 0:NT], EPS, None, ALU.add))
                root(l, NT, factor_done)
                if keep is not None:
                    dve.wait_ge(factor_done, at(l, 4, 1))
                    dve.tensor_copy(keep, r_out[:, 0:NT]).then_inc(token_ready, 1)
                dve.wait_ge(turn_done, at(l, N_TURN, t + 2))

            def factor(name):
                return turn[TURN_AT[("spread", name)] % 2][:, :]

            def mixer_input(l):
                for d in range(KD):
                    lo(l, ("h", "pre_mix", d), h_lo[:, d, :], x[:, d, :], h_hi[:, d, :], param("pre_mix", d))
                token_factor(l, "pre_mix", r_token)
                dve.tensor_copy(r_all[:, :], factor("pre_mix")).then_inc(mix_factor, 1)
                dve.wait_ge(mix_factor, at(l, 1, 1))

            def output_factor(l, name):
                sum_squares(l, name, KD - 1)
                dve.wait_ge(kept_done, at(l, 2 * KD, KD * (name == "post_ffn") + KD + 2))
                token_factor(l, name)

            def add_output(l, name, d, add):
                n, kept = KD * (name == "post_ffn") + d + 1, kept_of[name]
                dve.tensor_tensor(kept[:, d, :], kept[:, d, :], factor(name), ALU.mult).then_inc(scaled, 1)
                if add:
                    dve.wait_ge(scaled, at(l, 2 * KD, n))
                    dve.tensor_tensor(x[:, d, :], x[:, d, :], kept[:, d, :], ALU.add).then_inc(x_dve, 1)

            def wait_work_done(l, name):
                dve.wait_ge(work_done, at(l, N_WORK, WORK_AT[name] + 1))

            def value_parts(l, b, t, src, scale=None):
                last = dict(A=t | 1, B=t | 1, D=t).get(b, NT - 1)
                lo(l, ("V", b, t), value_place(v_lo, b, t), src, value_place(v_hi, b, t), scale, after=("V", b, last))

            def window_bias(l, h):
                a, blocks = 0, ((1, 2), (0, 3), (0, 2))
                for v, (b0, nb) in enumerate(blocks):
                    src = view(rpb[:, h, 16 * b0:], [[16, nb], [RPB_ROW, ROWS], [1, 16]])
                    mask = view(c("maskA")[:, 48 * v + 16 * b0:], [[16, nb], [0, ROWS], [1, 16]])
                    dst = bias_a[:, h % 2, a:a + nb * P].rearrange("p (b r c) -> p b r c", r=ROWS, c=16)
                    step(l, dve.tensor_tensor(dst, src, mask, ALU.add))
                    a += nb * P

            def head(l, b, h):
                q0, w0 = 16 * BR.index(b) + 4 * h, WORK_AT[("score", b, h, 0)]

                def maximum(t):
                    n = P * len(window(b, t))
                    scores = work[(w0 + t) % 3][:, 0:n]
                    dve.wait_ge(work_done, at(l, N_WORK, w0 + t + 1))
                    if not banded(b):
                        dve.tensor_reduce(negmax[:, t:t + 1], scores, AX.X, ALU.max, negate=True).then_inc(max_done, 1)
                        return
                    if b == "A":
                        bias = bias_a[:, h % 2, (0, 256, 256, 640)[t]:(0, 256, 256, 640)[t] + n]
                        least = -3.0e38
                    else:
                        bias = bias_b[:, h, (P if t == 0 else 0):(P if t == 0 else 0) + n]
                        least = param("sink", h)
                    dve.sem_inc(waited, 1)
                    dve.tensor_tensor_reduce(prob[:, t, 0:n], scores, bias, 1.0, least, ALU.add, ALU.max,
                                             maxima[:, t:t + 1]).then_inc(bias_done, 1)
                    dve.wait_ge(bias_done, at(l, 32, q0 - 16 + t + 1))
                    dve.tensor_scalar(negmax[:, t:t + 1], maxima[:, t:t + 1], -1.0, None, ALU.mult).then_inc(max_done, 1)

                def normalise(t):
                    n = P * len(window(b, t))
                    dve.wait_ge(exp_done, at(l, 64, q0 + t + 1))
                    if b == "B":
                        step(l, dve.tensor_tensor(sums[:, t:t + 1], sums[:, t:t + 1], esink[:, t:t + 1], ALU.add))
                    dve.reciprocal(recip[:, t:t + 1], sums[:, t:t + 1]).then_inc(recip_done, 1)
                    dve.wait_ge(recip_done, at(l, 64, q0 + t + 1))
                    dve.tensor_scalar(prob[:, t, 0:n], prob[:, t, 0:n], recip[:, t:t + 1], None, ALU.mult).then_inc(prob_done, 1)

                for t in range(NT):
                    maximum(t)
                    if t:
                        normalise(t - 1)
                    if t == NT - 1:
                        normalise(t)
                    gate_scale(l, b, gate_point(b, h, t))
                for k in range(NT):
                    qs = [q for q in range(NT) if k in window(b, q)]
                    a, z = P * qs[0], P * (qs[-1] + 1)
                    lo(l, ("prob", b, h, k), pt_lo[:, k % 2, a:z], turn[TURN_AT[("prob", b, h, k)] % 2][:, a:z], pt_hi[:, k % 2, a:z])
                    gate_scale(l, b, gate_point(b, h, 4 + k))
                if h % 2:
                    j = h // 2
                    dst, src, part = o_lo[:, j, :], pv[:, :], o_hi[:, j, :]
                    if b == "B":
                        dst, src, part = in_blocks(dst), in_sequence(src), in_blocks(part)
                    lo(l, ("o", b, j), dst, src, part)

            def gate_outputs(l, b):
                for d in range(KD + (b == BR[-1])):
                    if d < KD:
                        m = Y0[b] + d
                        dve.wait_ge(main_done, at(l, N_MAIN, m + 2))
                        dve.wait_ge(tanh_done, at(l, 4 * KD, KD * BR.index(b) + d + 1))
                        dst = merged[:, d, :] if b == BR[0] else yt[:, d % 2, :]
                        if b != BR[0] and d >= 2:
                            dve.wait_ge(merged_done, at(l, 3 * KD, KD * (BR.index(b) - 1) + d - 1))
                        dve.scalar_tensor_tensor(out=dst, in0=gates[:, d, :], scalar=1.0, in1=main[m % 2][:, :],
                                                 op0=ALU.add, op1=ALU.mult).then_inc(y_used, 1)
                        if b != BR[0]:
                            dve.wait_ge(y_used, at(l, 4 * KD, KD * BR.index(b) + d + 1))
                            dve.tensor_tensor(merged[:, d, :], merged[:, d, :], yt[:, d % 2, :], ALU.add).then_inc(merged_done, 1)
                    if b == BR[-1] and d:
                        lo(l, ("merged", d - 1), h_lo[:, d - 1, :], merged[:, d - 1, :], h_hi[:, d - 1, :], 0.5)

            with dve.Fori(0, L) as l:
                dve.wait_ge(params_in_place, 16 * l + 16)
                for part in (v_hi, v_lo):
                    dve.memset(part[:, :, :, HD:2 * HD].rearrange("p a b c -> p (a b) c").bitcast(F32), 0.0).then_inc(v_clear, 1)
                mixer_input(l)
                gate_scale(l, "D", 0)

                dve.wait_ge(copied, at(l, N_COPY, COPY_AT["Dlat3"] + 1))
                dve.tensor_scalar(r_in[:, 0:NT], r_in[:, 0:NT], 1.0 / QL, EPS, ALU.mult, ALU.add)
                step(l, dve.tensor_scalar(r_in[:, NT:2 * NT], r_in[:, NT:2 * NT], 1.0 / KVL, EPS, ALU.mult, ALU.add))
                root(l, 2 * NT)
                for i, (lo_c, hi_c) in enumerate(((0, QL), (QL, QL + KVL))):
                    dve.tensor_tensor(d_tm[:, :, lo_c:hi_c], d_tm[:, :, lo_c:hi_c],
                                      view(r_out[:, NT * i:], [[1, NT], [0, hi_c - lo_c]]), ALU.mult).then_inc(latents, 1)
                cos, sin = (c(n).rearrange("p (t c) -> p t c", t=NT) for n in ("cosD", "sinD"))
                k1, k2 = d_tm[:, :, 384:400], d_tm[:, :, 400:416]
                kr = [rope_d[:, i, 0:64].rearrange("p (t c) -> p t c", t=NT) for i in range(4)]
                for i, (a1, a2) in enumerate(((k1, cos), (k2, sin), (k2, cos), (k1, sin))):
                    e = dve.tensor_tensor(kr[i], a1, a2, ALU.mult)
                step(l, e)
                k_out = dk_tm[:, :, :].rearrange("p t (h c) -> p t h c", h=4)
                wide = [view(rope_d[:, i, 0:64], [[16, NT], [0, 4], [1, 16]]) for i in range(4)]
                dve.tensor_tensor(k_out[:, :, :, 64:80], wide[0], wide[1], ALU.subtract)
                dve.tensor_tensor(k_out[:, :, :, 80:96], wide[2], wide[3], ALU.add).then_inc(latents, 1)
                for j in range(3):
                    lo(l, ("latent", j), lat_lo[:, j, :], turn[TURN_AT[("latent", j)] % 2][:, :], lat_hi[:, j, :], param("latent", j))
                gate_scale(l, "D", 1)
                gate_scale(l, "D", 2)
                dve.wait_ge(copied, at(l, N_COPY, COPY_AT["Dq3"] + 1))
                q = dq_tm[:, :, :].rearrange("p t (h c) -> p t h c", h=4)
                q1, q2 = q[:, :, :, 64:80], q[:, :, :, 80:96]
                wcos, wsin = (view(c(n), [[16, NT], [0, 4], [1, 16]]) for n in ("cosD", "sinD"))
                qr = [rope_d[:, i, :].rearrange("p (t h c) -> p t h c", t=NT, h=4) for i in range(4)]
                for i, (a1, a2) in enumerate(((q1, wcos), (q2, wsin), (q2, wcos), (q1, wsin))):
                    e = dve.tensor_tensor(qr[i], a1, a2, ALU.mult)
                step(l, e)
                dve.tensor_tensor(q1, qr[0], qr[1], ALU.subtract)
                dve.tensor_tensor(q2, qr[2], qr[3], ALU.add).then_inc(latents, 1)
                for t in range(NT):
                    kv = work[WORK_AT[f"Dkv{t}"] % 3][:, :].rearrange("p (h c) -> p h c", h=4)
                    value_parts(l, "D", t, view(kv[:, :, HD:P], [[2 * P, 2], [P, 2], [1, HD]]))
                gate_scale(l, "D", 3)
                for h in range(4):
                    lo(l, ("Dq", h), qd_lo[0:DQK, h, :], turn[TURN_AT[("Dq", h)] % 2][0:DQK, :], qd_hi[0:DQK, h, :], DQK ** -0.5)
                    lo(l, ("Dk", h), kd_lo[0:DQK, h, :], turn[TURN_AT[("Dk", h)] % 2][0:DQK, :], kd_hi[0:DQK, h, :])
                for h in range(4):
                    head(l, "D", h)
                gate_outputs(l, "D")

                for n, (dst, part, scale) in enumerate(((qa_lo[:, 0, :], qa_hi[:, 0, :], HD ** -0.5), (qa_lo[:, 1, :], qa_hi[:, 1, :], HD ** -0.5),
                                                        (ka_lo[:, 0, :], ka_hi[:, 0, :], None), (ka_lo[:, 1, :], ka_hi[:, 1, :], None))):
                    feature_tile(l, FEATURE[n])
                    lo(l, FEATURE[n], dst, feature[:, n, :], part, scale)
                for t in range(NT):
                    assert next(splits) == ("V", "A", t)
                    dve.wait_ge(hi_done, at(l, N_SPLIT, SPLIT_AT[("V", "A", t | 1)] + 1))
                    for a in range(2):
                        src = work[WORK_AT[f"Av{t // 2}"] % 3][:, 256 * (t % 2) + P * a:256 * (t % 2) + P * a + P]
                        e = dve.scalar_tensor_tensor(out=value_place(v_lo, "A", t)[:, a], in0=src.rearrange("p (c d) -> p c d", d=HD),
                                                     scalar=r_token[:, t:t + 1], in1=value_place(v_hi, "A", t)[:, a].bitcast(F32),
                                                     op0=ALU.mult, op1=ALU.subtract)
                    e.then_inc(lo_done, 1)
                dve.wait_ge(rpb_in_place, 128 * l + 128)
                for h in range(4):
                    window_bias(l, h)
                    head(l, "A", h)
                gate_outputs(l, "A")

                dve.wait_ge(t5_ready, 16 * l + 16)
                for n, (dst, part, scale) in enumerate(((qa_lo[:, 0, :], qa_hi[:, 0, :], HD ** -0.5), (qa_lo[:, 1, :], qa_hi[:, 1, :], HD ** -0.5),
                                                        (ka_lo[:, 0, :], ka_hi[:, 0, :], None))):
                    feature_tile(l, FEATURE[4 + n], True)
                    lo(l, FEATURE[4 + n], dst, feature[:, n, :], part, scale)
                feature_tile(l, "Bv", True)
                for t in range(NT):
                    value_parts(l, "B", t, turn[TURN_AT[f"Bv{t // 2}"] % 2][:, P * (t % 2):P * (t % 2) + P].rearrange("p (c d) -> p c d", d=HD))
                for h in range(4):
                    head(l, "B", h)
                gate_outputs(l, "B")

                dve.wait_ge(copied, at(l, N_COPY, COPY_AT["Ck"] + 1))
                flat = c_tm[:, :, :].rearrange("p t c -> p (t c)")
                by_head = flat.rearrange("p (g d) -> p g d", d=HD)
                n_c = NT * 6
                step(l, dve.tensor_tensor(c_sq[:, :], flat, flat, ALU.mult))
                step(l, dve.tensor_reduce(r_in[:, 0:n_c], c_sq[:, :].rearrange("p (g d) -> p g d", d=HD), AX.X, ALU.add))
                step(l, dve.tensor_scalar(r_in[:, 0:n_c], r_in[:, 0:n_c], 1.0 / HD, EPS, ALU.mult, ALU.add))
                root(l, n_c)
                step(l, dve.tensor_tensor(by_head, by_head, view(r_out, [[1, n_c], [0, HD]]), ALU.mult))
                heads = c_tm[:, :, :].rearrange("p t (g d) -> p t g d", d=HD)
                dve.tensor_tensor(heads[:, :, 0:4, :], heads[:, :, 0:4, :], view(param("cq", 0, HD), [[0, NT], [0, 4], [1, HD]]), ALU.mult)
                step(l, dve.tensor_tensor(heads[:, :, 4:6, :], heads[:, :, 4:6, :],
                                          view(param("ck", 0, HD), [[0, NT], [0, 2], [1, HD]]), ALU.mult))
                for t in range(NT):
                    half = c_tm[:, t, :].rearrange("p (g f c) -> p g f c", f=2, c=32)
                    x1, x2 = half[:, :, :, 0:16], half[:, :, :, 16:32]
                    cos, sin = (view(c(n)[:, 32 * t:], [[0, 6], [16, 2], [1, 16]]) for n in ("cosC", "sinC"))
                    tmp = [c_sq[:, a:a + 192].rearrange("p (g f c) -> p g f c", g=6, f=2) for a in range(768 * (t % 2), 768 * (t % 2) + 768, 192)]
                    for i, (a1, a2) in enumerate(((x1, cos), (x2, sin), (x2, cos), (x1, sin))):
                        e = dve.tensor_tensor(tmp[i], a1, a2, ALU.mult)
                    step(l, e)
                    dve.tensor_tensor(x1, tmp[0], tmp[1], ALU.subtract)
                    e = dve.tensor_tensor(x2, tmp[2], tmp[3], ALU.add)
                    if t == NT - 1:
                        e.then_inc(c_ready, 1)
                for t in range(NT):
                    value_parts(l, "C", t, work[WORK_AT["Cv"] % 3][:, P * t:P * t + P].rearrange("p (c d) -> p c d", d=HD), r_token[:, t:t + 1])
                gate_scale(l, "C", 0)
                for j in range(3):
                    src = turn[TURN_AT[("C", j)] % 2][:, :]
                    if j < 2:
                        lo(l, ("C", j), qa_lo[:, j, :], src, qa_hi[:, j, :], HD ** -0.5)
                    else:
                        lo(l, ("C", j), ka_lo[:, 0, :], src, ka_hi[:, 0, :])
                for h in range(4):
                    head(l, "C", h)
                gate_outputs(l, "C")

                output_factor(l, "post_mix")
                for d in range(KD + 2):
                    if d < KD:
                        add_output(l, "post_mix", d, d < X_BY_DVE)
                    if d >= 2:
                        lo(l, ("h", "pre_ffn", d - 2), h_lo[:, d - 2, :], x[:, d - 2, :], h_hi[:, d - 2, :], param("pre_ffn", d - 2))
                sum_squares(l, "pre_ffn", KD)
                token_factor(l, "pre_ffn")
                step(l, dve.tensor_copy(r_ffn[:, :], factor("pre_ffn")))
                dve.sem_inc(waited, 1)
                with dve.Fori(0, KF // 2) as i:
                    for s in range(2):
                        n = l * KF + 2 * i + s
                        gate_bank, up_bank = ffn_bank[s]
                        dve.wait_ge(main_done, l * N_MAIN + 4 * i + (GUM0 + 2 * s + 2))
                        dve.wait_ge(lo_done, l * N_SPLIT + 2 * i + (ACT0 + s - 1))
                        dve.tensor_tensor(ffn_g[:, s, :], gate_bank[:, :], r_ffn[:, :], ALU.mult).then_inc(ffn_scaled, 1)
                        dve.wait_ge(ffn_tanh, n + 1)
                        dve.scalar_tensor_tensor(out=ffn_g[:, s, :], in0=ffn_t[:, s, :], scalar=1.0, in1=ffn_g[:, s, :],
                                                 op0=ALU.add, op1=ALU.mult).then_inc(ffn_gate, 1)
                        dve.wait_ge(ffn_gate, n + 1)
                        dve.wait_ge(main_done, l * N_MAIN + 4 * i + (GUM0 + 2 * s + 3))
                        dve.tensor_tensor(ffn_t[:, s, :], up_bank[:, :], r_ffn[:, :], ALU.mult).then_inc(ffn_up, 1)
                        dve.wait_ge(ffn_up, n + 3)
                        dve.scalar_tensor_tensor(out=ffn_g[:, s, :], in0=ffn_g[:, s, :], scalar=0.5, in1=ffn_t[:, s, :],
                                                 op0=ALU.mult, op1=ALU.mult).then_inc(ffn_full, 1)
                        dve.wait_ge(hi_done, l * N_SPLIT + 2 * i + (ACT0 + s + 1))
                        j = bass.ds(2 * i + s, 1)
                        dve.tensor_tensor(act_lo[:, j, :].rearrange("p a s -> p (a s)"), ffn_g[:, s, :],
                                          act_hi[:, j, :].rearrange("p a s -> p (a s)").bitcast(F32), ALU.subtract).then_inc(lo_done, 1)
                output_factor(l, "post_ffn")
                for d in range(KD):
                    add_output(l, "post_ffn", d, True)
                dve.sem_inc(chain, N_CHAIN - steps[0])


def weight_stream(w_in, w_q, w_kv, w_branch, w_out, w_gu, w_down):
    def piece(w):
        k, n = w.shape
        return w.reshape(k // P, P, n).transpose(1, 0, 2).reshape(P, -1)

    def order(heads):
        return heads.reshape(4, HD, -1)[[0, 2, 1, 3]].reshape(4 * HD, -1)

    stream = np.zeros((L, NP_, P, 2048), np.float32)
    for l in range(L):
        for n, (name, size) in enumerate(PIECES):
            if name == "Dup":
                p = np.concatenate([piece(w_q[l]), w_kv[l]], axis=1)
            elif name.startswith("Dlat"):
                a = 4 * P * int(name[4])
                p = piece(w_in[l][a:a + 4 * P, W_IN_AT["Dlat"]:W_IN_AT["gates"]])
            elif name.startswith("gate"):
                a = W_IN_AT["gates"] + "ABCD".index(name[4]) * DM + 256 * int(name[5])
                p = piece(w_in[l][:, a:a + 256])
            elif name.startswith("branch"):
                w = w_branch[l]["ABCD".index(name[6])]
                p = piece(order(w) if name[6] in "BC" else w)
            elif name.startswith("out"):
                p = piece(w_out[l][:, 256 * int(name[3:]):256 * int(name[3:]) + 256])
            elif name.startswith("gu"):
                j = P * int(name[2:])
                p = piece(np.concatenate([w_gu[l][:, j:j + P], w_gu[l][:, DFF + j:DFF + j + P]], axis=1))
            elif name.startswith("down"):
                d, h = int(name[4]), int(name[5])
                p = piece(w_down[l][KH * P * h:KH * P * (h + 1), P * d:P * d + P])
            else:
                w = w_in[l][:, W_IN_AT[name]:W_IN_AT[name] + size // KD]
                p = piece(order(w.T).T if name in ("Bq", "Cq") else w)
            assert p.shape == (P, size), (name, p.shape)
            stream[l, n, :, :size] = p
    return stream


def in_blocks_order(a):
    s = a.shape[:-1]
    return a.reshape(*s, ROWS, NT, 16).swapaxes(-3, -2).reshape(*s, S)


def t5_one_hot():
    hot = np.zeros((33, BIAS_X), np.float32)
    rel = np.arange(BIAS_X) - 255
    n = np.abs(rel)
    large = 8 + (np.log(np.maximum(n, 1) / 8) / np.log(128 / 8) * 8).astype(np.int32)
    bucket = (rel > 0).astype(np.int32) * 16 + np.where(n < 8, n, np.minimum(large, 15))
    hot[bucket, np.arange(BIAS_X)] = 1.0
    hot[32, n > 128] = NEG
    return hot


def constants():
    out = np.zeros((P, N_CONST), np.float32)

    def put(name, a):
        out[:, CONST[name][0]:CONST[name][1]] = a.reshape(P, -1)

    put("ident", np.eye(P, dtype=np.float32))
    put("mean", np.full((P, 1), 1.0 / DM, np.float32))

    def angles(pos, d):
        inv = 1.0 / (np.float32(ROPE_THETA) ** (np.arange(d // 2, dtype=np.float32) * np.float32(2.0 / d)))
        return pos.astype(np.float32)[:, None] * inv.astype(np.float32)[None, :]

    tok = in_blocks_order(np.arange(S))
    tiled = lambda a: a.reshape(NT, P, -1).transpose(1, 0, 2)
    axial = np.concatenate([angles(tok // GRID_W, 32), angles(tok % GRID_W, 32)], axis=1)
    for n, ang in (("C", axial), ("D", angles(tok, ROPE))):
        put("cos" + n, tiled(np.cos(ang)))
        put("sin" + n, tiled(np.sin(ang)))
    mask = np.zeros((P, 3, 48), np.float32)
    for v, block in enumerate((0, 1, 3)):
        for p in range(P):
            qc = 16 * block + p % 16
            start = min(max(qc - 8, 0), GRID_W - 16)
            kc = 16 * block - 16 + np.arange(48)
            mask[p, v, (kc < start) | (kc >= start + 16)] = NEG
    put("maskA", mask)
    return out


def kernel(x, w_in, a_rpb, b_sink, t5_bias, c_q_norm, c_k_norm, d_q_norm, d_kv_norm, d_w_q_up, d_w_kv_up,
           w_branch, w_out, ln_pre_mix, ln_post_mix, ln_pre_ffn, ln_post_ffn, ffn_w_gu, ffn_w_down):
    import concourse.bacc as bacc
    from concourse.bass_utils import run_bass_kernel_spmd

    given = [np.asarray(a) for a in (x, w_in, a_rpb, b_sink, t5_bias, c_q_norm, c_k_norm, d_q_norm, d_kv_norm, d_w_q_up,
                                     d_w_kv_up, w_branch, w_out, ln_pre_mix, ln_post_mix, ln_pre_ffn, ln_post_ffn,
                                     ffn_w_gu, ffn_w_down)]
    (x, w_in, a_rpb, b_sink, t5_bias, c_q_norm, c_k_norm, d_q_norm, d_kv_norm, d_w_q_up, d_w_kv_up,
     w_branch, w_out, ln_pre_mix, ln_post_mix, ln_pre_ffn, ln_post_ffn, ffn_w_gu, ffn_w_down) = given

    swap = [0, 2, 1, 3]
    params = np.zeros((L, P, N_PARAM), np.float32)

    def put(name, l, a):
        params[l, :, PARAMS[name][0]:PARAMS[name][1]] = a

    for l in range(L):
        for name, g in (("pre_mix", ln_pre_mix), ("post_mix", ln_post_mix), ("pre_ffn", ln_pre_ffn), ("post_ffn", ln_post_ffn)):
            put(name, l, g[l].reshape(-1, P).T)
        put("latent", l, np.concatenate([d_q_norm[l].reshape(-1, P), d_kv_norm[l].reshape(-1, P)]).T)
        put("sink", l, b_sink[l][swap][None, :])
        put("cq", l, c_q_norm[l][None, :])
        put("ck", l, c_k_norm[l][None, :])

    rpb = np.zeros((L, N_RPB), np.float32)
    rpb[:, :4 * RPB_HEAD].reshape(L, 4, 15, RPB_ROW)[:, :, :, 16:47] = a_rpb
    t5 = np.ones((33, 4), np.float32)
    t5[:32] = t5_bias[:, swap]

    arrays = dict(
        stream=weight_stream(w_in, d_w_q_up, d_w_kv_up, w_branch, w_out, ffn_w_gu, ffn_w_down),
        x_in=np.ascontiguousarray(in_blocks_order(x[0].T).reshape(KD, P, S).transpose(1, 0, 2)),
        const_in=constants(), params_in=params, rpb_in=rpb, t5_in=t5, hot_in=t5_one_hot())
    nc = bacc.Bacc("TRN2", target_bir_lowering=False, num_devices=1)
    args = [nc.dram_tensor(n, a.shape, F32, kind="ExternalInput").ap() for n, a in arrays.items()]
    args.append(nc.dram_tensor("out", (P, KD, S), F32, kind="ExternalOutput").ap())
    program(nc, *args)
    r = run_bass_kernel_spmd(nc, [arrays], core_ids=[0])
    y = np.asarray(r.results[0]["out"])
    y = y.transpose(1, 0, 2).reshape(DM, NT, ROWS, 16).swapaxes(1, 2).reshape(DM, S)
    return np.ascontiguousarray(y.T)[None]
```

```python
from contextlib import ExitStack

import numpy as np

import concourse.bass as bass
from concourse import mybir

ALU = mybir.AluOpType
ACT = mybir.ActivationFunctionType
AX = mybir.AxisListType
F32 = mybir.dt.float32
F32R = mybir.dt.float32r
I32 = mybir.dt.int32

P = 128
DM = 1024
KD = DM // P
S = 512
NT = S // P
L = 2
HD = 64
GRID_W, ROWS = 64, 8
DFF = 2816
KF = DFF // P
EPS = 1e-6
NEG = -1e30
QL, KVL, ROPE, DQK = 256, 128, 32, 96
ROPE_THETA = 10000.0

BR = "DABC"
W_IN_AT = dict(Aq=0, Ak=256, Av=512, Bq=768, Bkv=1024, Cq=1280, Ckv=1536, Dlat=1792, gates=2208)
N_LAT = W_IN_AT["gates"] - W_IN_AT["Dlat"]

PIECES = []
for _b in BR:
    PIECES += dict(D=[("Dlat0", 4 * N_LAT), ("Dlat1", 4 * N_LAT), ("gateD0", 2048), ("Dup", 1280), ("gateD1", 2048)],
                   A=[("Aq", 2048), ("Ak", 2048), ("Av", 2048)], B=[("Bq", 2048), ("Bkv", 2048)], C=[("Cq", 2048), ("Ckv", 2048)])[_b]
    PIECES += [(f"gate{_b}{j}", 2048) for j in dict(D=(2, 3), A=(1, 2, 3)).get(_b, range(4))]
    PIECES += [("gateA0", 2048)] * (_b == "D") + [(f"branch{_b}", 2048)]
N_FIRST = len(PIECES)
N_OUT, N_GU, N_DOWN = 4, KF, 2 * KD
OUT0 = N_FIRST
GU0 = OUT0 + N_OUT
DOWN0 = GU0 + N_GU
PIECES += [(f"out{j}", 2048) for j in range(N_OUT)] + [(f"gu{j}", 2048) for j in range(N_GU)]
PIECES += [(f"down{d}{h}", 1408) for d in range(KD) for h in range(2)]
NP_ = len(PIECES)
PIECE = {name: n for n, (name, _) in enumerate(PIECES)}
KH = KF // 2

EARLY = 2
MAIN = []
for _b in BR:
    MAIN += [("gate", _b, j) for j in range(EARLY * (_b == "A"), KD)]
    MAIN += [("gate", "A", j) for j in range(EARLY * (_b == "D"))] + [("y", _b, j) for j in range(KD)]
MAIN_AT = {n: i for i, n in enumerate(MAIN)}
WOUT0 = len(MAIN)
GUM0 = WOUT0 + KD
DOWNM0 = GUM0 + 2 * KF
N_MAIN = DOWNM0 + KD

WORK = []
for _b in BR:
    WORK += dict(D=["Dlat0", "Dlat1", "Dlat2"] + [f"Dq{t}" for t in range(NT)] + [f"Dkv{t}" for t in range(NT)],
                 A=["Aq0", "Aq1", "Ak0", "Ak1", "Av0", "Av1"], B=["Bq0", "Bq1", "Bk", "Bv"],
                 C=["Cq0", "Cq1", "Ckv0", "Ckv1"])[_b]
    WORK += [("score", _b, h, t) for h in range(4) for t in range(NT)]
WORK_AT = {n: i for i, n in enumerate(WORK)}
N_WORK = len(WORK)

TURN = [("stat", "pre_mix"), ("spread", "pre_mix")]
for _b in BR:
    TURN += dict(D=[("latent", c) for c in range(3)] + [(x, h) for h in range(4) for x in ("Dq", "Dk")],
                 B=["Bv0", "Bv1"], C=[("C", c) for c in range(3)]).get(_b, [])
    TURN += [("prob", _b, h, k) for h in range(4) for k in range(NT)]
for _n in ("post_mix", "pre_ffn", "post_ffn"):
    TURN += [("stat", _n), ("spread", _n)]
TURN_AT = {n: i for i, n in enumerate(TURN)}
N_TURN = len(TURN)

MIX_DVE, FFN_DVE = 3, 5
N_X = MIX_DVE + KD
LAG = 2
AHEAD = 3
X0 = KD - FFN_DVE
NORMS = ["pre_mix", "post_mix", "pre_ffn", "post_ffn"]

SPLIT = [("h", "pre_mix", d) for d in range(KD)]
for _b in BR:
    SPLIT += dict(D=[("latent", c) for c in range(3)] + [("V", "D", t) for t in range(NT)]
                  + [(x, h) for h in range(4) for x in ("Dq", "Dk")],
                  A=["Aq0", "Aq1", "Ak0", "Ak1"] + [("V", "A", t) for t in range(NT)],
                  B=["Bq0", "Bq1", "Bk"] + [("V", "B", t) for t in range(NT)],
                  C=[("V", "C", t) for t in range(NT)] + [("C", c) for c in range(3)])[_b]
    for _h in range(4):
        SPLIT += [("prob", _b, _h, k) for k in range(NT)]
        SPLIT += [("o", _b, _h // 2)] if _h % 2 else []
SPLIT += [("merged", d) for d in range(KD)] + [("h", "pre_ffn", d) for d in range(KD)]
ACT0 = len(SPLIT)
SPLIT += [("act", j) for j in range(KF)]
SPLIT_AT = {n: i for i, n in enumerate(SPLIT)}
N_SPLIT = len(SPLIT)

COPY = [f"Dlat{t}" for t in range(NT)] + [f"Dq{t}" for t in range(NT)] + [f"Dk{t}" for t in range(NT)] + ["Cq0", "Cq1", "Ckv0", "Ckv1"]
COPY_AT = {n: i for i, n in enumerate(COPY)}
N_COPY = len(COPY)

FEATURE = ["Aq0", "Aq1", "Ak0", "Ak1", "Bq0", "Bq1", "Bk", "Bv"]

STEPS = 3 * KD
BRANCH_STEPS = KD * STEPS
GATE_BEFORE = dict(D=[24, 48, 48, 78, 80, 83, 85, 88, 90, 93, 95, 98], A=[0], B=[0], C=[44, 48, 52, 56])


def gate_points(b):
    start = BR.index(b) * BRANCH_STEPS + EARLY * STEPS * (b == "A")
    end = (BR.index(b) + 1) * BRANCH_STEPS + EARLY * STEPS * (b == "D")
    heads, last = dict(D=((4, 4, 4, 11, 4, 3, 2, 4, 0), (4, 4, 3, 8, 4, 2, 2, 3, 4)),
                       A=((7, 7, 7, 7, 2, 2, 2, 2, 0), (6, 6, 6, 6, 2, 2, 1, 1, 6)),
                       B=((9, 9, 9, 9, 3, 3, 3, 3, 0), (8, 8, 8, 8, 3, 3, 2, 2, 6)),
                       C=((4, 4, 4, 8, 4, 4, 2, 4, 0), (4, 4, 3, 8, 3, 3, 2, 3, 4)))[b]
    points = [start + n for n in GATE_BEFORE[b]]
    for n in 3 * heads + last:
        points.append(points[-1] + n)
    assert points[-1] == end, (b, points[-1], end)
    return [start] + points


GATE_POINTS = {b: gate_points(b) for b in BR}


def gate_point(b, h, n):
    return len(GATE_BEFORE[b]) + 9 * h + n


def gates_after(b, t):
    return (t,) if banded(b) else range(NT) if t == NT - 1 else ()


def gate_tiles(b, point):
    before, now = GATE_POINTS[b][point:point + 2]
    return [(BR[i // KD], i % KD) for i in range(before // STEPS, now // STEPS)]


def banded(b):
    return b in "AB"


def window(b, t):
    return range(max(0, t - 1), min(NT, t + 2)) if banded(b) else range(NT)


PARAMS = {}
_at = 0
for _n, _w in (("pre_mix", 8), ("post_mix", 8), ("pre_ffn", 8), ("post_ffn", 8), ("latent", 3), ("sink", 4), ("cq", 64), ("ck", 64)):
    PARAMS[_n] = (_at, _at + _w)
    _at += _w
N_PARAM = _at
CONST = {}
_at = 0
for _n, _w in (("ident", P), ("mean", 1), ("cosC", NT * 32), ("sinC", NT * 32), ("cosD", NT * 16), ("sinD", NT * 16),
               ("maskA", 3 * 48)):
    CONST[_n] = (_at, _at + _w)
    _at += _w
N_CONST = _at
BIAS_X = 512
RPB_ROW = 64
RPB_HEAD = 15 * RPB_ROW
N_RPB = 4 * RPB_HEAD + RPB_ROW

N_CHAIN = 256


def at(l, per_layer, n):
    return l * per_layer + n


def view(ap, dims):
    return bass.AP(tensor=ap.tensor, offset=ap.offset, ap=[list(ap.ap[0])] + [list(d) for d in dims])


def program(nc, stream, x_in, const_in, params_in, rpb_in, t5_in, hot_in, out):
    stream = stream.rearrange("l n p c -> (l n) p c")
    rpb_line = nc.dram_tensor("rpb_line", (16, N_RPB), F32).ap()
    t5_first = nc.dram_tensor("t5_first", (4, BIAS_X), F32).ap()
    t5_line = nc.dram_tensor("t5_line", (P, 4 * BIAS_X), F32).ap()

    base = (nc.sbuf_base + 31) // 32 * 32

    def sb(name, shape, dt, offset):
        size = 4 * int(np.prod(shape[1:]))
        assert base + offset + size <= nc.sbuf_usable_end, (name, base + offset + size)
        return nc.alloc_sbuf_tensor_at(name, shape, dt, offset=base + offset)

    K = 1024
    x = sb("x", [P, KD, S], F32, 0)
    h_hi = sb("h_hi", [P, KD, S], F32R, 16 * K)
    h_lo = sb("h_lo", [P, KD, S], F32R, 32 * K)
    raw = sb("raw", [P, 2, 2048], F32, 48 * K)
    w_hi = sb("w_hi", [P, 2, 2048], F32R, 64 * K)
    w_lo = sb("w_lo", [P, 2, 2048], F32R, 80 * K)
    Z = 96 * K
    gates_d = sb("gates_d", [P, KD, S], F32, Z)
    gates = sb("gates", [P, KD, S], F32, Z + 16 * K)
    gates_of, merged = dict(D=gates_d, A=gates, B=gates, C=gates), gates_d
    o_hi = sb("o_hi", [P, 2, S], F32R, Z + 32 * K)
    o_lo = sb("o_lo", [P, 2, S], F32R, Z + 36 * K)
    prob = sb("prob", [P, NT, S], F32, Z + 40 * K)
    pt_hi = sb("pt_hi", [P, 2, S], F32R, Z + 48 * K)
    pt_lo = sb("pt_lo", [P, 2, S], F32R, Z + 52 * K)
    yt = sb("yt", [P, 2, S], F32, Z + 52 * K)
    QT, KT = Z + 56 * K, Z + 72 * K
    qa_hi, qa_lo = (sb(f"qa_{n}", [P, 2, S], F32R, QT + o * K) for n, o in (("hi", 0), ("lo", 4)))
    ka_hi, ka_lo = (sb(f"ka_{n}", [P, 2, S], F32R, KT + o * K) for n, o in (("hi", 0), ("lo", 4)))
    qd_hi, qd_lo = (sb(f"qd_{n}", [P, 4, S], F32R, QT + o * K) for n, o in (("hi", 0), ("lo", 8)))
    kd_hi, kd_lo = (sb(f"kd_{n}", [P, 4, S], F32R, KT + o * K) for n, o in (("hi", 0), ("lo", 8)))
    bias_a = sb("bias_a", [P, 2, 896], F32, QT + 8 * K)
    rpb = sb("rpb", [P, 4, 512], F32, KT + 8 * K)
    d_tm = sb("d_tm", [P, NT, 416], F32, QT)
    d_sq = sb("d_sq", [P, NT, 384], F32, QT + 6656)
    lat_hi = sb("lat_hi", [P, 3, S], F32R, KT)
    lat_lo = sb("lat_lo", [P, 3, S], F32R, KT + 6 * K)
    dq_tm = sb("dq_tm", [P, NT, 384], F32, Z + 40 * K)
    dk_tm = sb("dk_tm", [P, NT, 384], F32, Z + 46 * K)
    feature = sb("feature", [P, NT, S], F32, Z + 40 * K)
    rope_d = sb("rope_d", [P, 4, 256], F32, Z + 52 * K)
    c_tm = sb("c_tm", [P, NT, 384], F32, Z + 40 * K)
    c_sq = sb("c_sq", [P, NT * 384], F32, Z + 46 * K)
    act_hi = sb("act_hi", [P, KF, S], F32R, Z)
    act_lo = sb("act_lo", [P, KF, S], F32R, Z + 44 * K)
    hot = sb("hot", [33, BIAS_X], F32, QT)
    t5 = sb("t5", [33, 4], F32, QT + 2 * K)
    t5_row = sb("t5_row", [4, BIAS_X], F32, QT + 4 * K)
    V = Z + 88 * K
    v_hi = sb("v_hi", [P, NT, 2, 192], F32R, V)
    v_lo = sb("v_lo", [P, NT, 2, 192], F32R, V + 6 * K)
    ffn_t = sb("ffn_t", [P, 2, S], F32, V)
    ffn_g = sb("ffn_g", [P, 2, S], F32, V + 4 * K)
    r_ffn = sb("r_ffn", [P, S], F32, V + 8 * K)
    bias_b = sb("bias_b", [P, 4, 384], F32, V + 12 * K)
    const = sb("const", [P, N_CONST], F32, V + 18 * K)
    at_params = V + 18 * K + (4 * N_CONST + 31) // 32 * 32
    params = sb("params", [P, N_PARAM], F32, at_params)
    tiny = sb("tiny", [P, 76], F32, at_params + (4 * N_PARAM + 31) // 32 * 32)
    r_all = sb("r_all", [P, S], F32, at_params + (4 * N_PARAM + 31) // 32 * 32 + 320)

    def scratch(name, offset):
        return dict(sq=sb(f"sq_{name}", [P, 2, S], F32, offset), sum=sb(f"sum_{name}", [P, S], F32, offset + 4 * K))

    norm_z, norm_h = scratch("z", Z + 16 * K), scratch("h", 32 * K)
    norm_f = dict(sq=sb("sq_f", [P, KD, S], F32, Z + 40 * K), sum=sb("sum_f", [P, S], F32, Z + 56 * K))
    scratch_of = dict(pre_mix=norm_f, post_mix=norm_z, pre_ffn=norm_f, post_ffn=norm_h)
    kept_h = sb("kept_h", [P, KD, S], F32, 16 * K)
    kept_m = sb("kept_m", [P, KD, S], F32, Z)
    kept_of = dict(post_mix=kept_m, post_ffn=kept_h)

    def c(name):
        return const[:, CONST[name][0]:CONST[name][1]]

    def param(name, j=0, n=1):
        a = PARAMS[name][0] + j
        return params[:, a:a + n]

    ident, mean = c("ident"), c("mean")
    negmax, sums, recip, esink, maxima = (tiny[:, 4 * i:4 * i + 4] for i in range(5))
    r_in, r_out, r_tmp = tiny[:, 0:24], tiny[:, 24:48], tiny[:, 48:72]
    r_token = tiny[:, 72:76]

    def in_sequence(ap):
        return ap.rearrange("p (r b c) -> p b r c", r=ROWS, b=NT)

    def in_blocks(ap):
        return ap.rearrange("p (b r c) -> p b r c", r=ROWS, b=NT)


    with ExitStack() as ctx:
        def psum(name):
            return ctx.enter_context(nc.psum_tensor(name, [P, 512], F32))

        def sem(name):
            return ctx.enter_context(nc.semaphore(name))

        main = [psum(f"main{i}") for i in range(2)]
        work = [psum(f"work{i}") for i in range(3)]
        turn = [psum(f"turn{i}") for i in range(2)]
        pv = psum("pv")
        ffn_bank = [main, work[:2]]

        t5_loaded = sem("t5_loaded")
        loaded = sem("loaded")
        x_loaded = [sem(f"x_loaded{i}") for i in range(KD // 2)]
        piece_in = [sem(f"piece_in{i}") for i in range(2)]
        piece_hi = sem("piece_hi")
        piece_split = sem("piece_split")
        main_done = sem("main_done")
        down_half = sem("down_half")
        work_done = sem("work_done")
        turn_done = sem("turn_done")
        pv_done = sem("pv_done")
        hi_done = sem("hi_done")
        lo_done = sem("lo_done")
        copied = sem("copied")
        max_done = sem("max_done")
        exp_done = sem("exp_done")
        prob_done = sem("prob_done")
        bias_done = sem("bias_done")
        tanh_done = sem("tanh_done")
        y_used = sem("y_used")
        merged_done = sem("merged_done")
        squared = sem("squared")
        kept_done = sem("kept_done")
        recip_done = sem("recip_done")
        params_in_place = sem("params_in_place")
        lat_half = sem("lat_half")
        lat_squared = sem("lat_squared")
        token_ready = sem("token_ready")
        mix_factor = sem("mix_factor")
        feature_done = sem("feature_done")
        gate_scaled = sem("gate_scaled")
        summed = sem("summed")
        factor_done = sem("factor_done")
        scaled = sem("scaled")
        x_dve = sem("x_dve")
        x_pool = sem("x_pool")
        ffn_tanh = sem("ffn_tanh")
        ffn_scaled = sem("ffn_scaled")
        ffn_gate = sem("ffn_gate")
        ffn_up = sem("ffn_up")
        ffn_full = sem("ffn_full")
        latents = sem("latents")
        c_ready = sem("c_ready")
        v_clear = sem("v_clear")
        chain = sem("chain")
        t5_sem = sem("t5_sem")
        t5_mm = sem("t5_mm")
        t5_copied = sem("t5_copied")
        t5_ready = sem("t5_ready")
        rpb_sem = sem("rpb_sem")
        rpb_in_place = sem("rpb_in_place")
        waited = sem("waited")
        stored = sem("stored")

        def value_place(part, b, t):
            place = part[:, t, :, :].rearrange("p a (c d) -> p a c d", d=HD)[:, :, 0:3:2, :]
            return place if b in "AD" else place[:, 0]

        block = ctx.enter_context(nc.Block())

        @block.sync
        def _(sp):
            def load(l, n, slot, size):
                sp.wait_ge(piece_split, l * NP_ + n + 1)
                src = stream[bass.ds(l * NP_ + n, 1), :, 0:size].rearrange("a p c -> (a p) c")
                sp.dma_start(raw[:, slot, 0:size], src).then_inc(piece_in[slot], 16)

            with sp.Fori(0, L) as l:
                for n in range(4):
                    load(l, n, n % 2, PIECES[n][1])
                    if n == 0:
                        sp.wait_ge(kept_done, at(l, 2 * KD, 2))
                        sp.dma_start(params[:, :], params_in[bass.ds(l, 1), :, :].rearrange("a p c -> (a p) c")).then_inc(params_in_place, 16)
                with sp.Fori(2, DOWN0 // 2) as i:
                    for s in range(2):
                        load(l, 2 * i + s, s, 2048)
                with sp.Fori(DOWN0 // 2, NP_ // 2) as i:
                    for s in range(2):
                        load(l, 2 * i + s, s, KH * P)
            for d in [*range(FFN_DVE - 1), *range(FFN_DVE, KD), FFN_DVE - 1]:
                if d < FFN_DVE:
                    sp.wait_ge(x_dve, at(L, N_X, X0 + d + 1))
                else:
                    sp.wait_ge(x_pool, at(L, KD, d - FFN_DVE + 1))
                sp.dma_start(out[:, d, :], x[:, d, :]).then_inc(stored, 16)
            sp.wait_ge(stored, 16 * KD)

        @block.gpsimd
        def _(pool):
            pool.sem_inc(piece_split, 2)
            pool.sem_inc(x_pool, X0)

            def split(l, n, slot, size, freed):
                pool.wait_ge(piece_in[slot], l * (8 * NP_) + (n // 2 if isinstance(n, int) else n[1]) * 16 + 16)
                pool.wait_ge(*freed)
                pool.sem_inc(waited, 1)
                pool.tensor_scalar(w_hi[:, slot, 0:size], raw[:, slot, 0:size], 1.0, 0.0, ALU.mult, ALU.add).then_inc(piece_hi, 1)
                m = n if isinstance(n, int) else n[0]
                pool.wait_ge(piece_hi, l * NP_ + m + 1)
                pool.tensor_tensor(w_lo[:, slot, 0:size], raw[:, slot, 0:size], w_hi[:, slot, 0:size].bitcast(F32),
                                   ALU.subtract).then_inc(piece_split, 1)

            ends = dict(Dup=(work_done, "Dkv3"),
                        Aq=(work_done, "Aq1"), Ak=(work_done, "Ak1"), Av=(work_done, "Av1"), Bq=(work_done, "Bq1"),
                        Bkv=(work_done, "Bv"), Cq=(work_done, "Cq1"), Ckv=(work_done, "Ckv1"))

            def free_after(l, n):
                name = PIECES[n][0]
                if name == "Dlat0":
                    return lat_half, at(l, 1, 1)
                if name == "Dlat1":
                    return pv_done, at(l, 9, 1)
                if name in ends:
                    return work_done, at(l, N_WORK, WORK_AT[ends[name][1]] + 1)
                if name.startswith("out"):
                    return main_done, at(l, N_MAIN, WOUT0 + 2 * int(name[3:]) + 2 + 1)
                if name.startswith("gate"):
                    return main_done, at(l, N_MAIN, MAIN_AT[("gate", name[4], 2 * int(name[5]) + 1)] + 2)
                return main_done, at(l, N_MAIN, MAIN_AT[("y", name[6], KD - 1)] + 2)

            with pool.Fori(0, L) as l:
                split(l, 0, 0, PIECES[0][1], (main_done, at(l, N_MAIN, 1)))
                for n in range(1, GU0 + 2):
                    split(l, n, n % 2, PIECES[n][1], free_after(l, n - 2) if n >= 2 else (main_done, at(l, N_MAIN, 1)))
                for d in range(MIX_DVE, KD):
                    pool.wait_ge(scaled, at(l, 2 * KD, d + 1))
                    pool.tensor_tensor(x[:, d, :], x[:, d, :], kept_m[:, d, :], ALU.add).then_inc(x_pool, 1)
                with pool.Fori(GU0 // 2 + 1, DOWN0 // 2) as i:
                    for s in range(2):
                        split(l, (2 * i + s, i), s, 2048, (main_done, at(l, N_MAIN, (2 * i + s - OUT0) * 2 + WOUT0 - 2 + 1)))
                for n in (DOWN0, DOWN0 + 1):
                    split(l, n, n % 2, KH * P, (main_done, at(l, N_MAIN, (n - OUT0) * 2 + WOUT0 - 2 + 1)))
                with pool.Fori(DOWN0 // 2 + 1, NP_ // 2) as i:
                    split(l, (2 * i, i), 0, KH * P, (down_half, l * KD + i - DOWN0 // 2))
                    split(l, (2 * i + 1, i), 1, KH * P, (main_done, at(l, N_MAIN, DOWNM0 + i - DOWN0 // 2 + 1)))
                for i, d in enumerate(range(FFN_DVE, KD)):
                    pool.wait_ge(scaled, at(l, 2 * KD, KD + i + 1))
                    pool.tensor_tensor(x[:, d, :], x[:, d, :], kept_h[:, d, :], ALU.add).then_inc(x_pool, 1)

        @block.tensor
        def _(pe):
            pe.sem_inc(main_done, 1)
            pe.wait_ge(t5_loaded, 32)
            pe.matmul(work[0][0:4, :], t5[:, :], hot[:, :], start=True, stop=True).then_inc(t5_mm, 1)
            pe.wait_ge(t5_copied, 1)

            def three(dst, a_hi, a_lo, b_hi, b_lo, first, last, **kw):
                pe.matmul(dst, a_hi, b_hi, start=first, stop=False, **kw)
                pe.matmul(dst, a_hi, b_lo, start=False, stop=False, **kw)
                return pe.matmul(dst, a_lo, b_hi, start=False, stop=last, **kw)

            def wait_piece(l, n):
                pe.wait_ge(piece_split, at(l, NP_, n + 3))

            def wait_split(l, name):
                pe.wait_ge(lo_done, at(l, N_SPLIT, SPLIT_AT[name] + 1))

            def wait_main(l, m):
                if m < 2:
                    return
                kind, b, j = MAIN[m - 2]
                pe.wait_ge(gate_scaled if kind == "gate" else y_used, at(l, 4 * KD, KD * BR.index(b) + j + 1))

            def wait_work(l, w):
                p = w - 3
                if p < 0:
                    return
                n = WORK[p]
                if n[0] == "score":
                    q = 16 * BR.index(n[1]) + 4 * n[2] + n[3]
                    pe.wait_ge(max_done if banded(n[1]) else exp_done, at(l, 64, q + 1))
                elif n in FEATURE:
                    pe.wait_ge(feature_done, at(l, len(FEATURE), FEATURE.index(n) + 1))
                elif n[:3] == "Ckv":
                    wait_split(l, ("V", "C", 2 * int(n[3]) + 1))
                elif n in COPY:
                    pe.wait_ge(copied, at(l, N_COPY, COPY_AT[n] + 1))
                elif n[:3] == "Dkv":
                    wait_split(l, ("V", "D", int(n[3])))
                elif n[:2] == "Av":
                    wait_split(l, ("V", "A", 2 * int(n[2]) + 1))
                else:
                    wait_split(l, n)

            def wait_turn(l, t):
                p = t - 2
                if p < 0:
                    return
                n = TURN[p]
                if n[0] == "stat":
                    pe.wait_ge(factor_done, at(l, 4, NORMS.index(n[1]) + 1))
                elif n[1] == "pre_ffn":
                    pe.wait_ge(ffn_up, at(l, KF, KF + 2))
                elif n == ("spread", "pre_mix"):
                    pe.wait_ge(mix_factor, at(l, 1, 1))
                elif n[0] == "spread":
                    pe.wait_ge(scaled, at(l, 2 * KD, KD))
                elif n in ("Bv0", "Bv1"):
                    wait_split(l, ("V", "B", 2 * int(n[2]) + 1))
                else:
                    wait_split(l, n)

            def mean_square(l, name):
                sc, t = scratch_of[name], TURN_AT[("stat", name)]
                wait_turn(l, t)

                def tile(sq, first, last):
                    for tt in range(NT):
                        mm = pe.matmul(turn[t % 2][:, tt:tt + 1], sq[:, P * tt:P * tt + P], mean,
                                       start=first and tt == 0, stop=last, skip_group_check=True)
                    return mm

                if name == "pre_mix":
                    pe.wait_ge(summed, at(l, 4 * KD - 2, KD))
                    tile(sc["sum"][:, :], True, True).then_inc(turn_done, 1)
                elif name == "pre_ffn":
                    pe.wait_ge(summed, at(l, 4 * KD - 2, 3 * KD - 1))
                    tile(sc["sum"][:, :], True, True).then_inc(turn_done, 1)
                else:
                    pe.wait_ge(summed, at(l, 4 * KD - 2, 2 * KD - 1 if name == "post_mix" else 4 * KD - 2))
                    tile(sc["sum"][:, :], True, False)
                    pe.wait_ge(squared, at(l, 4 * KD, KD * (NORMS.index(name) + 1)))
                    tile(sc["sq"][:, 1, :], False, True).then_inc(turn_done, 1)

            def spread(l, name):
                t = TURN_AT[("spread", name)]
                wait_turn(l, t)
                pe.wait_ge(factor_done, at(l, 4, NORMS.index(name) + 1))
                for tt in range(NT):
                    mm = pe.matmul(turn[t % 2][:, P * tt:P * tt + P], view(r_out[:, tt:], [[0, P]]), ident, start=True, stop=True)
                mm.then_inc(turn_done, 1)

            def gate_steps(l, b, point):
                for s in range(*GATE_POINTS[b][point:point + 2]):
                    of, j = BR[s // BRANCH_STEPS], s % BRANCH_STEPS // STEPS
                    k, which = s % STEPS // 3, s % 3
                    m = MAIN_AT[("gate", of, j)]
                    if s % STEPS == 0:
                        wait_main(l, m)
                        if j % 2 == 0:
                            wait_piece(l, PIECE[f"gate{of}{j // 2}"])
                    slot = PIECE[f"gate{of}{j // 2}"] % 2
                    col = 256 * k + P * (j % 2)
                    w = (w_lo if which == 2 else w_hi)[:, slot, col:col + P]
                    mm = pe.matmul(main[m % 2][:, :], w, (h_lo if which == 1 else h_hi)[:, k, :],
                                   start=(s % STEPS == 0), stop=(s % STEPS == STEPS - 1))
                    if s % STEPS == STEPS - 1:
                        mm.then_inc(main_done, 1)

            def by_feature(l, name, n, col, width):
                w = WORK_AT[name]
                wait_work(l, w)
                for k in range(KD):
                    a = width * k + col
                    mm = three(work[w % 3][:, :], w_hi[:, n % 2, a:a + P], w_lo[:, n % 2, a:a + P],
                               h_hi[:, k, :], h_lo[:, k, :], k == 0, k == KD - 1)
                mm.then_inc(work_done, 1)

            def by_token(l, name, n, tiles, col, cols, width):
                w = WORK_AT[name]
                wait_work(l, w)
                for i, t in enumerate(tiles):
                    dst = work[w % 3][:, i * cols:(i + 1) * cols]
                    for k in range(KD):
                        a = width * k + col
                        mm = three(dst, h_hi[:, k, P * t:P * t + P], h_lo[:, k, P * t:P * t + P],
                                   w_hi[:, n % 2, a:a + cols], w_lo[:, n % 2, a:a + cols], k == 0, k == KD - 1)
                mm.then_inc(work_done, 1)

            def turn_tiles(l, name, sources, rows=P):
                t = TURN_AT[name]
                wait_turn(l, t)
                for i, src in enumerate(sources):
                    mm = pe.transpose(turn[t % 2][0:rows, P * i:P * i + P], src, ident)
                mm.then_inc(turn_done, 1)

            def queries(b, h):
                if b == "D":
                    return qd_hi[0:DQK, h, :], qd_lo[0:DQK, h, :]
                a = HD * (h % 2)
                return qa_hi[a:a + HD, h // 2, :], qa_lo[a:a + HD, h // 2, :]

            def keys(b, h):
                if b == "D":
                    return kd_hi[0:DQK, h, :], kd_lo[0:DQK, h, :]
                a, j = HD * (h % 2), h // 2 if b == "A" else 0
                return ka_hi[a:a + HD, j, :], ka_lo[a:a + HD, j, :]

            def head(l, b, h):
                (q_h, q_l), (k_h, k_l) = queries(b, h), keys(b, h)
                for t in range(NT):
                    w = WORK_AT[("score", b, h, t)]
                    ks = window(b, t)
                    a, n = P * ks[0], P * len(ks)
                    wait_work(l, w)
                    three(work[w % 3][:, 0:n], q_h[:, P * t:P * t + P], q_l[:, P * t:P * t + P],
                          k_h[:, a:a + n], k_l[:, a:a + n], True, True).then_inc(work_done, 1)
                    gate_steps(l, b, gate_point(b, h, t))

                def turn_prob(k):
                    t = TURN_AT[("prob", b, h, k)]
                    wait_turn(l, t)
                    qs = [q for q in range(NT) if k in window(b, q)]
                    pe.wait_ge(prob_done, at(l, 64, 16 * BR.index(b) + 4 * h + qs[-1] + 1))
                    for q in qs:
                        a = P * (k - window(b, q)[0])
                        mm = pe.transpose(turn[t % 2][:, P * q:P * q + P], prob[:, q, a:a + P], ident)
                    mm.then_inc(turn_done, 1)

                def values(k):
                    if h == 0 and k == 0:
                        wait_split(l, ("V", b, NT - 1))
                    qs = [q for q in range(NT) if k in window(b, q)]
                    a, z = P * qs[0], P * (qs[-1] + 1)
                    wait_split(l, ("prob", b, h, k))
                    v = slice(HD * (h % 2), HD * (h % 2) + P)
                    j = 0 if b in "BC" else h // 2
                    mm = three(pv[:, a:z], v_hi[:, k, j, v], v_lo[:, k, j, v], pt_hi[:, k % 2, a:z],
                               pt_lo[:, k % 2, a:z], h % 2 == 0 and k == 0, h % 2 == 1 and k == NT - 1, skip_group_check=True)
                    if h % 2 == 1 and k == NT - 1:
                        mm.then_inc(pv_done, 1)

                turn_prob(0)
                gate_steps(l, b, gate_point(b, h, 4))
                turn_prob(1)
                gate_steps(l, b, gate_point(b, h, 5))
                if h == 2:
                    wait_split(l, ("o", b, 0))
                values(0)
                turn_prob(2)
                gate_steps(l, b, gate_point(b, h, 6))
                values(1)
                turn_prob(3)
                gate_steps(l, b, gate_point(b, h, 7))
                values(2)
                values(3)
                gate_steps(l, b, gate_point(b, h, 8))

            def branch_out(l, b):
                n = PIECE[f"branch{b}"]
                wait_piece(l, n)
                for d in range(KD):
                    m = MAIN_AT[("y", b, d)]
                    wait_main(l, m)
                    for k in range(2):
                        if d == 0:
                            wait_split(l, ("o", b, k))
                        a = DM * k + P * d
                        mm = three(main[m % 2][:, :], w_hi[:, n % 2, a:a + P], w_lo[:, n % 2, a:a + P],
                                   o_hi[:, k, :], o_lo[:, k, :], k == 0, k == 1)
                    mm.then_inc(main_done, 1)

            with pe.Fori(0, L) as l:
                for t in range(3):
                    wait_work(l, WORK_AT[f"Dlat{t}"])
                for k in range(KD):
                    if k % 4 == 0:
                        wait_piece(l, PIECE[f"Dlat{k // 4}"])
                    wait_split(l, ("h", "pre_mix", k))
                    a, slot = N_LAT * (k % 4), k // 4
                    for t in range(NT):
                        mm = three((work[t] if t < 3 else pv)[:, 0:N_LAT],
                                   h_hi[:, k, P * t:P * t + P], h_lo[:, k, P * t:P * t + P],
                                   w_hi[:, slot, a:a + N_LAT], w_lo[:, slot, a:a + N_LAT], k == 0, k == KD - 1)
                        if k == KD - 1:
                            mm.then_inc(work_done if t < 3 else pv_done, 1)
                    if k == 3:
                        mm.then_inc(lat_half, 1)
                pe.wait_ge(loaded, 16)
                mean_square(l, "pre_mix")
                gate_steps(l, "D", 0)
                spread(l, "pre_mix")
                gate_steps(l, "D", 1)
                for j in range(3):
                    pe.wait_ge(latents, at(l, 4, 1 if j < 2 else 2))
                    turn_tiles(l, ("latent", j), [d_tm[:, t, P * j:P * j + P] for t in range(NT)])
                gate_steps(l, "D", 2)
                n = PIECE["Dup"]
                wait_piece(l, n)
                for t in range(NT):
                    w = WORK_AT[f"Dq{t}"]
                    wait_work(l, w)
                    for j in range(2):
                        if t == 0:
                            wait_split(l, ("latent", j))
                        mm = three(work[w % 3][:, 0:384], lat_hi[:, j, P * t:P * t + P], lat_lo[:, j, P * t:P * t + P],
                                   w_hi[:, n % 2, 384 * j:384 * j + 384], w_lo[:, n % 2, 384 * j:384 * j + 384], j == 0, j == 1)
                    mm.then_inc(work_done, 1)
                wait_split(l, ("latent", 2))
                for t in range(NT):
                    w = WORK_AT[f"Dkv{t}"]
                    wait_work(l, w)
                    three(work[w % 3][:, :], lat_hi[:, 2, P * t:P * t + P], lat_lo[:, 2, P * t:P * t + P],
                          w_hi[:, n % 2, 768:1280], w_lo[:, n % 2, 768:1280], True, True).then_inc(work_done, 1)
                gate_steps(l, "D", 3)
                pe.wait_ge(copied, at(l, N_COPY, COPY_AT["Dk3"] + 1))
                for h in range(4):
                    for i, (name, tm, count) in enumerate((("Dq", dq_tm, 4), ("Dk", dk_tm, 3))):
                        pe.wait_ge(latents, at(l, 4, count))
                        turn_tiles(l, (name, h), [tm[:, t, DQK * h:DQK * h + DQK] for t in range(NT)], DQK)
                        gate_steps(l, "D", 4 + 2 * h + i)
                for h in range(4):
                    wait_split(l, ("Dk", h))
                    head(l, "D", h)
                branch_out(l, "D")

                for name in ("Aq", "Ak"):
                    wait_piece(l, PIECE[name])
                    for j in range(2):
                        by_feature(l, f"{name}{j}", PIECE[name], P * j, 256)
                wait_piece(l, PIECE["Av"])
                for j in range(2):
                    by_token(l, f"Av{j}", PIECE["Av"], (2 * j, 2 * j + 1), 0, 256, 256)
                for h in range(4):
                    if h == 0:
                        wait_split(l, "Ak1")
                    head(l, "A", h)
                branch_out(l, "A")

                wait_piece(l, PIECE["Bq"])
                for j in range(2):
                    by_feature(l, f"Bq{j}", PIECE["Bq"], P * j, 256)
                wait_piece(l, PIECE["Bkv"])
                by_feature(l, "Bk", PIECE["Bkv"], 0, 256)
                by_feature(l, "Bv", PIECE["Bkv"], P, 256)
                pe.wait_ge(feature_done, at(l, len(FEATURE), FEATURE.index("Bv") + 1))
                for j in range(2):
                    turn_tiles(l, f"Bv{j}", [feature[:, 3, P * t:P * t + P] for t in (2 * j, 2 * j + 1)])
                for h in range(4):
                    if h == 0:
                        wait_split(l, "Bk")
                    head(l, "B", h)
                branch_out(l, "B")

                wait_piece(l, PIECE["Cq"])
                by_token(l, "Cq0", PIECE["Cq"], (0, 1), 0, 256, 256)
                by_token(l, "Cq1", PIECE["Cq"], (2, 3), 0, 256, 256)
                wait_piece(l, PIECE["Ckv"])
                by_token(l, "Ckv0", PIECE["Ckv"], (0, 1), 0, 256, 256)
                by_token(l, "Ckv1", PIECE["Ckv"], (2, 3), 0, 256, 256)
                gate_steps(l, "C", 0)
                for j in range(3):
                    pe.wait_ge(c_ready, at(l, 2, 1 + j // 2))
                    turn_tiles(l, ("C", j), [c_tm[:, t, P * j:P * j + P] for t in range(NT)])
                    gate_steps(l, "C", 1 + j)
                for h in range(4):
                    if h == 0:
                        wait_split(l, ("C", 2))
                    head(l, "C", h)
                branch_out(l, "C")

                with pe.Fori(0, 2) as i:
                    for s in range(2):
                        pe.wait_ge(piece_split, l * NP_ + 2 * i + (OUT0 + s + 3))
                        for j in range(2):
                            m = 2 * s + j
                            if m < 2:
                                pe.wait_ge(y_used, at(l, 4 * KD, 3 * KD + 6 + m + 1))
                            pe.wait_ge(kept_done, l * 2 * KD + 4 * i + m + 1)
                            for k in range(KD):
                                if m == 0:
                                    wait_split(l, ("merged", k))
                                a = 256 * k + P * j
                                mm = three(main[m % 2][:, :], w_hi[:, s, a:a + P], w_lo[:, s, a:a + P],
                                           h_hi[:, k, :], h_lo[:, k, :], k == 0, k == KD - 1)
                            mm.then_inc(main_done, 1)

                mean_square(l, "post_mix")
                spread(l, "post_mix")

                def gate_up(i, s, js, ks=range(KD), first=False):
                    for j in js if ks[0] == 0 else ():
                        pe.wait_ge(ffn_up if j else ffn_scaled, l * KF + 2 * i + s + 1)
                    for k in ks:
                        if first:
                            wait_split(l, ("h", "pre_ffn", k))
                        for j in js:
                            a = 256 * k + P * j
                            mm = three(ffn_bank[s][j][:, :], w_hi[:, s, a:a + P], w_lo[:, s, a:a + P],
                                       h_hi[:, k, :], h_lo[:, k, :], k == 0, k == KD - 1)
                            if k == KD - 1:
                                mm.then_inc(main_done, 1)

                wait_piece(l, GU0)
                gate_up(0, 0, (0, 1), first=True)
                wait_piece(l, GU0 + 1)
                gate_up(0, 1, (0,), range(2))
                mean_square(l, "pre_ffn")
                gate_up(0, 1, (0,), range(2, KD))
                gate_up(0, 1, (1,), range(1))
                spread(l, "pre_ffn")
                gate_up(0, 1, (1,), range(1, KD))
                with pe.Fori(1, KF // 2) as i:
                    for s in range(2):
                        pe.wait_ge(piece_split, l * NP_ + 2 * i + (GU0 + s + 3))
                        gate_up(i, s, (0,))
                        gate_up(i, s, (1,))

                with pe.Fori(0, KD // 2) as i:
                    for d in range(2):
                        pe.wait_ge(ffn_up if d else ffn_scaled, at(l, KF, KF + 2))
                        pe.wait_ge(kept_done, l * 2 * KD + 2 * i + KD + d + 1)
                        for s in range(2):
                            pe.wait_ge(piece_split, l * NP_ + 4 * i + (DOWN0 + 2 * d + s + 3))
                            for k in range(KH):
                                if d == 0:
                                    wait_split(l, ("act", KH * s + k))
                                kk = KH * s + k
                                mm = three(main[d][:, :], w_hi[:, s, P * k:P * k + P], w_lo[:, s, P * k:P * k + P],
                                           act_hi[:, kk, :], act_lo[:, kk, :], kk == 0, kk == KF - 1)
                            mm.then_inc(main_done if s else down_half, 1)
                mean_square(l, "post_ffn")
                spread(l, "post_ffn")

        @block.scalar
        def _(act):
            splits = iter(SPLIT)

            def hi(l, name, dst, src, scale=1.0):
                assert next(splits) == name
                act.activation(dst, src, ACT.Copy, scale=scale).then_inc(hi_done, 1)

            def wait_turn_done(l, name):
                act.wait_ge(turn_done, at(l, N_TURN, TURN_AT[name] + 1))

            def wait_work_done(l, name):
                act.wait_ge(work_done, at(l, N_WORK, WORK_AT[name] + 1))

            copies = iter(COPY)

            def copy(l, name, dst, src):
                assert next(copies) == name
                act.activation(dst, src, ACT.Copy).then_inc(copied, 1)

            def keep(l, name):
                i, sc, kept = NORMS.index(name), scratch_of[name], kept_of[name]
                m0 = WOUT0 if name == "post_mix" else DOWNM0
                for d in range(KD):
                    act.wait_ge(main_done, at(l, N_MAIN, m0 + d + 2))
                    if d >= 2:
                        act.wait_ge(summed, at(l, 4 * KD - 2, (KD if name == "post_mix" else 3 * KD - 1) + d - 1))
                    act.activation(sc["sq"][:, d % 2, :], main[d % 2][:, :], ACT.Square).then_inc(squared, 1)
                    act.activation(kept[:, d, :], main[d % 2][:, :], ACT.Copy, scale=param(name, d)).then_inc(kept_done, 1)

            def mixer_input(l):
                for d in range(KD):
                    act.wait_ge(x_loaded[d // 2], 16)
                    act.wait_ge(x_dve, at(l, N_X, X0 + d + 1 if d < FFN_DVE else N_X))
                    if d >= FFN_DVE:
                        act.wait_ge(x_pool, at(l, KD, d - FFN_DVE + 1))
                    hi(l, ("h", "pre_mix", d), h_hi[:, d, :], x[:, d, :], param("pre_mix", d))
                    act.activation(norm_f["sq"][:, d, :], x[:, d, :], ACT.Square).then_inc(squared, 1)

            def ffn_input(l):
                for d in range(KD):
                    if d < MIX_DVE:
                        act.wait_ge(x_dve, at(l, N_X, N_X + d + 1))
                    else:
                        act.wait_ge(x_pool, at(l, KD, X0 + d - MIX_DVE + 1))
                    hi(l, ("h", "pre_ffn", d), h_hi[:, d, :], x[:, d, :], param("pre_ffn", d))
                    act.activation(norm_f["sq"][:, d, :], x[:, d, :], ACT.Square).then_inc(squared, 1)

            def gate_tanh(l, b, point):
                for of, j in gate_tiles(b, point):
                    act.wait_ge(gate_scaled, at(l, 4 * KD, KD * BR.index(of) + j + 1))
                    act.activation(gates_of[of][:, j, :], gates_of[of][:, j, :], ACT.Tanh, scale=0.5).then_inc(tanh_done, 1)

            def value_parts(l, b, t, src, scale=1.0):
                hi(l, ("V", b, t), value_place(v_hi, b, t), src, scale)

            def head(l, b, h):
                q0 = 16 * BR.index(b) + 4 * h
                for t in range(NT):
                    w = WORK_AT[("score", b, h, t)]
                    n = P * len(window(b, t))
                    src = prob[:, t, 0:n] if banded(b) else work[w % 3][:, 0:n]
                    act.wait_ge(max_done, at(l, 64, q0 + t + 1))
                    e = act.activation(prob[:, t, 0:n], src, ACT.Exp, bias=negmax[:, t:t + 1], accum_out=sums[:, t:t + 1])
                    if b == "B":
                        e = act.activation(esink[:, t:t + 1], param("sink", h), ACT.Exp, bias=negmax[:, t:t + 1])
                    e.then_inc(exp_done, 1)
                    for n in gates_after(b, t):
                        gate_tanh(l, b, gate_point(b, h, n))
                for k in range(NT):
                    qs = [q for q in range(NT) if k in window(b, q)]
                    a, z = P * qs[0], P * (qs[-1] + 1)
                    wait_turn_done(l, ("prob", b, h, k))
                    hi(l, ("prob", b, h, k), pt_hi[:, k % 2, a:z], turn[TURN_AT[("prob", b, h, k)] % 2][:, a:z])
                    gate_tanh(l, b, gate_point(b, h, 4 + k))
                if h % 2:
                    act.wait_ge(pv_done, at(l, 9, 1 + 2 * BR.index(b) + h // 2 + 1))
                    dst, src = o_hi[:, h // 2, :], pv[:, :]
                    if b == "B":
                        dst, src = in_blocks(dst), in_sequence(src)
                    hi(l, ("o", b, h // 2), dst, src)
                gate_tanh(l, b, gate_point(b, h, 8))

            act.sem_inc(kept_done, 2)
            act.dma_start(hot[:, :], hot_in).then_inc(t5_loaded, 16)
            act.dma_start(t5[:, :], t5_in).then_inc(t5_loaded, 16)
            for d in range(0, KD, 2):
                act.dma_start(x[:, d:d + 2, :], x_in[:, d:d + 2, :]).then_inc(x_loaded[d // 2], 16)
            act.dma_start(const[:, :], const_in).then_inc(loaded, 16)
            act.wait_ge(t5_copied, 1)
            act.dma_start(t5_first, t5_row[:, :]).then_inc(t5_sem, 16)
            with act.Fori(0, L) as l:
                line = rpb_in[bass.ds(l, 1), :]
                act.dma_start(rpb_line, bass.AP(tensor=line.tensor, offset=line.offset, ap=[[0, 16], [1, N_RPB]])).then_inc(rpb_sem, 16)
                act.wait_ge(params_in_place, 16 * l + 16)
                mixer_input(l)
                act.wait_ge(t5_sem, 16 * l + 16)
                act.dma_start(t5_line, bass.AP(tensor=t5_first.tensor, offset=0, ap=[[0, P], [1, 4 * BIAS_X]])).then_inc(t5_sem, 16)

                act.wait_ge(token_ready, at(l, 1, 1))
                act.wait_ge(pv_done, at(l, 9, 1))
                banks = work + [pv]
                for t in range(NT):
                    r = r_token[:, t:t + 1]
                    act.activation(d_sq[:, t, 0:QL], banks[t][:, 0:QL], ACT.Square, scale=r, accum_out=r_in[:, t:t + 1])
                    e = act.activation(d_sq[:, t, QL:384], banks[t][:, QL:384], ACT.Square, scale=r, accum_out=r_in[:, NT + t:NT + t + 1])
                e.then_inc(lat_squared, 1)
                for t in range(NT):
                    assert next(copies) == f"Dlat{t}"
                    act.activation(d_tm[:, t, :], banks[t][:, 0:N_LAT], ACT.Copy, scale=r_token[:, t:t + 1]).then_inc(copied, 1)
                act.wait_ge(t5_sem, 16 * l + 32)
                act.dma_start(bias_b[:, :, :], bass.AP(tensor=t5_line.tensor, offset=P - 1,
                                                       ap=[[4 * BIAS_X - 1, P], [BIAS_X, 4], [1, 384]])).then_inc(t5_ready, 16)
                for j in range(3):
                    wait_turn_done(l, ("latent", j))
                    hi(l, ("latent", j), lat_hi[:, j, :], turn[TURN_AT[("latent", j)] % 2][:, :], param("latent", j))
                for t in range(NT):
                    wait_work_done(l, f"Dq{t}")
                    copy(l, f"Dq{t}", dq_tm[:, t, :], work[WORK_AT[f"Dq{t}"] % 3][:, 0:384])
                act.wait_ge(v_clear, at(l, 2, 2))
                for t in range(NT):
                    wait_work_done(l, f"Dkv{t}")
                    kv = work[WORK_AT[f"Dkv{t}"] % 3][:, :].rearrange("p (h c) -> p h c", h=4)
                    copy(l, f"Dk{t}", dk_tm[:, t, :].rearrange("p (h c) -> p h c", h=4)[:, :, 0:HD], kv[:, :, 0:HD])
                    value_parts(l, "D", t, view(kv[:, :, HD:P], [[2 * P, 2], [P, 2], [1, HD]]))
                for n in range(4):
                    gate_tanh(l, "D", n)
                for h in range(4):
                    wait_turn_done(l, ("Dq", h))
                    hi(l, ("Dq", h), qd_hi[0:DQK, h, :], turn[TURN_AT[("Dq", h)] % 2][0:DQK, :], DQK ** -0.5)
                    wait_turn_done(l, ("Dk", h))
                    hi(l, ("Dk", h), kd_hi[0:DQK, h, :], turn[TURN_AT[("Dk", h)] % 2][0:DQK, :])
                for n in range(4, 12):
                    gate_tanh(l, "D", n)
                for h in range(4):
                    head(l, "D", h)

                for name, dst, scale in (("Aq", qa_hi, HD ** -0.5), ("Ak", ka_hi, 1.0)):
                    for j in range(2):
                        n = FEATURE.index(f"{name}{j}")
                        act.wait_ge(feature_done, at(l, len(FEATURE), n + 1))
                        hi(l, f"{name}{j}", dst[:, j, :], feature[:, n, :], scale)
                        if n == 0:
                            act.wait_ge(rpb_sem, 16 * l + 16)
                            for r in range(ROWS):
                                act.dma_start(rpb[16 * r:16 * r + 16, :, :],
                                              bass.AP(tensor=rpb_line.tensor, offset=(7 - r) * RPB_ROW + 15,
                                                      ap=[[N_RPB - 1, 16], [RPB_HEAD, 4], [1, 512]])).then_inc(rpb_in_place, 16)
                for j in range(2):
                    wait_work_done(l, f"Av{j}")
                    for i in range(2):
                        src = work[WORK_AT[f"Av{j}"] % 3][:, 256 * i:256 * i + 256].rearrange("p (a c d) -> p a c d", a=2, c=2)
                        value_parts(l, "A", 2 * j + i, src, r_token[:, 2 * j + i:2 * j + i + 1])
                for h in range(4):
                    head(l, "A", h)

                for j, (name, dst, scale) in enumerate((("Bq0", qa_hi[:, 0, :], HD ** -0.5), ("Bq1", qa_hi[:, 1, :], HD ** -0.5),
                                                        ("Bk", ka_hi[:, 0, :], 1.0))):
                    act.wait_ge(feature_done, at(l, len(FEATURE), FEATURE.index(name) + 1))
                    hi(l, name, dst, feature[:, j, :], scale)
                for t in range(NT):
                    wait_turn_done(l, f"Bv{t // 2}")
                    src = turn[TURN_AT[f"Bv{t // 2}"] % 2][:, P * (t % 2):P * (t % 2) + P]
                    value_parts(l, "B", t, src.rearrange("p (c d) -> p c d", d=HD))
                for h in range(4):
                    head(l, "B", h)

                def copy_tiles(name, cols, at_col):
                    wait_work_done(l, name)
                    assert next(copies) == name
                    for t in (2 * int(name[-1]), 2 * int(name[-1]) + 1):
                        e = act.activation(c_tm[:, t, at_col:at_col + cols], work[WORK_AT[name] % 3][:, 256 * (t % 2):256 * (t % 2) + cols],
                                           ACT.Copy, scale=r_token[:, t:t + 1])
                    e.then_inc(copied, 1)

                copy_tiles("Cq0", 256, 0)
                copy_tiles("Cq1", 256, 0)
                for j in range(2):
                    copy_tiles(f"Ckv{j}", P, 256)
                    for t in (2 * j, 2 * j + 1):
                        src = work[WORK_AT[f"Ckv{j}"] % 3][:, 256 * (t % 2) + P:256 * (t % 2) + 2 * P]
                        value_parts(l, "C", t, src.rearrange("p (c d) -> p c d", d=HD), r_token[:, t:t + 1])
                for j in range(3):
                    wait_turn_done(l, ("C", j))
                    src = turn[TURN_AT[("C", j)] % 2][:, :]
                    if j < 2:
                        hi(l, ("C", j), qa_hi[:, j, :], src, HD ** -0.5)
                    else:
                        hi(l, ("C", j), ka_hi[:, 0, :], src)
                for j in range(4):
                    gate_tanh(l, "C", j)
                for h in range(4):
                    head(l, "C", h)
                for d in range(KD):
                    act.wait_ge(merged_done, at(l, 3 * KD, 2 * KD + d + 1))
                    hi(l, ("merged", d), h_hi[:, d, :], merged[:, d, :], 0.5)

                keep(l, "post_mix")
                ffn_input(l)
                with act.Fori(0, KF // 2) as i:
                    for s in range(2):
                        act.wait_ge(ffn_scaled, l * KF + 2 * i + s + 3)
                        act.activation(ffn_t[:, s, :], ffn_g[:, s, :], ACT.Tanh, scale=0.5).then_inc(ffn_tanh, 1)
                        act.wait_ge(ffn_full, l * KF + 2 * i + s + 1)
                        act.sem_inc(waited, 1)
                        act.activation(act_hi[:, bass.ds(2 * i + s, 1), :].rearrange("p a s -> p (a s)"), ffn_g[:, s, :],
                                       ACT.Copy).then_inc(hi_done, 1)
                keep(l, "post_ffn")

        @block.vector
        def _(dve):
            dve.sem_inc(ffn_scaled, 2)
            dve.sem_inc(ffn_up, 2)
            dve.sem_inc(x_dve, X0 + KD)
            dve.wait_ge(t5_mm, 1)
            dve.tensor_copy(t5_row[:, :], work[0][0:4, :]).then_inc(t5_copied, 1)
            steps = [0]

            def step(l, ins):
                ins.then_inc(chain, 1)
                steps[0] += 1
                dve.wait_ge(chain, at(l, N_CHAIN, steps[0]))

            splits = iter(SPLIT)

            def lo(l, name, dst, src, part, scale=None, after=None):
                assert next(splits) == name
                dve.wait_ge(hi_done, at(l, N_SPLIT, SPLIT_AT[after or name] + 1))
                if scale is None:
                    dve.tensor_tensor(dst, src, part.bitcast(F32), ALU.subtract).then_inc(lo_done, 1)
                else:
                    dve.scalar_tensor_tensor(out=dst, in0=src, scalar=scale, in1=part.bitcast(F32),
                                             op0=ALU.mult, op1=ALU.subtract).then_inc(lo_done, 1)

            def feature_tile(l, name, in_order=False):
                n = FEATURE.index(name)
                dve.wait_ge(work_done, at(l, N_WORK, WORK_AT[name] + 1))
                dst, src, factors = feature[:, n % 4, :], work[WORK_AT[name] % 3][:, :], r_all[:, :]
                if in_order:
                    dst, src, factors = in_sequence(dst), in_blocks(src), in_blocks(factors)
                dve.tensor_tensor(dst, src, factors, ALU.mult).then_inc(feature_done, 1)

            def gate_scale(l, b, point):
                for of, j in gate_tiles(b, point):
                    if j == 0 and of in BR[2:]:
                        dve.wait_ge(y_used, at(l, 4 * KD, KD * BR.index(of)))
                    m = MAIN_AT[("gate", of, j)]
                    dve.wait_ge(main_done, at(l, N_MAIN, m + 2))
                    dve.tensor_tensor(gates_of[of][:, j, :], main[m % 2][:, :], r_all[:, :], ALU.mult).then_inc(gate_scaled, 1)

            def root(l, n, last=None):
                v, y, t = r_in[:, 0:n], r_out[:, 0:n], r_tmp[:, 0:n]
                step(l, dve.tensor_scalar(y.bitcast(I32), v.bitcast(I32), -0.5, float(0x5F3759DF), ALU.mult, ALU.add))
                for i in range(3):
                    step(l, dve.tensor_tensor(t, y, y, ALU.mult))
                    step(l, dve.scalar_tensor_tensor(out=t, in0=t, scalar=-0.5, in1=v, op0=ALU.mult, op1=ALU.mult))
                    e = dve.scalar_tensor_tensor(out=y, in0=t, scalar=1.5, in1=y, op0=ALU.add, op1=ALU.mult)
                    if i == 2 and last is not None:
                        e.then_inc(last, 1)
                    else:
                        step(l, e)

            def sum_squares(l, name, tiles):
                base = dict(pre_mix=0, post_mix=KD, pre_ffn=2 * KD - 1, post_ffn=3 * KD - 1)[name]
                i, sc = NORMS.index(name), scratch_of[name]
                ring = sc["sq"].shape[1]
                for d in range(tiles):
                    dve.wait_ge(squared, at(l, 4 * KD, KD * i + d + 1))
                    if d == 0:
                        dve.tensor_copy(sc["sum"][:, :], sc["sq"][:, 0, :]).then_inc(summed, 1)
                    else:
                        dve.wait_ge(summed, at(l, 4 * KD - 2, base + d))
                        dve.tensor_tensor(sc["sum"][:, :], sc["sum"][:, :], sc["sq"][:, d % ring, :], ALU.add).then_inc(summed, 1)

            def token_factor(l, name, keep=None):
                t = TURN_AT[("stat", name)]
                dve.wait_ge(turn_done, at(l, N_TURN, t + 1))
                step(l, dve.tensor_scalar(r_in[:, 0:NT], turn[t % 2][:, 0:NT], EPS, None, ALU.add))
                root(l, NT, factor_done)
                if keep is not None:
                    dve.wait_ge(factor_done, at(l, 4, 1))
                    dve.tensor_copy(keep, r_out[:, 0:NT]).then_inc(token_ready, 1)

            def factor(l, name):
                dve.wait_ge(turn_done, at(l, N_TURN, TURN_AT[("spread", name)] + 1))
                return turn[TURN_AT[("spread", name)] % 2][:, :]

            def mixer_input(l):
                for d in range(KD):
                    lo(l, ("h", "pre_mix", d), h_lo[:, d, :], x[:, d, :], h_hi[:, d, :], param("pre_mix", d))
                sum_squares(l, "pre_mix", KD)
                token_factor(l, "pre_mix", r_token)

            def output_factor(l, name):
                sum_squares(l, name, KD - 1)
                dve.wait_ge(kept_done, at(l, 2 * KD, KD * (name == "post_ffn") + KD + 2))
                token_factor(l, name)

            def add_output(l, name, d, i, add):
                n, kept = KD * (name == "post_ffn") + i + 1, kept_of[name]
                dve.tensor_tensor(kept[:, d, :], kept[:, d, :], factor(l, name), ALU.mult).then_inc(scaled, 1)
                if add:
                    dve.wait_ge(scaled, at(l, 2 * KD, n))
                    dve.tensor_tensor(x[:, d, :], x[:, d, :], kept[:, d, :], ALU.add).then_inc(x_dve, 1)

            def wait_work_done(l, name):
                dve.wait_ge(work_done, at(l, N_WORK, WORK_AT[name] + 1))

            def value_parts(l, b, t, src, scale=None):
                last = t if b == "D" else t | 1
                lo(l, ("V", b, t), value_place(v_lo, b, t), src, value_place(v_hi, b, t), scale, after=("V", b, last))

            def norm_and_rotate(l, g0, n, gain):
                x = c_tm[:, :, HD * g0:HD * (g0 + n)]
                heads = x.rearrange("p t (g d) -> p t g d", d=HD)
                squares = c_sq[:, 0:NT * HD * n]
                step(l, dve.tensor_tensor(squares.rearrange("p (t d) -> p t d", t=NT), x, x, ALU.mult))
                step(l, dve.tensor_reduce(r_in[:, 0:NT * n], squares.rearrange("p (g d) -> p g d", d=HD), AX.X, ALU.add))
                step(l, dve.tensor_scalar(r_in[:, 0:NT * n], r_in[:, 0:NT * n], 1.0 / HD, EPS, ALU.mult, ALU.add))
                root(l, NT * n)
                step(l, dve.tensor_tensor(heads, heads, view(r_out, [[n, NT], [1, n], [0, HD]]), ALU.mult))
                step(l, dve.tensor_tensor(heads, heads, view(param(gain, 0, HD), [[0, NT], [0, n], [1, HD]]), ALU.mult))
                cos, sin = (c(name).rearrange("p (t f c) -> p t f c", t=NT, f=2) for name in ("cosC", "sinC"))
                for g in range(n):
                    half = heads[:, :, g, :].rearrange("p t (f c) -> p t f c", f=2)
                    x1, x2 = half[:, :, :, 0:16], half[:, :, :, 16:32]
                    tmp = [c_sq[:, a:a + P].rearrange("p (t f c) -> p t f c", t=NT, f=2) for a in range(512 * (g % 2), 512 * (g % 2) + 512, P)]
                    for i, (a1, a2) in enumerate(((x1, cos), (x2, sin), (x2, cos), (x1, sin))):
                        e = dve.tensor_tensor(tmp[i], a1, a2, ALU.mult)
                    step(l, e)
                    dve.tensor_tensor(x1, tmp[0], tmp[1], ALU.subtract)
                    e = dve.tensor_tensor(x2, tmp[2], tmp[3], ALU.add)
                e.then_inc(c_ready, 1)

            def window_bias(l, h):
                a, blocks = 0, ((1, 2), (0, 3), (0, 2))
                for v, (b0, nb) in enumerate(blocks):
                    src = view(rpb[:, h, 16 * b0:], [[16, nb], [RPB_ROW, ROWS], [1, 16]])
                    mask = view(c("maskA")[:, 48 * v + 16 * b0:], [[16, nb], [0, ROWS], [1, 16]])
                    dst = bias_a[:, h % 2, a:a + nb * P].rearrange("p (b r c) -> p b r c", r=ROWS, c=16)
                    step(l, dve.tensor_tensor(dst, src, mask, ALU.add))
                    a += nb * P

            def head(l, b, h):
                q0, w0 = 16 * BR.index(b) + 4 * h, WORK_AT[("score", b, h, 0)]

                def maximum(t):
                    n = P * len(window(b, t))
                    scores = work[(w0 + t) % 3][:, 0:n]
                    dve.wait_ge(work_done, at(l, N_WORK, w0 + t + 1))
                    if not banded(b):
                        dve.tensor_reduce(negmax[:, t:t + 1], scores, AX.X, ALU.max, negate=True).then_inc(max_done, 1)
                        return
                    if b == "A":
                        bias = bias_a[:, h % 2, (0, 256, 256, 640)[t]:(0, 256, 256, 640)[t] + n]
                        least = -3.0e38
                    else:
                        bias = bias_b[:, h, (P if t == 0 else 0):(P if t == 0 else 0) + n]
                        least = param("sink", h)
                    dve.sem_inc(waited, 1)
                    dve.tensor_tensor_reduce(prob[:, t, 0:n], scores, bias, 1.0, least, ALU.add, ALU.max,
                                             maxima[:, t:t + 1]).then_inc(bias_done, 1)
                    dve.wait_ge(bias_done, at(l, 32, q0 - 16 + t + 1))
                    dve.tensor_scalar(negmax[:, t:t + 1], maxima[:, t:t + 1], -1.0, None, ALU.mult).then_inc(max_done, 1)

                def normalise(t):
                    n = P * len(window(b, t))
                    dve.wait_ge(exp_done, at(l, 64, q0 + t + 1))
                    if b == "B":
                        step(l, dve.tensor_tensor(sums[:, t:t + 1], sums[:, t:t + 1], esink[:, t:t + 1], ALU.add))
                    dve.reciprocal(recip[:, t:t + 1], sums[:, t:t + 1]).then_inc(recip_done, 1)
                    dve.wait_ge(recip_done, at(l, 64, q0 + t + 1))
                    dve.tensor_scalar(prob[:, t, 0:n], prob[:, t, 0:n], recip[:, t:t + 1], None, ALU.mult).then_inc(prob_done, 1)

                for t in range(NT):
                    maximum(t)
                    if t:
                        normalise(t - 1)
                    if t == NT - 1:
                        normalise(t)
                    for n in gates_after(b, t):
                        gate_scale(l, b, gate_point(b, h, n))
                for k in range(NT):
                    qs = [q for q in range(NT) if k in window(b, q)]
                    a, z = P * qs[0], P * (qs[-1] + 1)
                    lo(l, ("prob", b, h, k), pt_lo[:, k % 2, a:z], turn[TURN_AT[("prob", b, h, k)] % 2][:, a:z], pt_hi[:, k % 2, a:z])
                    gate_scale(l, b, gate_point(b, h, 4 + k))
                if h % 2:
                    j = h // 2
                    dst, src, part = o_lo[:, j, :], pv[:, :], o_hi[:, j, :]
                    if b == "B":
                        dst, src, part = in_blocks(dst), in_sequence(src), in_blocks(part)
                    lo(l, ("o", b, j), dst, src, part)
                gate_scale(l, b, gate_point(b, h, 8))

            def gate_outputs(l, b):
                def merged_lo(d):
                    lo(l, ("merged", d), h_lo[:, d, :], merged[:, d, :], h_hi[:, d, :], 0.5)

                for d in range(KD):
                    m = MAIN_AT[("y", b, d)]
                    dve.wait_ge(main_done, at(l, N_MAIN, m + 2))
                    dve.wait_ge(tanh_done, at(l, 4 * KD, KD * BR.index(b) + d + 1))
                    dst = merged[:, d, :] if b == BR[0] else yt[:, d % 2, :]
                    if b != BR[0] and d >= 2:
                        dve.wait_ge(merged_done, at(l, 3 * KD, KD * (BR.index(b) - 1) + d - 1))
                    dve.scalar_tensor_tensor(out=dst, in0=gates_of[b][:, d, :], scalar=1.0, in1=main[m % 2][:, :],
                                             op0=ALU.add, op1=ALU.mult).then_inc(y_used, 1)
                    if b != BR[0]:
                        dve.wait_ge(y_used, at(l, 4 * KD, KD * BR.index(b) + d + 1))
                        dve.tensor_tensor(merged[:, d, :], merged[:, d, :], yt[:, d % 2, :], ALU.add).then_inc(merged_done, 1)
                    if b == BR[-1] and d >= KD - AHEAD:
                        merged_lo(d - (KD - AHEAD))
                for d in range(AHEAD, KD) if b == BR[-1] else ():
                    merged_lo(d)

            with dve.Fori(0, L) as l:
                dve.wait_ge(params_in_place, 16 * l + 16)
                mixer_input(l)
                dve.wait_ge(loaded, 16)
                dve.wait_ge(lat_squared, at(l, 1, 1))
                dve.wait_ge(turn_done, at(l, N_TURN, TURN_AT[("spread", "pre_mix")] + 1))
                dve.tensor_scalar(r_in[:, 0:NT], r_in[:, 0:NT], 1.0 / QL, EPS, ALU.mult, ALU.add)
                step(l, dve.tensor_scalar(r_in[:, NT:2 * NT], r_in[:, NT:2 * NT], 1.0 / KVL, EPS, ALU.mult, ALU.add))
                root(l, 2 * NT)
                dve.tensor_copy(r_all[:, :], factor(l, "pre_mix")).then_inc(mix_factor, 1)
                dve.wait_ge(copied, at(l, N_COPY, COPY_AT["Dlat3"] + 1))
                for i, (lo_c, hi_c) in enumerate(((0, QL), (QL, QL + KVL))):
                    dve.tensor_tensor(d_tm[:, :, lo_c:hi_c], d_tm[:, :, lo_c:hi_c],
                                      view(r_out[:, NT * i:], [[1, NT], [0, hi_c - lo_c]]), ALU.mult).then_inc(latents, 1)
                cos, sin = (c(n).rearrange("p (t c) -> p t c", t=NT) for n in ("cosD", "sinD"))
                k1, k2 = d_tm[:, :, 384:400], d_tm[:, :, 400:416]
                kr = [rope_d[:, i, 0:64].rearrange("p (t c) -> p t c", t=NT) for i in range(4)]
                for i, (a1, a2) in enumerate(((k1, cos), (k2, sin), (k2, cos), (k1, sin))):
                    e = dve.tensor_tensor(kr[i], a1, a2, ALU.mult)
                step(l, e)
                k_out = dk_tm[:, :, :].rearrange("p t (h c) -> p t h c", h=4)
                wide = [view(rope_d[:, i, 0:64], [[16, NT], [0, 4], [1, 16]]) for i in range(4)]
                dve.tensor_tensor(k_out[:, :, :, 64:80], wide[0], wide[1], ALU.subtract)
                dve.tensor_tensor(k_out[:, :, :, 80:96], wide[2], wide[3], ALU.add).then_inc(latents, 1)
                for j in range(3):
                    lo(l, ("latent", j), lat_lo[:, j, :], turn[TURN_AT[("latent", j)] % 2][:, :], lat_hi[:, j, :], param("latent", j))
                dve.wait_ge(mix_factor, at(l, 1, 1))
                gate_scale(l, "D", 0)
                gate_scale(l, "D", 1)
                gate_scale(l, "D", 2)
                for part in (v_hi, v_lo):
                    dve.memset(part[:, :, :, HD:2 * HD].rearrange("p a b c -> p (a b) c").bitcast(F32), 0.0).then_inc(v_clear, 1)
                for t in range(NT):
                    kv = work[WORK_AT[f"Dkv{t}"] % 3][:, :].rearrange("p (h c) -> p h c", h=4)
                    value_parts(l, "D", t, view(kv[:, :, HD:P], [[2 * P, 2], [P, 2], [1, HD]]))
                dve.wait_ge(copied, at(l, N_COPY, COPY_AT["Dq3"] + 1))
                q = dq_tm[:, :, :].rearrange("p t (h c) -> p t h c", h=4)
                q1, q2 = q[:, :, :, 64:80], q[:, :, :, 80:96]
                wcos, wsin = (view(c(n), [[16, NT], [0, 4], [1, 16]]) for n in ("cosD", "sinD"))
                qr = [rope_d[:, i, :].rearrange("p (t h c) -> p t h c", t=NT, h=4) for i in range(4)]
                for i, (a1, a2) in enumerate(((q1, wcos), (q2, wsin), (q2, wcos), (q1, wsin))):
                    e = dve.tensor_tensor(qr[i], a1, a2, ALU.mult)
                step(l, e)
                dve.tensor_tensor(q1, qr[0], qr[1], ALU.subtract)
                dve.tensor_tensor(q2, qr[2], qr[3], ALU.add).then_inc(latents, 1)
                gate_scale(l, "D", 3)
                for h in range(4):
                    lo(l, ("Dq", h), qd_lo[0:DQK, h, :], turn[TURN_AT[("Dq", h)] % 2][0:DQK, :], qd_hi[0:DQK, h, :], DQK ** -0.5)
                    lo(l, ("Dk", h), kd_lo[0:DQK, h, :], turn[TURN_AT[("Dk", h)] % 2][0:DQK, :], kd_hi[0:DQK, h, :])
                for n in range(4, 12):
                    gate_scale(l, "D", n)
                for h in range(4):
                    head(l, "D", h)
                gate_outputs(l, "D")

                for n, (dst, part, scale) in enumerate(((qa_lo[:, 0, :], qa_hi[:, 0, :], HD ** -0.5), (qa_lo[:, 1, :], qa_hi[:, 1, :], HD ** -0.5),
                                                        (ka_lo[:, 0, :], ka_hi[:, 0, :], None), (ka_lo[:, 1, :], ka_hi[:, 1, :], None))):
                    feature_tile(l, FEATURE[n])
                    lo(l, FEATURE[n], dst, feature[:, n, :], part, scale)
                dve.wait_ge(rpb_in_place, 128 * l + 128)
                window_bias(l, 0)
                for t in range(NT):
                    assert next(splits) == ("V", "A", t)
                    dve.wait_ge(hi_done, at(l, N_SPLIT, SPLIT_AT[("V", "A", t | 1)] + 1))
                    for a in range(2):
                        src = work[WORK_AT[f"Av{t // 2}"] % 3][:, 256 * (t % 2) + P * a:256 * (t % 2) + P * a + P]
                        e = dve.scalar_tensor_tensor(out=value_place(v_lo, "A", t)[:, a], in0=src.rearrange("p (c d) -> p c d", d=HD),
                                                     scalar=r_token[:, t:t + 1], in1=value_place(v_hi, "A", t)[:, a].bitcast(F32),
                                                     op0=ALU.mult, op1=ALU.subtract)
                    e.then_inc(lo_done, 1)
                for h in range(4):
                    if h:
                        window_bias(l, h)
                    head(l, "A", h)
                gate_outputs(l, "A")

                dve.wait_ge(t5_ready, 16 * l + 16)
                for n, (dst, part, scale) in enumerate(((qa_lo[:, 0, :], qa_hi[:, 0, :], HD ** -0.5), (qa_lo[:, 1, :], qa_hi[:, 1, :], HD ** -0.5),
                                                        (ka_lo[:, 0, :], ka_hi[:, 0, :], None))):
                    feature_tile(l, FEATURE[4 + n], True)
                    lo(l, FEATURE[4 + n], dst, feature[:, n, :], part, scale)
                feature_tile(l, "Bv", True)
                for t in range(NT):
                    value_parts(l, "B", t, turn[TURN_AT[f"Bv{t // 2}"] % 2][:, P * (t % 2):P * (t % 2) + P].rearrange("p (c d) -> p c d", d=HD))
                for h in range(4):
                    head(l, "B", h)
                gate_outputs(l, "B")

                dve.wait_ge(copied, at(l, N_COPY, COPY_AT["Cq1"] + 1))
                norm_and_rotate(l, 0, 4, "cq")
                for t in range(NT):
                    src = work[WORK_AT[f"Ckv{t // 2}"] % 3][:, 256 * (t % 2) + P:256 * (t % 2) + 2 * P]
                    value_parts(l, "C", t, src.rearrange("p (c d) -> p c d", d=HD), r_token[:, t:t + 1])
                dve.wait_ge(copied, at(l, N_COPY, COPY_AT["Ckv1"] + 1))
                dve.wait_ge(c_ready, at(l, 2, 1))
                norm_and_rotate(l, 4, 2, "ck")
                gate_scale(l, "C", 0)
                for j in range(3):
                    src = turn[TURN_AT[("C", j)] % 2][:, :]
                    if j < 2:
                        lo(l, ("C", j), qa_lo[:, j, :], src, qa_hi[:, j, :], HD ** -0.5)
                    else:
                        lo(l, ("C", j), ka_lo[:, 0, :], src, ka_hi[:, 0, :])
                for j in range(1, 4):
                    gate_scale(l, "C", j)
                for h in range(4):
                    head(l, "C", h)
                gate_outputs(l, "C")

                output_factor(l, "post_mix")
                for d in range(KD + LAG):
                    if d < KD:
                        add_output(l, "post_mix", d, d, d < MIX_DVE)
                    if d >= LAG:
                        e = d - LAG
                        lo(l, ("h", "pre_ffn", e), h_lo[:, e, :], x[:, e, :], h_hi[:, e, :], param("pre_ffn", e))
                sum_squares(l, "pre_ffn", KD)
                token_factor(l, "pre_ffn")
                step(l, dve.tensor_copy(r_ffn[:, :], factor(l, "pre_ffn")))
                dve.sem_inc(waited, 1)
                with dve.Fori(0, KF // 2) as i:
                    for s in range(2):
                        n = l * KF + 2 * i + s
                        gate_bank, up_bank = ffn_bank[s]
                        dve.wait_ge(main_done, l * N_MAIN + 4 * i + (GUM0 + 2 * s + 2))
                        dve.wait_ge(lo_done, l * N_SPLIT + 2 * i + (ACT0 + s - 1))
                        dve.tensor_tensor(ffn_g[:, s, :], gate_bank[:, :], r_ffn[:, :], ALU.mult).then_inc(ffn_scaled, 1)
                        dve.wait_ge(ffn_tanh, n + 1)
                        dve.scalar_tensor_tensor(out=ffn_g[:, s, :], in0=ffn_t[:, s, :], scalar=1.0, in1=ffn_g[:, s, :],
                                                 op0=ALU.add, op1=ALU.mult).then_inc(ffn_gate, 1)
                        dve.wait_ge(ffn_gate, n + 1)
                        dve.wait_ge(main_done, l * N_MAIN + 4 * i + (GUM0 + 2 * s + 3))
                        dve.tensor_tensor(ffn_t[:, s, :], up_bank[:, :], r_ffn[:, :], ALU.mult).then_inc(ffn_up, 1)
                        dve.wait_ge(ffn_up, n + 3)
                        dve.scalar_tensor_tensor(out=ffn_g[:, s, :], in0=ffn_g[:, s, :], scalar=0.5, in1=ffn_t[:, s, :],
                                                 op0=ALU.mult, op1=ALU.mult).then_inc(ffn_full, 1)
                        dve.wait_ge(hi_done, l * N_SPLIT + 2 * i + (ACT0 + s + 1))
                        j = bass.ds(2 * i + s, 1)
                        dve.tensor_tensor(act_lo[:, j, :].rearrange("p a s -> p (a s)"), ffn_g[:, s, :],
                                          act_hi[:, j, :].rearrange("p a s -> p (a s)").bitcast(F32), ALU.subtract).then_inc(lo_done, 1)
                output_factor(l, "post_ffn")
                for i, d in enumerate([*range(FFN_DVE, KD), *range(FFN_DVE)]):
                    add_output(l, "post_ffn", d, i, d < FFN_DVE)
                dve.wait_ge(x_dve, at(l, N_X, N_X + MIX_DVE + FFN_DVE))
                dve.sem_inc(x_dve, X0)
                dve.sem_inc(chain, N_CHAIN - steps[0])


def weight_stream(w_in, w_q, w_kv, w_branch, w_out, w_gu, w_down):
    def piece(w):
        k, n = w.shape
        return w.reshape(k // P, P, n).transpose(1, 0, 2).reshape(P, -1)

    def order(heads):
        return heads.reshape(4, HD, -1)[[0, 2, 1, 3]].reshape(4 * HD, -1)

    stream = np.zeros((L, NP_, P, 2048), np.float32)
    for l in range(L):
        for n, (name, size) in enumerate(PIECES):
            if name == "Dup":
                p = np.concatenate([piece(w_q[l]), w_kv[l]], axis=1)
            elif name.startswith("Dlat"):
                a = 4 * P * int(name[4])
                p = piece(w_in[l][a:a + 4 * P, W_IN_AT["Dlat"]:W_IN_AT["gates"]])
            elif name.startswith("gate"):
                a = W_IN_AT["gates"] + "ABCD".index(name[4]) * DM + 256 * int(name[5])
                p = piece(w_in[l][:, a:a + 256])
            elif name.startswith("branch"):
                w = w_branch[l]["ABCD".index(name[6])]
                p = piece(order(w) if name[6] in "BC" else w)
            elif name.startswith("out"):
                p = piece(w_out[l][:, 256 * int(name[3:]):256 * int(name[3:]) + 256])
            elif name.startswith("gu"):
                j = P * int(name[2:])
                p = piece(np.concatenate([w_gu[l][:, j:j + P], w_gu[l][:, DFF + j:DFF + j + P]], axis=1))
            elif name.startswith("down"):
                d, h = int(name[4]), int(name[5])
                p = piece(w_down[l][KH * P * h:KH * P * (h + 1), P * d:P * d + P])
            else:
                w = w_in[l][:, W_IN_AT[name]:W_IN_AT[name] + size // KD]
                p = piece(order(w.T).T if name in ("Bq", "Cq") else w)
            assert p.shape == (P, size), (name, p.shape)
            stream[l, n, :, :size] = p
    return stream


def in_blocks_order(a):
    s = a.shape[:-1]
    return a.reshape(*s, ROWS, NT, 16).swapaxes(-3, -2).reshape(*s, S)


def t5_one_hot():
    hot = np.zeros((33, BIAS_X), np.float32)
    rel = np.arange(BIAS_X) - 255
    n = np.abs(rel)
    large = 8 + (np.log(np.maximum(n, 1) / 8) / np.log(128 / 8) * 8).astype(np.int32)
    bucket = (rel > 0).astype(np.int32) * 16 + np.where(n < 8, n, np.minimum(large, 15))
    hot[bucket, np.arange(BIAS_X)] = 1.0
    hot[32, n > 128] = NEG
    return hot


def constants():
    out = np.zeros((P, N_CONST), np.float32)

    def put(name, a):
        out[:, CONST[name][0]:CONST[name][1]] = a.reshape(P, -1)

    put("ident", np.eye(P, dtype=np.float32))
    put("mean", np.full((P, 1), 1.0 / DM, np.float32))

    def angles(pos, d):
        inv = 1.0 / (np.float32(ROPE_THETA) ** (np.arange(d // 2, dtype=np.float32) * np.float32(2.0 / d)))
        return pos.astype(np.float32)[:, None] * inv.astype(np.float32)[None, :]

    tok = in_blocks_order(np.arange(S))
    tiled = lambda a: a.reshape(NT, P, -1).transpose(1, 0, 2)
    axial = np.concatenate([angles(tok // GRID_W, 32), angles(tok % GRID_W, 32)], axis=1)
    for n, ang in (("C", axial), ("D", angles(tok, ROPE))):
        put("cos" + n, tiled(np.cos(ang)))
        put("sin" + n, tiled(np.sin(ang)))
    mask = np.zeros((P, 3, 48), np.float32)
    for v, block in enumerate((0, 1, 3)):
        for p in range(P):
            qc = 16 * block + p % 16
            start = min(max(qc - 8, 0), GRID_W - 16)
            kc = 16 * block - 16 + np.arange(48)
            mask[p, v, (kc < start) | (kc >= start + 16)] = NEG
    put("maskA", mask)
    return out


def kernel(x, w_in, a_rpb, b_sink, t5_bias, c_q_norm, c_k_norm, d_q_norm, d_kv_norm, d_w_q_up, d_w_kv_up,
           w_branch, w_out, ln_pre_mix, ln_post_mix, ln_pre_ffn, ln_post_ffn, ffn_w_gu, ffn_w_down):
    import concourse.bacc as bacc
    from concourse.bass_utils import run_bass_kernel_spmd

    given = [np.asarray(a) for a in (x, w_in, a_rpb, b_sink, t5_bias, c_q_norm, c_k_norm, d_q_norm, d_kv_norm, d_w_q_up,
                                     d_w_kv_up, w_branch, w_out, ln_pre_mix, ln_post_mix, ln_pre_ffn, ln_post_ffn,
                                     ffn_w_gu, ffn_w_down)]
    (x, w_in, a_rpb, b_sink, t5_bias, c_q_norm, c_k_norm, d_q_norm, d_kv_norm, d_w_q_up, d_w_kv_up,
     w_branch, w_out, ln_pre_mix, ln_post_mix, ln_pre_ffn, ln_post_ffn, ffn_w_gu, ffn_w_down) = given

    swap = [0, 2, 1, 3]
    params = np.zeros((L, P, N_PARAM), np.float32)

    def put(name, l, a):
        params[l, :, PARAMS[name][0]:PARAMS[name][1]] = a

    for l in range(L):
        for name, g in (("pre_mix", ln_pre_mix), ("post_mix", ln_post_mix), ("pre_ffn", ln_pre_ffn), ("post_ffn", ln_post_ffn)):
            put(name, l, g[l].reshape(-1, P).T)
        put("latent", l, np.concatenate([d_q_norm[l].reshape(-1, P), d_kv_norm[l].reshape(-1, P)]).T)
        put("sink", l, b_sink[l][swap][None, :])
        put("cq", l, c_q_norm[l][None, :])
        put("ck", l, c_k_norm[l][None, :])

    rpb = np.zeros((L, N_RPB), np.float32)
    rpb[:, :4 * RPB_HEAD].reshape(L, 4, 15, RPB_ROW)[:, :, :, 16:47] = a_rpb
    t5 = np.ones((33, 4), np.float32)
    t5[:32] = t5_bias[:, swap]

    arrays = dict(
        stream=weight_stream(w_in, d_w_q_up, d_w_kv_up, w_branch, w_out, ffn_w_gu, ffn_w_down),
        x_in=np.ascontiguousarray(in_blocks_order(x[0].T).reshape(KD, P, S).transpose(1, 0, 2)),
        const_in=constants(), params_in=params, rpb_in=rpb, t5_in=t5, hot_in=t5_one_hot())
    nc = bacc.Bacc("TRN2", target_bir_lowering=False, num_devices=1)
    args = [nc.dram_tensor(n, a.shape, F32, kind="ExternalInput").ap() for n, a in arrays.items()]
    args.append(nc.dram_tensor("out", (P, KD, S), F32, kind="ExternalOutput").ap())
    program(nc, *args)
    r = run_bass_kernel_spmd(nc, [arrays], core_ids=[0])
    y = np.asarray(r.results[0]["out"])
    y = y.transpose(1, 0, 2).reshape(DM, NT, ROWS, 16).swapaxes(1, 2).reshape(DM, S)
    return np.ascontiguousarray(y.T)[None]
```
